# Optimizing a Trainium2 kernel written in Bass

```python
import math
import jax, jax.numpy as jnp
from jax import lax
import numpy as np

D_MODEL = 1024
BATCH = 1
SEQ = 256
DEPTH = 1

N_BRANCH = 4
D_MIX = D_MODEL // N_BRANCH
HEAD_A = 64
H_A = D_MIX // HEAD_A
LORA_W = 32
LORA_A = 32
LORA_V = 32
LORA_G = 64
LNX_EPS = 64e-5
CHUNK = 128
GROUP_B = 64
G_B = D_MIX // GROUP_B
CONV_K = 3
GROUP_D = 16
G_D = D_MIX // GROUP_D
N_STATE = 64
D_FF = 4 * D_MODEL
EPS = 1e-6
LN_EPS = 1e-5

A_COLS = 3 * D_MIX + LORA_W + LORA_A + LORA_G
B_COLS = 2 * D_MIX
C_COLS = 3 * D_MIX
D_COLS = D_MIX
GATE_COLS = N_BRANCH * D_MODEL
OFF_B = A_COLS
OFF_C = OFF_B + B_COLS
OFF_D = OFF_C + C_COLS
OFF_G = OFF_D + D_COLS
N_IN = OFF_G + GATE_COLS


def rms_norm(x, g):
    xf = x.astype(jnp.float32)
    return xf * lax.rsqrt(jnp.mean(xf * xf, axis=-1, keepdims=True) + EPS) * g.astype(jnp.float32)

def layer_norm(x, w, b, eps):
    xf = x.astype(jnp.float32)
    mu = jnp.mean(xf, axis=-1, keepdims=True)
    var = jnp.mean(jnp.square(xf - mu), axis=-1, keepdims=True)
    return (xf - mu) * lax.rsqrt(var + eps) * w.astype(jnp.float32) + b.astype(jnp.float32)

def shift_prev(p):
    return jnp.pad(p, ((0, 0), (1, 0), (0, 0)))[:, :-1]

def wkv7(r, w, k, v, a, b):
    bsz, _, nh, n = r.shape

    def step(state, inp):
        r_t, w_t, k_t, v_t, a_t, b_t = inp
        sa = jnp.einsum('bhij,bhj->bhi', state, a_t)
        state = (state * w_t[:, :, None, :] + sa[..., None] * b_t[:, :, None, :]
                 + v_t[..., None] * k_t[:, :, None, :])
        return state, jnp.einsum('bhij,bhj->bhi', state, r_t)

    xs = tuple(jnp.moveaxis(t, 1, 0) for t in (r, w, k, v, a, b))
    s0 = jnp.zeros((bsz, nh, n, n), jnp.float32)
    _, out = lax.scan(step, s0, xs)
    return jnp.moveaxis(out, 0, 1)

def rwkv7_mixer(p, v_first, v_mix, mu, w0, w2, a0, a2, g2, k_k, k_a, r_k, lnx_w, lnx_b, w_out):
    bsz, seq, _ = p.shape
    p = p + (shift_prev(p) - p) * mu
    r = p[..., :D_MIX]
    k = p[..., D_MIX:2 * D_MIX]
    v = p[..., 2 * D_MIX:3 * D_MIX]
    wd = p[..., 3 * D_MIX:3 * D_MIX + LORA_W]
    ad = p[..., 3 * D_MIX + LORA_W:3 * D_MIX + LORA_W + LORA_A]
    gd = p[..., 3 * D_MIX + LORA_W + LORA_A:]
    log_w = -jax.nn.softplus(-(w0 + jnp.tanh(wd) @ w2)) - 0.5
    decay = jnp.exp(-jnp.exp(log_w))
    if v_mix is None:
        v_first = v
    else:
        v0, v1, v2 = v_mix
        v = v + (v_first - v) * jax.nn.sigmoid(v0 + (v @ v1) @ v2)
    a = jax.nn.sigmoid(a0 + ad @ a2)
    g = jax.nn.sigmoid(gd) @ g2

    def heads(t):
        return t.reshape(bsz, seq, H_A, HEAD_A).astype(jnp.float32)

    kk = heads(k * k_k)
    kk = kk / jnp.maximum(jnp.sqrt(jnp.sum(kk * kk, axis=-1, keepdims=True)), 1e-12)
    k = k * (1.0 + (a - 1.0) * k_a)
    rh, kh, vh, ah = heads(r), heads(k), heads(v), heads(a)
    o = wkv7(rh, heads(decay), kh, vh, -kk, kk * ah)
    o = layer_norm(o, lnx_w.reshape(H_A, HEAD_A), lnx_b.reshape(H_A, HEAD_A), LNX_EPS)
    o = o + jnp.sum(rh * kh * r_k, axis=-1, keepdims=True) * vh
    return (o.reshape(bsz, seq, D_MIX) * g) @ w_out, v_first

def spatial_gating_mixer(p, ln_w, ln_b, w_s, b_s, w_out):
    bsz, seq, _ = p.shape
    z = jax.nn.gelu(p)
    u = z[..., :D_MIX]
    v = layer_norm(z[..., D_MIX:], ln_w, ln_b, LN_EPS)
    v = v.reshape(bsz, seq // CHUNK, CHUNK, G_B, GROUP_B)
    mask = jnp.tril(jnp.ones((CHUNK, CHUNK), jnp.float32))
    mixed = jnp.einsum('gts,bnsgc->bntgc', w_s * mask, v) + b_s.T[None, None, :, :, None]
    return (u * mixed.reshape(bsz, seq, D_MIX)) @ w_out

def short_conv_mixer(p, conv_w, w_out):
    seq = p.shape[1]
    bg = p[..., :D_MIX]
    cg = p[..., D_MIX:2 * D_MIX]
    xin = p[..., 2 * D_MIX:]
    zp = jnp.pad(cg * xin, ((0, 0), (CONV_K - 1, 0), (0, 0)))
    y = sum(conv_w[j] * zp[:, j:j + seq] for j in range(CONV_K))
    return (bg * y) @ w_out

def _complex_affine_combine(e1, e2):
    a1r, a1i, b1r, b1i = e1
    a2r, a2i, b2r, b2i = e2
    return (a2r * a1r - a2i * a1i,
            a2r * a1i + a2i * a1r,
            a2r * b1r - a2i * b1i + b2r,
            a2r * b1i + a2i * b1r + b2i)

def s5_mixer(u, a_re, a_im, b_re, b_im, c_re, c_im, d, log_dt, glu_w):
    f32 = jnp.float32
    bsz, seq, _ = u.shape
    u32 = u.astype(f32)
    ug = u32.reshape(bsz, seq, G_D, GROUP_D)
    lam_re = jnp.minimum(a_re.astype(f32), -1e-4)
    lam_im = a_im.astype(f32)
    dt = jnp.exp(log_dt.astype(f32))[:, None]
    mag = jnp.exp(lam_re * dt)
    ab_re = mag * jnp.cos(lam_im * dt)
    ab_im = mag * jnp.sin(lam_im * dt)
    den = lam_re * lam_re + lam_im * lam_im
    q_re = ((ab_re - 1.0) * lam_re + ab_im * lam_im) / den
    q_im = (ab_im * lam_re - (ab_re - 1.0) * lam_im) / den
    bb_re = q_re[..., None] * b_re - q_im[..., None] * b_im
    bb_im = q_re[..., None] * b_im + q_im[..., None] * b_re
    bu_re = jnp.einsum('gnc,bsgc->bsgn', bb_re, ug)
    bu_im = jnp.einsum('gnc,bsgc->bsgn', bb_im, ug)
    ar = jnp.broadcast_to(ab_re, bu_re.shape)
    ai = jnp.broadcast_to(ab_im, bu_im.shape)
    _, _, x_re, x_im = lax.associative_scan(_complex_affine_combine, (ar, ai, bu_re, bu_im), axis=1)
    y = (jnp.einsum('gcn,bsgn->bsgc', c_re, x_re) - jnp.einsum('gcn,bsgn->bsgc', c_im, x_im))
    y = y.reshape(bsz, seq, D_MIX) + d * u32
    h = jax.nn.gelu(y) @ glu_w
    return h[..., :D_MODEL] * jax.nn.sigmoid(h[..., D_MODEL:])

def first_inputs(seed: int = 0) -> dict:
    key = jax.random.key(seed)
    ks = iter(jax.random.split(key, 64))
    f32 = jnp.float32
    L = DEPTH

    def nrm(shape, scale):
        return scale * jax.random.normal(next(ks), shape, f32)

    def uni(shape, lo, hi):
        return jax.random.uniform(next(ks), shape, f32, lo, hi)

    return {
        'x': nrm((BATCH, SEQ, D_MODEL), 1.0),
        'c': nrm((BATCH, D_MODEL), 1.0),
        'ada_w': nrm((L, D_MODEL, 6 * D_MODEL), 0.5 * D_MODEL ** -0.5),
        'ada_b': nrm((L, 6 * D_MODEL), 0.02),
        'norm_mix_g': 1.0 + nrm((L, D_MODEL), 0.1),
        'w_in': nrm((L, D_MODEL, N_IN), D_MODEL ** -0.5),
        'rwkv_mu': uni((L, A_COLS), 0.0, 1.0),
        'rwkv_w0': uni((L, D_MIX), -6.0, -1.0),
        'rwkv_w2': nrm((L, LORA_W, D_MIX), 0.1),
        'rwkv_a0': nrm((L, D_MIX), 0.1),
        'rwkv_a2': nrm((L, LORA_A, D_MIX), 0.1),
        'rwkv_g2': nrm((L, LORA_G, D_MIX), LORA_G ** -0.5),
        'rwkv_v0': 1.0 + nrm((L - 1, D_MIX), 0.1),
        'rwkv_v1': nrm((L - 1, D_MIX, LORA_V), D_MIX ** -0.5),
        'rwkv_v2': nrm((L - 1, LORA_V, D_MIX), 0.1),
        'rwkv_kk': 0.85 + nrm((L, D_MIX), 0.1),
        'rwkv_ka': 1.0 + nrm((L, D_MIX), 0.1),
        'rwkv_rk': nrm((L, H_A, HEAD_A), 0.1),
        'rwkv_lnx_w': 1.0 + nrm((L, D_MIX), 0.1),
        'rwkv_lnx_b': nrm((L, D_MIX), 0.02),
        'rwkv_out': nrm((L, D_MIX, D_MODEL), D_MIX ** -0.5),
        'sg_ln_w': 1.0 + nrm((L, D_MIX), 0.1),
        'sg_ln_b': nrm((L, D_MIX), 0.02),
        'sg_ws': nrm((L, G_B, CHUNK, CHUNK), CHUNK ** -0.5),
        'sg_bs': 1.0 + nrm((L, G_B, CHUNK), 0.1),
        'sg_out': nrm((L, D_MIX, D_MODEL), D_MIX ** -0.5),
        'conv_w': nrm((L, CONV_K, D_MIX), CONV_K ** -0.5),
        'conv_out': nrm((L, D_MIX, D_MODEL), D_MIX ** -0.5),
        's5_a_re': -0.5 + nrm((L, G_D, N_STATE), 0.01),
        's5_a_im': jnp.pi * jnp.arange(N_STATE, dtype=f32)[None, None, :] + nrm((L, G_D, N_STATE), 0.01),
        's5_b_re': nrm((L, G_D, N_STATE, GROUP_D), (2 * GROUP_D) ** -0.5),
        's5_b_im': nrm((L, G_D, N_STATE, GROUP_D), (2 * GROUP_D) ** -0.5),
        's5_c_re': nrm((L, G_D, GROUP_D, N_STATE), (2 * N_STATE) ** -0.5),
        's5_c_im': nrm((L, G_D, GROUP_D, N_STATE), (2 * N_STATE) ** -0.5),
        's5_d': nrm((L, D_MIX), 1.0),
        's5_log_dt': uni((L, G_D), math.log(1e-3), math.log(1e-1)),
        's5_glu_w': nrm((L, D_MIX, 2 * D_MODEL), D_MIX ** -0.5),
        'w_o': nrm((L, D_MODEL, D_MODEL), D_MODEL ** -0.5),
        'norm_ffn_g': 1.0 + nrm((L, D_MODEL), 0.1),
        'ffn_w1': nrm((L, D_MODEL, D_FF), D_MODEL ** -0.5),
        'ffn_w2': nrm((L, D_FF, D_MODEL), D_FF ** -0.5),
        'final_g': 1.0 + nrm((D_MODEL,), 0.1),
    }

def first_block(x, c, ada_w, ada_b, norm_mix_g, w_in, rwkv_mu, rwkv_w0, rwkv_w2, rwkv_a0, rwkv_a2,
              rwkv_g2, rwkv_v0, rwkv_v1, rwkv_v2, rwkv_kk, rwkv_ka, rwkv_rk, rwkv_lnx_w, rwkv_lnx_b,
              rwkv_out, sg_ln_w, sg_ln_b, sg_ws, sg_bs, sg_out, conv_w, conv_out, s5_a_re, s5_a_im,
              s5_b_re, s5_b_im, s5_c_re, s5_c_im, s5_d, s5_log_dt, s5_glu_w, w_o, norm_ffn_g,
              ffn_w1, ffn_w2, final_g):
    in_dtype = x.dtype
    bsz, seq, _ = x.shape
    c_act = jax.nn.silu(c.astype(jnp.float32))
    v_first = None
    for l in range(DEPTH):
        mod = (c_act @ ada_w[l] + ada_b[l])[:, None, :]
        sh1, sc1, gt1, sh2, sc2, gt2 = jnp.split(mod, 6, axis=-1)

        h = rms_norm(x, norm_mix_g[l]) * (1.0 + sc1) + sh1
        p = h @ w_in[l]
        v_mix = None if l == 0 else (rwkv_v0[l - 1], rwkv_v1[l - 1], rwkv_v2[l - 1])
        y_a, v_first = rwkv7_mixer(p[..., :OFF_B], v_first, v_mix, rwkv_mu[l], rwkv_w0[l], rwkv_w2[l],
                                   rwkv_a0[l], rwkv_a2[l], rwkv_g2[l], rwkv_kk[l], rwkv_ka[l],
                                   rwkv_rk[l], rwkv_lnx_w[l], rwkv_lnx_b[l], rwkv_out[l])
        y_b = spatial_gating_mixer(p[..., OFF_B:OFF_C], sg_ln_w[l], sg_ln_b[l], sg_ws[l], sg_bs[l], sg_out[l])
        y_c = short_conv_mixer(p[..., OFF_C:OFF_D], conv_w[l], conv_out[l])
        y_d = s5_mixer(p[..., OFF_D:OFF_G], s5_a_re[l], s5_a_im[l], s5_b_re[l], s5_b_im[l],
                       s5_c_re[l], s5_c_im[l], s5_d[l], s5_log_dt[l], s5_glu_w[l])
        gates = jax.nn.sigmoid(p[..., OFF_G:]).reshape(bsz, seq, N_BRANCH, D_MODEL)
        merged = (gates[:, :, 0] * y_a + gates[:, :, 1] * y_b
                  + gates[:, :, 2] * y_c + gates[:, :, 3] * y_d)
        x = x + gt1 * (merged @ w_o[l])

        h = rms_norm(x, norm_ffn_g[l]) * (1.0 + sc2) + sh2
        x = x + gt2 * (jnp.square(jax.nn.relu(h @ ffn_w1[l])) @ ffn_w2[l])
    return rms_norm(x, final_g).astype(in_dtype)


HEAD_DIM = 64
MOBA_HEADS = 8
FOX_HEADS = 8
A_WIDTH = MOBA_HEADS * HEAD_DIM
B_WIDTH = FOX_HEADS * HEAD_DIM
ROPE_DIM = HEAD_DIM // 4
ROPE_THETA = 500000.0
MOBA_BLOCK = 256
MOBA_TOPK = 3
MOBA_Q_CHUNK = 64
Q_BLOCK = 128
FORGET_BIAS_CENTER = 3.0
PEER_HEADS = 8
PEER_NKEYS = 128
PEER_NEXPERTS = PEER_NKEYS * PEER_NKEYS
PEER_KEY_DIM = 256
PEER_HALF = PEER_KEY_DIM // 2
PEER_TOPK = 16
PEER_TOKEN_CHUNK = 128
IN_COLS = 3 * A_WIDTH + 3 * B_WIDTH + FOX_HEADS + 2 * D_MODEL
RMS_EPS = 1e-6


def rms_norm_2(x, g):
    xf = x.astype(jnp.float32)
    y = xf * lax.rsqrt(jnp.mean(xf * xf, axis=-1, keepdims=True) + RMS_EPS)
    return (y * g.astype(jnp.float32)).astype(x.dtype)

def partial_rope(x, pos):
    half = ROPE_DIM // 2
    inv_freq = jnp.power(ROPE_THETA, -jnp.arange(half, dtype=jnp.float32) / half)
    ang = pos.astype(jnp.float32)[:, None] * inv_freq[None, :]
    cos = jnp.cos(ang).astype(x.dtype)
    sin = jnp.sin(ang).astype(x.dtype)
    x1 = x[..., :half]
    x2 = x[..., half:ROPE_DIM]
    return jnp.concatenate([x1 * cos - x2 * sin, x1 * sin + x2 * cos, x[..., ROPE_DIM:]], axis=-1)

def moba_attention(q, k, v):
    B, H, S, dh = q.shape
    L = MOBA_BLOCK
    nb = -(-S // L)
    pad = nb * L - S
    k_blk = jnp.pad(k, ((0, 0), (0, 0), (0, pad), (0, 0))).reshape(B, H, nb, L, dh)
    v_blk = jnp.pad(v, ((0, 0), (0, 0), (0, pad), (0, 0))).reshape(B, H, nb, L, dh)
    k_mean = jnp.mean(k_blk.astype(jnp.float32), axis=3).astype(k.dtype)
    scale = dh ** -0.5
    qpos = jnp.arange(S)
    gate = jnp.einsum('bhsd,bhnd->bhsn', q, k_mean).astype(jnp.float32)
    past = jnp.arange(nb)[None, :] < (qpos // L)[:, None]
    gate = jnp.where(past, gate, -jnp.inf)
    kk = min(MOBA_TOPK, nb)
    top_val, top_idx = lax.top_k(gate, kk)
    sel_valid = jnp.isfinite(top_val)
    C = MOBA_Q_CHUNK
    nq = S // C
    q_c = q.reshape(B, H, nq, C, dh).transpose(2, 0, 1, 3, 4)
    idx_c = top_idx.reshape(B, H, nq, C, kk).transpose(2, 0, 1, 3, 4)
    val_c = sel_valid.reshape(B, H, nq, C, kk).transpose(2, 0, 1, 3, 4)
    take_blocks = jax.vmap(jax.vmap(lambda tab, ix: tab[ix]))

    def step(args):
        ci, qi, ii, vi = args
        q0 = ci * C
        own = q0 // L
        ks = take_blocks(k_blk, ii)
        vs = take_blocks(v_blk, ii)
        s_sel = jnp.einsum('bhcd,bhcjld->bhcjl', qi, ks).astype(jnp.float32) * scale
        s_sel = jnp.where(vi[..., None], s_sel, -jnp.inf).reshape(B, H, C, kk * L)
        k_own = lax.dynamic_index_in_dim(k_blk, own, axis=2, keepdims=False)
        v_own = lax.dynamic_index_in_dim(v_blk, own, axis=2, keepdims=False)
        s_own = jnp.einsum('bhcd,bhld->bhcl', qi, k_own).astype(jnp.float32) * scale
        causal = (own * L + jnp.arange(L))[None, :] <= (q0 + jnp.arange(C))[:, None]
        s_own = jnp.where(causal, s_own, -jnp.inf)
        p = jax.nn.softmax(jnp.concatenate([s_sel, s_own], axis=-1), axis=-1)
        p_sel = p[..., :kk * L].reshape(B, H, C, kk, L).astype(v.dtype)
        p_own = p[..., kk * L:].astype(v.dtype)
        return (jnp.einsum('bhcjl,bhcjld->bhcd', p_sel, vs)
                + jnp.einsum('bhcl,bhld->bhcd', p_own, v_own))

    out = lax.map(step, (jnp.arange(nq), q_c, idx_c, val_c))
    return out.transpose(1, 2, 0, 3, 4).reshape(B, H, S, dh)

def forgetting_attention(q, k, v, log_f):
    B, H, S, dh = q.shape
    scale = dh ** -0.5
    c = jnp.cumsum(log_f, axis=-1)
    nq = S // Q_BLOCK
    q_c = q.reshape(B, H, nq, Q_BLOCK, dh).transpose(2, 0, 1, 3, 4)
    c_c = c.reshape(B, H, nq, Q_BLOCK).transpose(2, 0, 1, 3)
    kpos = jnp.arange(S)

    def step(args):
        ci, qi, cq = args
        s = (jnp.einsum('bhqd,bhkd->bhqk', qi, k).astype(jnp.float32) * scale
             + cq[..., None] - c[:, :, None, :])
        qpos = ci * Q_BLOCK + jnp.arange(Q_BLOCK)
        s = jnp.where(kpos[None, :] <= qpos[:, None], s, -jnp.inf)
        p = jax.nn.softmax(s, axis=-1).astype(v.dtype)
        return jnp.einsum('bhqk,bhkd->bhqd', p, v)

    out = lax.map(step, (jnp.arange(nq), q_c, c_c))
    return out.transpose(1, 2, 0, 3, 4).reshape(B, H, S, dh)

def hybrid_mixer(xn, w_in, b_forget, w_branch_a, w_branch_b, w_out):
    B, S, _ = xn.shape
    proj = xn @ w_in
    cuts = [A_WIDTH, 2 * A_WIDTH, 3 * A_WIDTH,
            3 * A_WIDTH + B_WIDTH, 3 * A_WIDTH + 2 * B_WIDTH, 3 * A_WIDTH + 3 * B_WIDTH,
            3 * A_WIDTH + 3 * B_WIDTH + FOX_HEADS, 3 * A_WIDTH + 3 * B_WIDTH + FOX_HEADS + D_MODEL]
    qa, ka, va, qb, kb, vb, f_logit, g_a, g_b = jnp.split(proj, cuts, axis=-1)

    def heads(t, n):
        return t.reshape(B, S, n, HEAD_DIM).transpose(0, 2, 1, 3)

    pos = jnp.arange(S)
    ya = moba_attention(partial_rope(heads(qa, MOBA_HEADS), pos),
                        partial_rope(heads(ka, MOBA_HEADS), pos),
                        heads(va, MOBA_HEADS))
    ya = ya.transpose(0, 2, 1, 3).reshape(B, S, A_WIDTH) @ w_branch_a
    log_f = jax.nn.log_sigmoid((f_logit + b_forget).astype(jnp.float32)).transpose(0, 2, 1)
    yb = forgetting_attention(heads(qb, FOX_HEADS), heads(kb, FOX_HEADS), heads(vb, FOX_HEADS), log_f)
    yb = yb.transpose(0, 2, 1, 3).reshape(B, S, B_WIDTH) @ w_branch_b
    merged = jax.nn.sigmoid(g_a) * ya + jax.nn.sigmoid(g_b) * yb
    return merged @ w_out

def peer_ffn(xn, w_peer_q, sub_keys, expert_u, expert_v):
    B, S, D = xn.shape
    T = B * S
    xt = xn.reshape(T, D)
    qh = (xt @ w_peer_q).reshape(T, PEER_HEADS, 2, PEER_HALF)
    s = jnp.einsum('thpd,hpnd->thpn', qh, sub_keys).astype(jnp.float32)
    sv, si = lax.top_k(s, PEER_TOPK)
    cand = (sv[:, :, 0, :, None] + sv[:, :, 1, None, :]).reshape(T, PEER_HEADS, PEER_TOPK * PEER_TOPK)
    cand_idx = (si[:, :, 0, :, None] * PEER_NKEYS + si[:, :, 1, None, :]).reshape(T, PEER_HEADS, PEER_TOPK * PEER_TOPK)
    best, pick = lax.top_k(cand, PEER_TOPK)
    expert_idx = jnp.take_along_axis(cand_idx, pick, axis=-1)
    gates = jax.nn.softmax(best, axis=-1)
    C = PEER_TOKEN_CHUNK
    n_chunks = T // C

    def step(args):
        xc, ic, gc = args
        u = expert_u[ic]
        hval = jnp.einsum('cd,chkd->chk', xc, u).astype(jnp.float32)
        a = (gc * jax.nn.gelu(hval, approximate=False)).astype(xc.dtype)
        return jnp.einsum('chk,chkd->cd', a, expert_v[ic])

    out = lax.map(step, (xt.reshape(n_chunks, C, D),
                         expert_idx.reshape(n_chunks, C, PEER_HEADS, PEER_TOPK),
                         gates.reshape(n_chunks, C, PEER_HEADS, PEER_TOPK)))
    return out.reshape(B, S, D)

def second_inputs(seed: int = 0) -> dict:
    key = jax.random.key(seed)
    ks = jax.random.split(key, 14)
    f32 = jnp.float32

    def nrm(k, shape, scale):
        return jax.random.normal(k, shape, f32) * scale

    return {
        "x": nrm(ks[0], (BATCH, SEQ, D_MODEL), 1.0),
        "norm_mix_g": 1.0 + nrm(ks[1], (DEPTH, D_MODEL), 0.02),
        "w_in": nrm(ks[2], (DEPTH, D_MODEL, IN_COLS), D_MODEL ** -0.5),
        "b_forget": FORGET_BIAS_CENTER + nrm(ks[3], (DEPTH, FOX_HEADS), 0.5),
        "w_branch_a": nrm(ks[4], (DEPTH, A_WIDTH, D_MODEL), A_WIDTH ** -0.5),
        "w_branch_b": nrm(ks[5], (DEPTH, B_WIDTH, D_MODEL), B_WIDTH ** -0.5),
        "w_out": nrm(ks[6], (DEPTH, D_MODEL, D_MODEL), D_MODEL ** -0.5),
        "norm_ffn_g": 1.0 + nrm(ks[7], (DEPTH, D_MODEL), 0.02),
        "w_peer_q": nrm(ks[8], (DEPTH, D_MODEL, PEER_HEADS * PEER_KEY_DIM), D_MODEL ** -0.5),
        "peer_sub_keys": nrm(ks[9], (DEPTH, PEER_HEADS, 2, PEER_NKEYS, PEER_HALF), PEER_HALF ** -0.5),
        "peer_expert_u": nrm(ks[10], (DEPTH, PEER_NEXPERTS, D_MODEL), D_MODEL ** -0.5),
        "peer_expert_v": nrm(ks[11], (DEPTH, PEER_NEXPERTS, D_MODEL), PEER_HEADS ** -0.5),
        "norm_final_g": 1.0 + nrm(ks[12], (D_MODEL,), 0.02),
    }

def second_block(x, norm_mix_g, w_in, b_forget, w_branch_a, w_branch_b, w_out, norm_ffn_g,
              w_peer_q, peer_sub_keys, peer_expert_u, peer_expert_v, norm_final_g):
    h = x
    for l in range(DEPTH):
        h = h + hybrid_mixer(rms_norm_2(h, norm_mix_g[l]), w_in[l], b_forget[l],
                             w_branch_a[l], w_branch_b[l], w_out[l])
        h = h + peer_ffn(rms_norm_2(h, norm_ffn_g[l]), w_peer_q[l], peer_sub_keys[l],
                         peer_expert_u[l], peer_expert_v[l])
    return rms_norm_2(h, norm_final_g)


def setup_inputs(seed=0):
    out = dict(first_inputs(seed))
    for name, value in second_inputs(seed + 1).items():
        if name != "x":
            out[name + "_2"] = value
    return out


def reference(
    x, c, ada_w, ada_b, norm_mix_g, w_in, rwkv_mu, rwkv_w0, rwkv_w2, rwkv_a0, rwkv_a2, rwkv_g2,
    rwkv_v0, rwkv_v1, rwkv_v2, rwkv_kk, rwkv_ka, rwkv_rk, rwkv_lnx_w, rwkv_lnx_b, rwkv_out,
    sg_ln_w, sg_ln_b, sg_ws, sg_bs, sg_out, conv_w, conv_out, s5_a_re, s5_a_im, s5_b_re,
    s5_b_im, s5_c_re, s5_c_im, s5_d, s5_log_dt, s5_glu_w, w_o, norm_ffn_g, ffn_w1, ffn_w2,
    final_g, norm_mix_g_2, w_in_2, b_forget_2, w_branch_a_2, w_branch_b_2, w_out_2,
    norm_ffn_g_2, w_peer_q_2, peer_sub_keys_2, peer_expert_u_2, peer_expert_v_2, norm_final_g_2,
):
    x = first_block(
        x, c, ada_w, ada_b, norm_mix_g, w_in, rwkv_mu, rwkv_w0, rwkv_w2, rwkv_a0, rwkv_a2,
        rwkv_g2, rwkv_v0, rwkv_v1, rwkv_v2, rwkv_kk, rwkv_ka, rwkv_rk, rwkv_lnx_w, rwkv_lnx_b,
        rwkv_out, sg_ln_w, sg_ln_b, sg_ws, sg_bs, sg_out, conv_w, conv_out, s5_a_re, s5_a_im,
        s5_b_re, s5_b_im, s5_c_re, s5_c_im, s5_d, s5_log_dt, s5_glu_w, w_o, norm_ffn_g, ffn_w1,
        ffn_w2, final_g,
    )
    return second_block(
        x, norm_mix_g_2, w_in_2, b_forget_2, w_branch_a_2, w_branch_b_2, w_out_2, norm_ffn_g_2,
        w_peer_q_2, peer_sub_keys_2, peer_expert_u_2, peer_expert_v_2, norm_final_g_2,
    )


_drawn_inputs = setup_inputs


def setup_inputs(seed=0):
    import zlib

    import numpy as np

    out = dict(_drawn_inputs(seed))
    spreads = {}
    factors = {'rwkv_w2': 4.403,
     'rwkv_a0': 4.418,
     'rwkv_lnx_w': 3.091,
     'rwkv_lnx_b': 6.764,
     'sg_ln_w': 3.187,
     'sg_ln_b': 8.0,
     's5_a_re': 64.0,
     's5_a_im': 36.784,
     's5_b_re': 44.656,
     's5_b_im': 46.096,
     's5_c_re': 41.496,
     's5_c_im': 46.024,
     's5_log_dt': 38.536,
     'norm_mix_g_2': 3.421,
     'norm_final_g_2': 8.055,
     'norm_ffn_g_2': 6.112}
    for name, (base, spread) in spreads.items():
        noise = np.random.default_rng([zlib.crc32(name.encode()), seed]).standard_normal(out[name].shape)
        drawn = base * np.exp(spread * noise) if base else spread * noise
        out[name] = __import__('jax').numpy.asarray(drawn.astype(out[name].dtype))
    for name, factor in factors.items():
        out[name] = (out[name] * factor).astype(out[name].dtype)
    return out
```

```python
from contextlib import ExitStack

import numpy as np

import concourse.bass as bass
from concourse import mybir

ALU = mybir.AluOpType
ACT = mybir.ActivationFunctionType
F32 = mybir.dt.float32
U32 = mybir.dt.uint32
X = mybir.AxisListType.X

P = 128
S = 256
D = 1024
RING = 4
TILE = 4096
ARENA = 25500
NG = 16

C_MU, C_W0, C_A0, C_KK, C_KA, C_RK, C_CONV, C_SD = 0, 7, 9, 11, 13, 15, 17, 23
C_ARE, C_AIM, C_DT, C_C, C_GMIX, C_GFFN, C_GMIX2, C_ADAB, N_COLS = 25, 33, 41, 49, 57, 65, 73, 81, 113

R_LNXW, R_LNXB, R_SGW, R_SGB, R_BF, N_ROWA = 0, 256, 512, 768, 1024, 1032

K_ID, K_SU, K_IU, K_SL, K_NEG, K_BLK, K_HSEL, K_ROT, K_COS, K_SIN = 0, 128, 256, 384, 512, 640, 768, 770, 898, 1154
K_LEV, K_IOTA, N_K = 1410, 1410 + 7 * 128, 1410 + 7 * 128 + 16


class Queue:

    def __init__(self, eng, sem, chain):
        self.eng, self.sem, self.chain = eng, sem, chain
        self.count, self.last, self.seen = 0, None, {}

    def wait(self, *tokens):
        need = {}
        for t in tokens:
            if t is not None and self.seen.get(t[0].name, 0) < t[1]:
                self.seen[t[0].name] = t[1]
                need[t[0].name] = t
        for s, n in need.values():
            self.eng.wait_ge(s, n)

    def do(self, f, *tokens, loose=False, count=True):
        if self.chain and not loose:
            tokens = tokens + (self.last,)
        self.wait(*tokens)
        ins = f()
        if count:
            ins.then_inc(self.sem, 1)
            self.count += 1
            self.last = (self.sem, self.count)
        return self.last

    def dma(self, f, sem, value, *tokens):
        self.wait(*tokens)
        f().then_inc(sem, 16)
        return (sem, value)


def build(nc, A, out, scratch=None):
    with ExitStack() as ctx:
        def sb(name, shape, dt=F32):
            return ctx.enter_context(nc.sbuf_tensor(name, shape, dt))

        def sem(name):
            return ctx.enter_context(nc.semaphore(name))

        V = Queue(nc.vector, sem("v"), True)
        SC = Queue(nc.scalar, sem("a"), True)
        G = Queue(nc.gpsimd, sem("g"), True)
        PE = Queue(nc.tensor, sem("pe"), False)
        SP = Queue(nc.sync, sem("sp"), False)
        v, sc, gp, te = nc.vector, nc.scalar, nc.gpsimd, nc.tensor

        ring = sb("ring", [P, RING, TILE])
        xr = sb("xr", [P, 2, D])
        hT = sb("hT", [P, 8, S])
        cols = sb("cols", [P, N_COLS])
        rowa = sb("rowa", [P, N_ROWA])
        K = sb("K", [P, N_K])
        gt = sb("gt", [P, 2, D])
        modT = sb("modT", [P, 32])
        small = sb("small", [P, 64])
        ones = sb("ones", [P, P])
        cact = sb("cact", [P, 16])
        cb = sb("cb", [P, 8, P])
        arena = sb("arena", [P, ARENA])
        banks = [ctx.enter_context(nc.psum_tensor(f"ps{i}", [P, 512], F32)) for i in range(8)]
        drained = [()] * 8
        turn = {"main": 0, "misc": 0}
        POOLS = {"main": (0, 1, 2, 3), "misc": (4, 5, 6, 7)}

        top = [0]

        def area(*shape):
            n = int(np.prod(shape))
            a = arena[:, top[0]:top[0] + n]
            top[0] += n
            assert top[0] <= ARENA, top
            if len(shape) == 2:
                a = a.rearrange("p (a b) -> p a b", a=shape[0])
            if len(shape) == 3:
                a = a.rearrange("p (a b c) -> p a b c", a=shape[0], b=shape[1])
            return a

        def bank(pool):
            t = turn[pool]
            turn[pool] = t + 1
            return POOLS[pool][t % 4]

        ident, su, iu, sl, neg = (K[:, o:o + 128] for o in (K_ID, K_SU, K_IU, K_SL, K_NEG))
        blk, hsel, rotm = K[:, K_BLK:K_BLK + 128], K[:, K_HSEL:K_HSEL + 2], K[:, K_ROT:K_ROT + 128]

        def load(name, dst, src, *tokens, q=SC):
            s = sem("l_" + name)
            return q.dma(lambda: q.eng.dma_start(dst, src), s, 16, *tokens)

        t_cols = load("cols", cols[:], A["cols"])
        t_x = load("x", xr[:], A["x"])
        t_K = load("K", K[:], A["K"])
        t_rowa = load("rowa", rowa[:], A["rowa"].broadcast_to([P, N_ROWA]))

        stream = ([("ada", i, TILE) for i in range(4)] + [("wp", i, TILE) for i in range(5)]
                  + [("gates", 4, TILE), ("gates", 5, TILE), ("gates", 2, TILE), ("gates", 3, TILE),
                     ("o_ab", 0, TILE), ("o_c", 0, 2048),
                     ("ada", 4, TILE), ("ada", 5, TILE), ("gates", 6, TILE), ("gates", 7, TILE), ("glu", 0, TILE),
                     ("gates", 0, TILE), ("gates", 1, TILE)]
                  + [("ada", i, TILE) for i in range(6, 12)]
                  + [("o_ab", 0, TILE)]
                  + [("w_o", i, TILE) for i in range(2)]
                  + [("w1", 0, TILE)]
                  + [x for i in range(8) for x in ([("w1", i + 1, TILE)] if i < 7 else []) + [("w2", i, TILE)]]
                  + [("qkv", i, TILE) for i in range(6)]
                  + [("ba", 0, TILE), ("bb", 0, TILE)] + [("g2", i, TILE) for i in range(4)]
                  + [("wout", i, TILE) for i in range(2)]
                  + [("pq", i, TILE) for i in range(4)] + [("keys", 0, 2048)])
        ring_sems = [sem(f"ring{i}") for i in range(RING)]
        state = {"loaded": 0, "used": 0, "free": [()] * RING}

        def prefetch():
            n = state["loaded"]
            if n == len(stream):
                return
            state["loaded"] += 1
            name, i, w = stream[n]
            r = n % RING
            dst, src = ring[:, r, 0:w], A[name][i]
            SP.dma(lambda: nc.sync.dma_start(dst, src), ring_sems[r], 16 * (n // RING + 1), *state["free"][r])

        for _ in range(RING):
            prefetch()

        def tile(name, i=0):
            n = state["used"]
            assert stream[n][:2] == (name, i), (stream[n], name, i)
            state["used"] += 1
            return ring[:, n % RING, :], (ring_sems[n % RING], 16 * (n // RING + 1)), n % RING

        def done(r, *tokens):
            state["free"][r] = tokens
            prefetch()

        def mm(o, pairs, *tokens):
            n = len(pairs)
            for i, (l, r) in enumerate(pairs):
                t = PE.do(lambda l=l, r=r, i=i: te.matmul(o, l, r, start=(i == 0), stop=(i == n - 1)),
                          *(tokens if i == 0 else ()), count=(i == n - 1))
            return t

        def tr(o, i, *tokens):
            return PE.do(lambda: te.transpose(o, i, ident), *tokens)

        t_one = V.do(lambda: v.memset(ones[:], 1.0))
        t_sg = SC.do(lambda: sc.activation(cact[:, 8:16], cols[:, C_C:C_C + 8], ACT.Sigmoid), t_cols)
        t_c = V.do(lambda: v.tensor_tensor(cact[:, 0:8], cols[:, C_C:C_C + 8], cact[:, 8:16], ALU.mult), t_sg, t_cols)
        for k in range(8):
            t_cb = V.do(lambda k=k: v.tensor_scalar(cb[:, k, :], ones[:], cact[:, k:k + 1], None, ALU.mult), t_one, t_c)

        mrow = area(512)
        junk = area(D)
        merged = area(2, D)
        xn = area(2, D)
        base2 = top[0]
        gtb = gt[:].rearrange("p a b -> p (a b)")
        t_gtb = load("gtb", gtb, A["adab_g"].broadcast_to([P, 2 * D]))

        m_tok = {"row": None, "gt": t_gtb}

        def mod_T(i, j0):
            w, tw, r = tile("ada", i)
            b = bank("misc")
            t = mm(banks[b][0:1, :], [(cact[:, k:k + 1], w[:, k * 512:(k + 1) * 512]) for k in range(8)],
                   tw, t_c, *drained[b])
            done(r, t)
            ta = V.do(lambda: v.tensor_copy(mrow[0:1, :], banks[b][0:1, :]), t, m_tok["row"])
            drained[b] = (ta,)
            b2 = bank("misc")
            for q in range(4):
                t = mm(banks[b2][:, q:q + 1], [(mrow[0:1, q * 128:(q + 1) * 128], ones[0:1, 0:1])], ta, t_one,
                       *drained[b2])
            tc = V.do(lambda: v.tensor_tensor(modT[:, j0:j0 + 4], banks[b2][:, 0:4],
                                              cols[:, C_ADAB + j0:C_ADAB + j0 + 4], ALU.add), t, t_cols)
            drained[b2] = (tc,)
            m_tok["row"] = t
            return tc

        def mod_gt(i, which, half):
            w, tw, r = tile("ada", i)
            b = bank("misc")
            t = mm(banks[b][:], [(cb[:, k, :], w[:, k * 512:(k + 1) * 512]) for k in range(8)], tw, t_cb, *drained[b])
            done(r, t)
            dst = gt[:, which, half * 512:(half + 1) * 512]
            m_tok["gt"] = V.do(lambda: v.tensor_tensor(dst, dst, banks[b][:], ALU.add), t, m_tok["gt"])
            drained[b] = (m_tok["gt"],)

        def rms(dst, gain=None, *tokens):
            o = 0
            t1 = []
            for tt in range(2):
                t1.append(SC.do(lambda tt=tt: sc.activation(junk, xr[:, tt, :], ACT.Square,
                                                            accum_out=small[:, tt:tt + 1]), *tokens))
            V.do(lambda: v.tensor_scalar(small[:, 2:4], small[:, 0:2], 1.0 / D, 1e-6, ALU.mult, ALU.add), *t1)
            t2 = SC.do(lambda: sc.activation(small[:, 4:6], small[:, 2:4], ACT.Sqrt), V.last)
            V.do(lambda: v.reciprocal(small[:, 6:8], small[:, 4:6]), t2)
            r = []
            for tt in range(2):
                if gain is None:
                    r.append(V.do(lambda tt=tt: v.tensor_scalar(dst[:, tt, :], xr[:, tt, :], small[:, 6 + tt:7 + tt],
                                                                None, ALU.mult)))
                else:
                    r.append(V.do(lambda tt=tt: v.scalar_tensor_tensor(dst[:, tt, :], xr[:, tt, :],
                                                                       small[:, 6 + tt:7 + tt], gain, ALU.mult,
                                                                       ALU.mult)))
            return r

        def to_T(src, dst, toks, evac):
            ts = []
            for k in range(8):
                b = bank("misc")
                for tt in range(2):
                    t = tr(banks[b][:, tt * 128:(tt + 1) * 128], src[:, tt, k * 128:(k + 1) * 128], toks[tt], t_K,
                           *drained[b])
                te_ = evac(k, dst[:, k, :], banks[b][:, 0:S], t)
                drained[b] = (te_,)
                ts.append(te_)
            return ts

        def norm_T(gain, sh, scl, toks, *after):
            if scl is None:
                def ev(k, o, i, t):
                    return SC.do(lambda: sc.mul(o, i, cols[:, gain + k:gain + k + 1]), t, t_cols, *after)
            else:
                tg = V.do(lambda: v.scalar_tensor_tensor(small[:, 8:16], modT[:, scl:scl + 8], 1.0,
                                                         cols[:, gain:gain + 8], ALU.add, ALU.mult), t_cols, *after)

                def ev(k, o, i, t):
                    return SC.do(lambda: sc.activation(o, i, ACT.Identity, bias=modT[:, sh + k:sh + k + 1],
                                                       scale=small[:, 8 + k:9 + k]), t, tg, *after)
            return to_T(xn, hT, toks, ev)

        t_xn = rms(xn, None, t_x)
        tm = [mod_T(i, 4 * i) for i in range(4)]
        t_h = norm_T(C_GMIX, 0, 8, t_xn, *tm)
        hl = t_h[-1]

        def gemm_T(w, chunk, o, *tokens):
            return mm(o, [(w[:, k * 512 + chunk * 128:k * 512 + chunk * 128 + 128], hT[:, k, :]) for k in range(8)],
                      *tokens)

        def gemm_rows(w, tt, o, n0, n, *tokens):
            return mm(o, [(hT[:, k, tt * 128:(tt + 1) * 128], w[:, k * 512 + n0:k * 512 + n0 + n]) for k in range(8)],
                      *tokens)

        pc = area(6, S)
        uB = area(2, S)
        vB = area(2, S)
        pa = area(7, 257)
        uD = area(2, S)
        gb = area(2, 2, D)
        t_z = V.do(lambda: v.memset(pa[:, :, 0:1], 0.0))
        dest = {**{c: pa[:, c, 1:257] for c in range(7)}, 7: uB[:, 0, :], 8: uB[:, 1, :],
                **{11 + i: pc[:, i, :] for i in range(6)}, 17: uD[:, 0, :], 18: uD[:, 1, :]}
        tp = {}
        for i in range(5):
            w, tw, r = tile("wp", i)
            ch = 0
            while ch < 4 and 4 * i + ch < 19:
                c = 4 * i + ch
                b = bank("main")
                if c == 9:
                    for tt in range(2):
                        t = gemm_rows(w, tt, banks[b][:, tt * S:(tt + 1) * S], 128, 256, tw, hl, *drained[b])
                    te_ = SC.do(lambda b=b: sc.activation(vB.rearrange("p a b -> p (a b)"), banks[b][:],
                                                          ACT.Gelu_apprx_tanh), t)
                    tp[9] = te_
                    ch += 2
                else:
                    t = gemm_T(w, ch, banks[b][:, 0:S], tw, hl, *drained[b])
                    if c in (7, 8):
                        te_ = SC.do(lambda b=b, c=c: sc.activation(dest[c], banks[b][:, 0:S], ACT.Gelu_apprx_tanh), t)
                    elif c % 2:
                        te_ = SC.do(lambda b=b, c=c: sc.copy(dest[c], banks[b][:, 0:S]), t)
                    else:
                        te_ = V.do(lambda b=b, c=c: v.tensor_copy(dest[c], banks[b][:, 0:S]), t)
                    tp[c] = te_
                    ch += 1
                drained[b] = (te_,)
            done(r, t)

        gtok = {}

        def gate_tile(g, slot, *tokens):
            w, tw, r = tile("gates", g)
            ts = []
            for tt in range(2):
                b = bank("main")
                t = gemm_rows(w, tt, banks[b][:], 0, 512, tw, hl, *drained[b])
                o = gb[:, slot, tt, (g % 2) * 512:(g % 2) * 512 + 512]
                te_ = SC.do(lambda b=b, o=o: sc.activation(o, banks[b][:], ACT.Sigmoid), t, *tokens)
                drained[b] = (te_,)
                ts.append(te_)
            done(r, t)
            gtok[g] = ts

        mt = {}

        def merge(br, slot, zT, toff, w, w0, tw, tz, first):
            for tt in range(2):
                for hf in range(2):
                    b = bank("main")
                    t = mm(banks[b][:], [(zT[:, c, toff + tt * 128:toff + (tt + 1) * 128],
                                          w[:, w0 + c * D + hf * 512:w0 + c * D + hf * 512 + 512]) for c in range(2)],
                           tw, *tz, *drained[b])
                    gsl = gb[:, slot, tt, hf * 512:(hf + 1) * 512]
                    m = merged[:, tt, hf * 512:(hf + 1) * 512]
                    tg = gtok[2 * br + hf][tt]
                    if first:
                        te_ = V.do(lambda b=b, g=gsl, m=m: v.tensor_tensor(m, g, banks[b][:], ALU.mult), t, tg)
                        drained[b] = (te_,)
                    else:
                        te_ = V.do(lambda b=b, g=gsl: v.tensor_tensor(g, g, banks[b][:], ALU.mult), t, tg)
                        drained[b] = (te_,)
                        te_ = G.do(lambda g=gsl, m=m: gp.tensor_tensor(m, m, g, ALU.add), te_, mt[(tt, hf)])
                    mt[(tt, hf)] = te_
            return t

        mark = top[0]
        zc = area(2, 258)
        yc = area(2, S)
        V.do(lambda: v.memset(zc[:, :, 0:2], 0.0))
        V.do(lambda: v.tensor_tensor(zc[:, :, 2:258], pc[:, 2:4, :], pc[:, 4:6, :], ALU.mult),
             *[tp[c] for c in range(11, 17)])
        for c in range(2):
            for j in range(3):
                cw = cols[:, C_CONV + 2 * j + c:C_CONV + 2 * j + c + 1]
                if j == 0:
                    V.do(lambda c=c, cw=cw: v.tensor_scalar(yc[:, c, :], zc[:, c, 0:S], cw, None, ALU.mult))
                else:
                    V.do(lambda c=c, cw=cw, j=j: v.scalar_tensor_tensor(yc[:, c, :], zc[:, c, j:j + S], cw,
                                                                        yc[:, c, :], ALU.mult, ALU.add))
        t_yc = V.do(lambda: v.tensor_tensor(yc, yc, pc[:, 0:2, :], ALU.mult))

        vln = area(2, S)
        zB = area(2, S)
        bnb = area(2, 2, 6)
        wsT = area(4, 128)
        bsT = area(2, 128)
        t_ws = load("ws", wsT, A["ws"], q=SP)
        t_bs = load("bs", bsT, A["bs"], q=SP)
        tws = G.do(lambda: gp.tensor_tensor(wsT, wsT, iu.unsqueeze(1).broadcast_to([P, 4, P]), ALU.mult), t_ws, t_K)

        def mean_var(src, dst, n):
            V.do(lambda: v.bn_stats(bnb[:, 0, 0, :], src))
            V.do(lambda: v.bn_aggr(dst, bnb[:, 0, 0, :]))

        V.wait(tp[9])
        for tt in range(2):
            mean_var(vB[:, tt, :], small[:, 20 + 2 * tt:22 + 2 * tt], 256)
        mv = small[:, 20:24].rearrange("p (a b) -> p a b", b=2)
        V.do(lambda: v.tensor_scalar(small[:, 24:26].unsqueeze(2), mv[:, :, 1:2], 1e-5, None, ALU.add))
        ts_ = SC.do(lambda: sc.activation(small[:, 26:28], small[:, 24:26], ACT.Sqrt), V.last)
        V.do(lambda: v.reciprocal(small[:, 28:30], small[:, 26:28]), ts_)
        for tt in range(2):
            V.do(lambda tt=tt: v.tensor_scalar(vln[:, tt, :], vB[:, tt, :], small[:, 20 + 2 * tt:21 + 2 * tt],
                                               small[:, 28 + tt:29 + tt], ALU.subtract, ALU.mult))
        V.do(lambda: v.tensor_tensor(vln, vln, rowa[:, R_SGW:R_SGW + 256].unsqueeze(1).broadcast_to([P, 2, S]),
                                     ALU.mult), t_rowa)
        t_vln = V.do(lambda: v.tensor_tensor(vln, vln, rowa[:, R_SGB:R_SGB + 256].unsqueeze(1).broadcast_to([P, 2, S]),
                                             ALU.add))

        gate_tile(4, 0)
        tzb = []
        for pr in range(2):
            b = bank("misc")
            for n in range(2):
                t = mm(banks[b][:, n * S:(n + 1) * S],
                       [(vln[:, n, pr * 128:(pr + 1) * 128], wsT[:, 2 * pr:2 * pr + 2, :])], t_vln, tws, *drained[b])
            for g in range(2):
                pv = banks[b][64 * g:64 * g + 64, :].rearrange("p (n g t) -> p n g t", n=2, g=2)[:, :, g, :]
                o = zB[64 * g:64 * g + 64, pr, :].rearrange("p (n t) -> p n t", n=2)
                bsv = bsT[64 * g:64 * g + 64, pr, :].unsqueeze(1).broadcast_to([64, 2, P])
                te_ = V.do(lambda pv=pv, o=o, bsv=bsv: v.tensor_tensor(o, pv, bsv, ALU.add), t, t_bs)
            drained[b] = (te_,)
        t_zb = V.do(lambda: v.tensor_tensor(zB, zB, uB, ALU.mult), tp[7], tp[8])
        gate_tile(5, 0)
        gate_tile(2, 1)
        gate_tile(3, 1)
        w, tw, r = tile("o_ab")
        w2_, tw2, r2 = tile("o_c")
        tC = merge(2, 0, yc, 0, w2_, 0, tw2, (t_yc,), True)
        tB = merge(1, 1, zB, 0, w, 2048, tw, (t_zb,), False)
        done(r, tB)
        done(r2, tC)
        t_free_c = (tB, tC, V.last)
        gb_free = {0: tuple(mt[k] for k in mt), 1: tuple(mt[k] for k in mt)}
        top[0] = mark

        keep = top[0]
        top[0] = base2 - 2 * D
        MT, Mak, Mrb, Mrk, Dm, DT, Mo, Xs = (area(4, 128) for _ in range(8))
        L = area(2, S)
        top[0] = keep
        ps = area(7, S)
        a6 = ps[:, 6, :]
        lw = area(2, S)
        Wp = area(2, S)
        aa = area(2, S)
        gr = area(2, S)
        kk = area(2, S)
        tmp = area(2, S)
        vr = area(2, S)
        W6 = area(768)
        t_w6 = load("w6", W6, A["w6"], *t_free_c, q=SP)
        V.do(lambda: v.tensor_tensor(ps, pa[:, :, 0:S], pa[:, :, 1:257], ALU.subtract), *[tp[c] for c in range(7)],
             *t_free_c)
        for c in range(7):
            V.do(lambda c=c: v.scalar_tensor_tensor(ps[:, c, :], ps[:, c, :], cols[:, C_MU + c:C_MU + c + 1],
                                                    pa[:, c, 1:257], ALU.mult, ALU.add), t_cols)
        t_ps = V.last
        rT, kT, vT = ps[:, 0:2, :], ps[:, 2:4, :], ps[:, 4:6, :]
        SC.do(lambda: sc.activation(a6[0:32, :], a6[0:32, :], ACT.Tanh), t_ps)
        t_a6 = SC.do(lambda: sc.activation(a6[64:128, :], a6[64:128, :], ACT.Sigmoid))
        b1, b2, b3 = bank("misc"), bank("misc"), bank("misc")
        for c in range(2):
            t1 = mm(banks[b1][:, c * S:(c + 1) * S], [(W6[:, c * 128:(c + 1) * 128], a6)], t_a6, t_w6, *drained[b1])
        for c in range(2):
            t2 = mm(banks[b2][:, c * S:(c + 1) * S], [(W6[:, 256 + c * 128:256 + (c + 1) * 128], a6)], *drained[b2])
        for tt in range(2):
            t3 = mm(banks[b3][:, tt * S:(tt + 1) * S], [(a6[:, tt * 128:(tt + 1) * 128], W6[:, 512:768])],
                    *drained[b3])
        for c in range(2):
            te_ = SC.do(lambda c=c: sc.activation(lw[:, c, :], banks[b1][:, c * S:(c + 1) * S], ACT.Sigmoid,
                                                  bias=cols[:, C_W0 + c:C_W0 + c + 1]), t1, t_cols)
        drained[b1] = (te_,)
        t_lw = te_
        for c in range(2):
            te_ = SC.do(lambda c=c: sc.activation(aa[:, c, :], banks[b2][:, c * S:(c + 1) * S], ACT.Sigmoid,
                                                  bias=cols[:, C_A0 + c:C_A0 + c + 1]), t2)
        drained[b2] = (te_,)
        t_aa = te_
        t_gr = SC.do(lambda: sc.copy(gr.rearrange("p a b -> p (a b)"), banks[b3][:]), t3)
        drained[b3] = (t_gr,)
        b = bank("misc")
        for tt in range(2):
            for c in range(2):
                t = tr(banks[b][:, tt * S + c * 128:tt * S + (c + 1) * 128], vT[:, c, tt * 128:(tt + 1) * 128], t_ps,
                       *drained[b])
        t_vr = SC.do(lambda b=b: sc.copy(vr.rearrange("p a b -> p (a b)"), banks[b][:]), t)
        drained[b] = (t_vr,)
        for c in range(2):
            V.do(lambda c=c: v.tensor_scalar(kk[:, c, :], kT[:, c, :], cols[:, C_KK + c:C_KK + c + 1], None, ALU.mult))
        t = V.do(lambda: v.tensor_tensor(tmp, kk, kk, ALU.mult))
        b = bank("misc")
        t = mm(banks[b][:], [(blk, tmp)], t, *drained[b])
        tf = tmp.rearrange("p a b -> p (a b)")
        te_ = SC.do(lambda b=b: sc.activation(tf, banks[b][:], ACT.Sqrt), t)
        drained[b] = (te_,)
        V.do(lambda: v.tensor_scalar(tf, tf, 1e-12, None, ALU.max), te_)
        V.do(lambda: v.reciprocal(tf, tf))
        V.do(lambda: v.tensor_tensor(kk, kk, tmp, ALU.mult))
        for c in range(2):
            V.do(lambda c=c: v.tensor_scalar(tmp[:, c, :], aa[:, c, :], -1.0, cols[:, C_KA + c:C_KA + c + 1], ALU.add,
                                             ALU.mult), t_aa)
        V.do(lambda: v.scalar_tensor_tensor(kT, tmp, 1.0, kT, ALU.add, ALU.mult))
        for c in range(2):
            V.do(lambda c=c: v.scalar_tensor_tensor(tmp[:, c, :], rT[:, c, :], cols[:, C_RK + c:C_RK + c + 1],
                                                    kT[:, c, :], ALU.mult, ALU.mult))
        tb_ = V.last
        bon = small[:, 32:40]
        b = bank("misc")
        for tt in range(2):
            for c in range(2):
                t = mm(banks[b][:, 4 * tt + 2 * c:4 * tt + 2 * c + 2], [(tmp[:, c, tt * 128:(tt + 1) * 128], hsel)],
                       tb_, *drained[b])
        t_bon = SC.do(lambda b=b: sc.copy(bon, banks[b][:, 0:8]), t)
        drained[b] = (t_bon,)
        V.do(lambda: v.tensor_scalar(lw, lw, -float(np.exp(-0.5)), None, ALU.mult), t_lw)
        for c in range(2):
            for tt in range(2):
                sl_ = slice(tt * 128, (tt + 1) * 128)
                V.do(lambda c=c, s_=sl_: v.tensor_tensor_scan(L[:, c, s_], ones[:], lw[:, c, s_], 0.0, ALU.mult,
                                                              ALU.add))
        em = small[:, 40:48]
        L4 = L.rearrange("p c (a t) -> p (c a) t", t=128)
        V.do(lambda: v.tensor_copy(em[:, 0:4].unsqueeze(2), L4[:, :, 63:64]))
        V.do(lambda: v.tensor_tensor(em[:, 4:8].unsqueeze(2), L4[:, :, 127:128], L4[:, :, 63:64], ALU.subtract))
        V.do(lambda: v.tensor_tensor(L4, L4, em[:, 0:4].unsqueeze(2).broadcast_to([P, 4, P]), ALU.subtract))
        V.do(lambda: v.tensor_tensor(Wp, L, lw, ALU.subtract))
        t_L = V.last
        Lf, Wf = L.rearrange("p a b -> p (a b)"), Wp.rearrange("p a b -> p (a b)")
        lwf = lw.rearrange("p a b -> p (a b)")
        SC.do(lambda: sc.activation(Wf, Wf, ACT.Exp), t_L)
        SC.do(lambda: sc.activation(lwf, Lf, ACT.Exp))
        SC.do(lambda: sc.activation(Lf, Lf, ACT.Exp, scale=-1.0))
        t_W = SC.do(lambda: sc.activation(em, em, ACT.Exp))
        pb4 = pa.rearrange("p a b -> p (a b)")
        at_, bt_ = (pb4[:, i * 512:(i + 1) * 512].rearrange("p (a b) -> p a b", a=2) for i in range(2))
        kt_ = pb4[:, 1024:1536].rearrange("p (a b) -> p a b", a=2)
        V.do(lambda: v.scalar_tensor_tensor(at_, kk, -1.0, Wp, ALU.mult, ALU.mult), t_W)
        V.do(lambda: v.tensor_tensor(bt_, kk, aa, ALU.mult))
        V.do(lambda: v.tensor_tensor(bt_, bt_, L, ALU.mult))
        V.do(lambda: v.tensor_tensor(kt_, kT, L, ALU.mult))
        V.do(lambda: v.tensor_tensor(rT, rT, lw, ALU.mult))
        t_abkr = V.last
        am = area(2, 2, S)
        rm = area(2, 2, S)
        for e in range(2):
            hs = K[:, K_HSEL + e:K_HSEL + e + 1]
            SC.do(lambda e=e, hs=hs: sc.mul(am[:, e, :, :], at_, hs), t_abkr)
            t_arm = SC.do(lambda e=e, hs=hs: sc.mul(rm[:, e, :, :], rT, hs))

        U = area(4, 64)
        St = area(2, 128)
        oo = area(2, S)
        lev = lambda i: K[:, K_LEV + i * 128:K_LEV + (i + 1) * 128].unsqueeze(1).broadcast_to([P, 4, P])
        bc4 = lambda m: m.unsqueeze(1).broadcast_to([P, 4, P])
        f4 = lambda a: a.rearrange("p a b -> p (a b)")

        t_o = []
        prev_reads = {}

        def head_mats(tt, lhs, rhs, dst, mask, *after):
            b = bank("misc")
            sl_ = slice(tt * 128, (tt + 1) * 128)
            for h in range(4):
                t = mm(banks[b][:, h * 128:(h + 1) * 128], [(lhs[:, h // 2, sl_], rhs[:, h % 2, h // 2, sl_])],
                       t_arm, t_abkr, *drained[b])
            te_ = V.do(lambda: v.tensor_tensor(f4(dst), banks[b][:], bc4(mask), ALU.mult), t, *after)
            drained[b] = (te_,)
            return te_

        fillers = []

        def fill(n=1):
            for _ in range(n):
                if fillers:
                    fillers.pop(0)()

        fillers += [lambda: mod_gt(4, 0, 0), lambda: mod_gt(5, 0, 1), lambda: gate_tile(6, 0, *gb_free[0]),
                    lambda: gate_tile(7, 0)]
        tU = None
        for tt in range(2):
            t_MT = head_mats(tt, bt_, am, MT, su, PE.last, G.last)
            t_Mak = head_mats(tt, kt_, am, Mak, su)
            t_Mrb = head_mats(tt, bt_, rm, Mrb, iu)
            t_Mrk = head_mats(tt, kt_, rm, Mrk, iu)
            G.do(lambda: gp.tensor_tensor(Mo, MT, lev(0), ALU.mult), t_MT, PE.last)
            t_DT = G.do(lambda: gp.tensor_tensor(DT, Mo, bc4(ident), ALU.add), PE.last)
            b = bank("misc")
            for h in range(4):
                t = tr(banks[b][:, h * 128:(h + 1) * 128], DT[:, h, :], t_DT, *drained[b])
            t_D = SC.do(lambda b=b: sc.copy(f4(Dm), banks[b][:]), t)
            drained[b] = (t_D,)
            t_moread = None
            for k in range(1, 7):
                t_Mo = G.do(lambda k=k: gp.tensor_tensor(Mo, MT, lev(k), ALU.mult), t_moread)
                bx = bank("misc")
                for h in range(4):
                    t = mm(banks[bx][:, h * 128:(h + 1) * 128], [(Mo[:, h, :], Dm[:, h, :])], t_Mo, t_D,
                           *drained[bx])
                t_moread = t
                t_X = SC.do(lambda bx=bx: sc.copy(f4(Xs), banks[bx][:]), t)
                drained[bx] = (t_X,)
                by = bank("misc")
                if k < 6:
                    for h in range(4):
                        t = mm(banks[by][:, h * 128:(h + 1) * 128], [(DT[:, h, :], Xs[:, h, :])], t_X, t_DT,
                               *drained[by])
                    t_D = V.do(lambda by=by: v.tensor_tensor(f4(Dm), f4(Dm), banks[by][:], ALU.add), t)
                    drained[by] = (t_D,)
                    bz = bank("misc")
                else:
                    bz = by
                for h in range(4):
                    t = mm(banks[bz][:, h * 128:(h + 1) * 128], [(Xs[:, h, :], DT[:, h, :])], t_X, t_DT, *drained[bz])
                t_DT = V.do(lambda bz=bz: v.tensor_tensor(f4(DT), f4(DT), banks[bz][:], ALU.add), t)
                drained[bz] = (t_DT,)
                if k % 3 == 0:
                    fill()
            b = bank("misc")
            for h in range(4):
                c, e = h // 2, h % 2
                sl_ = slice(tt * 128, (tt + 1) * 128)
                pairs = [(Mak[:, h, :], vr[:, tt, h * 64:h * 64 + 64])]
                if tt:
                    pairs.append((am[:, e, c, sl_], St[:, c, e * 64:e * 64 + 64]))
                t = mm(banks[b][:, h * 64:h * 64 + 64], pairs, t_Mak, t_vr, *([tS] if tt else []), *drained[b])
            Xv = f4(Xs)[:, 0:256]
            t_X = SC.do(lambda b=b: sc.copy(Xv, banks[b][:, 0:256]), t)
            drained[b] = (t_X,)
            b = bank("misc")
            for h in range(4):
                t = mm(banks[b][:, h * 64:h * 64 + 64], [(DT[:, h, :], Xv[:, h * 64:h * 64 + 64])], t_X, t_DT,
                       *drained[b])
            t_U = SC.do(lambda b=b: sc.copy(f4(U), banks[b][:, 0:256]), t)
            drained[b] = (t_U,)
            b = bank("misc")
            for h in range(4):
                c, e = h // 2, h % 2
                sl_ = slice(tt * 128, (tt + 1) * 128)
                pairs = [(Mrb[:, h, :], U[:, h, :]), (Mrk[:, h, :], vr[:, tt, h * 64:h * 64 + 64])]
                if tt:
                    pairs.append((rm[:, e, c, sl_], St[:, c, e * 64:e * 64 + 64]))
                t = mm(banks[b][:, h * 64:h * 64 + 64], pairs, t_U, t_Mrb, t_Mrk, *drained[b])
            te_ = SC.do(lambda b=b, tt=tt: sc.copy(oo[:, tt, :], banks[b][:, 0:256]), t)
            drained[b] = (te_,)
            t_o.append(te_)
            if tt == 0:
                b = bank("misc")
                for i, src in enumerate((bt_, kt_)):
                    for c in range(2):
                        t = tr(banks[b][:, (i * 2 + c) * 128:(i * 2 + c + 1) * 128], src[:, c, 0:128], t_abkr,
                               *drained[b])
                bkr = f4(Mo)
                t_r = SC.do(lambda b=b: sc.copy(bkr, banks[b][:]), t, t)
                drained[b] = (t_r,)
                b = bank("misc")
                for c in range(2):
                    t = mm(banks[b][:, c * 128:(c + 1) * 128],
                           [(bkr[:, c * 128:(c + 1) * 128], f4(U)[:, c * 128:(c + 1) * 128]),
                            (bkr[:, 256 + c * 128:256 + (c + 1) * 128], vr[:, 0, c * 128:(c + 1) * 128])],
                           t_r, t_U, t_vr, *drained[b])
                for c in range(2):
                    V.do(lambda b=b, c=c: v.tensor_scalar(St[:, c, :], banks[b][:, c * 128:(c + 1) * 128],
                                                          em[:, 4 + 2 * c:5 + 2 * c], em[:, 2 * c + 1:2 * c + 2],
                                                          ALU.mult, ALU.mult), t, t_W)
                tS = V.last
                drained[b] = (tS,)
            fill()
        V.wait(*t_o)
        mvh = small[:, 48:64].rearrange("p (a b) -> p a b", b=2)
        bn8 = area(8, 6)
        for i in range(8):
            src = oo[:, i // 4, (i % 4) * 64:(i % 4 + 1) * 64]
            V.do(lambda src=src, i=i: v.bn_stats(bn8[:, i, :], src))
        for i in range(8):
            V.do(lambda i=i: v.bn_aggr(mvh[:, i, :], bn8[:, i, :]))
        rs8 = small[:, 8:16]
        V.do(lambda: v.tensor_scalar(rs8.unsqueeze(2), mvh[:, :, 1:2], 64e-5, None, ALU.add))
        ts_ = SC.do(lambda: sc.activation(rs8, rs8, ACT.Sqrt), V.last)
        V.do(lambda: v.reciprocal(rs8, rs8), ts_)
        o8 = oo.rearrange("p a (h i) -> p (a h) i", h=4)
        V.do(lambda: v.tensor_tensor(o8, o8, mvh[:, :, 0:1].broadcast_to([P, 8, 64]), ALU.subtract))
        V.do(lambda: v.tensor_tensor(o8, o8, rs8.unsqueeze(2).broadcast_to([P, 8, 64]), ALU.mult))
        V.do(lambda: v.tensor_tensor(oo, oo, rowa[:, R_LNXW:R_LNXW + 256].unsqueeze(1).broadcast_to([P, 2, S]),
                                     ALU.mult))
        V.do(lambda: v.tensor_tensor(oo, oo, rowa[:, R_LNXB:R_LNXB + 256].unsqueeze(1).broadcast_to([P, 2, S]),
                                     ALU.add))
        vr8 = vr.rearrange("p a (h i) -> p (a h) i", h=4)
        V.do(lambda: v.tensor_tensor(vr8, vr8, bon.unsqueeze(2).broadcast_to([P, 8, 64]), ALU.mult), t_bon, PE.last)
        V.do(lambda: v.tensor_tensor(oo, oo, vr, ALU.add))
        t = V.do(lambda: v.tensor_tensor(oo, oo, gr, ALU.mult), t_gr)
        b = bank("misc")
        for c in range(2):
            for tt in range(2):
                t2 = tr(banks[b][:, c * S + tt * 128:c * S + (tt + 1) * 128], oo[:, tt, c * 128:(c + 1) * 128], t,
                        *drained[b])
        zA = kk
        t_zA = SC.do(lambda b=b: sc.copy(f4(zA), banks[b][:]), t2)
        drained[b] = (t_zA,)
        while fillers:
            fill()
        rw_end = (t_zA, V.last, G.last)

        top[0] = mark
        ps_, _lw, _wp, _aa, _gr, zA_ = area(7, S), area(2, S), area(2, S), area(2, S), area(2, S), area(2, S)
        zA = zA_
        t5 = rw_end + (PE.last,)
        sp = area(16, 8)
        pw = area(24)
        bre = area(4, 128)
        bim = area(4, 128)
        xa = area(2, 4, S)
        xb = area(2, 4, S)
        yD = area(2, S)
        lre, lim, dt_, mag, abr, abi, qr, qi = (sp[:, i, :] for i in range(8))
        s1, s2, s3, s4, s5_, s6 = (sp[:, i, :] for i in range(8, 14))
        V.do(lambda: v.tensor_scalar(lre, cols[:, C_ARE:C_ARE + 8], -1e-4, None, ALU.min), *t5)
        V.do(lambda: v.tensor_copy(lim, cols[:, C_AIM:C_AIM + 8]))
        t = SC.do(lambda: sc.activation(dt_, cols[:, C_DT:C_DT + 8], ACT.Exp), V.last, *t5)
        V.do(lambda: v.tensor_tensor(s1, lre, dt_, ALU.mult), t)
        t = SC.do(lambda: sc.activation(mag, s1, ACT.Exp), V.last)
        V.do(lambda: v.tensor_tensor(s1, lim, dt_, ALU.mult), t)
        BIG = 12582912.0
        V.do(lambda: v.tensor_scalar(s2, s1, float(np.float32(1 / (2 * np.pi))), BIG, ALU.mult, ALU.add))
        V.do(lambda: v.tensor_scalar(s2, s2, -BIG, None, ALU.add))
        for cst in (6.28125, 0.0019350051879882812, 3.0199159819567e-07):
            V.do(lambda cst=cst: v.scalar_tensor_tensor(s1, s2, -cst, s1, ALU.mult, ALU.add))
        V.do(lambda: v.tensor_scalar(s1, s1, 3.1415925, -3.1415925, ALU.min, ALU.max))
        V.do(lambda: v.tensor_scalar(s3, s1, 0.5, None, ALU.mult))
        SC.do(lambda: sc.activation(s4, s1, ACT.Sin), V.last)
        t = SC.do(lambda: sc.activation(s5_, s3, ACT.Sin))
        V.do(lambda: v.tensor_tensor(s5_, s5_, s5_, ALU.mult), t)
        V.do(lambda: v.tensor_scalar(s5_, s5_, -2.0, 1.0, ALU.mult, ALU.add))
        V.do(lambda: v.tensor_tensor(abr, mag, s5_, ALU.mult))
        V.do(lambda: v.tensor_tensor(abi, mag, s4, ALU.mult))
        V.do(lambda: v.tensor_tensor(s1, lre, lre, ALU.mult))
        V.do(lambda: v.tensor_tensor(s2, lim, lim, ALU.mult))
        V.do(lambda: v.tensor_tensor(s1, s1, s2, ALU.add))
        V.do(lambda: v.reciprocal(s1, s1))
        V.do(lambda: v.tensor_scalar(s2, abr, -1.0, None, ALU.add))
        V.do(lambda: v.tensor_tensor(s3, s2, lre, ALU.mult))
        V.do(lambda: v.tensor_tensor(s4, abi, lim, ALU.mult))
        V.do(lambda: v.tensor_tensor(s3, s3, s4, ALU.add))
        V.do(lambda: v.tensor_tensor(qr, s3, s1, ALU.mult))
        V.do(lambda: v.tensor_tensor(s3, abi, lre, ALU.mult))
        V.do(lambda: v.tensor_tensor(s4, s2, lim, ALU.mult))
        V.do(lambda: v.tensor_tensor(s3, s3, s4, ALU.subtract))
        V.do(lambda: v.tensor_tensor(qi, s3, s1, ALU.mult))
        V.do(lambda: v.tensor_scalar(s6, qi, -1.0, None, ALU.mult))
        nqi = s6
        s5sem = sem("s5ld")
        s5n = [0]

        def s5load(dst, src, *tokens):
            s5n[0] += 16
            return SP.dma(lambda: nc.sync.dma_start(dst, src), s5sem, s5n[0], *tokens)

        t_prev = t5
        for hf in range(2):
            s5load(bre, A["s5b"][2 * hf], *t_prev)
            tl = s5load(bim, A["s5b"][2 * hf + 1])
            for q in range(4):
                b = bank("misc")
                for i, wt in enumerate((bre, bim)):
                    t = mm(banks[b][:, i * S:(i + 1) * S], [(wt[:, q, :], uD[:, hf, :])], tl, tp[17], tp[18],
                           *drained[b])
                j = 4 * hf + q
                for i in range(2):
                    s_a = (qr if i == 0 else qi)[:, j:j + 1]
                    s_b = (nqi if i == 0 else qr)[:, j:j + 1]
                    te1 = SC.do(lambda b=b, i=i, q=q, s_a=s_a: sc.mul(xa[:, i, q, :], banks[b][:, 0:S], s_a), t,
                                V.last)
                    te_ = V.do(lambda b=b, i=i, q=q, s_b=s_b: v.scalar_tensor_tensor(
                        xa[:, i, q, :], banks[b][:, S:2 * S], s_b, xa[:, i, q, :], ALU.mult, ALU.add), te1)
                drained[b] = (te_, te1)
            pr_, pi_, npi = pw[:, 0:4], pw[:, 4:8], pw[:, 8:12]
            V.do(lambda hf=hf: v.tensor_copy(pr_, abr[:, 4 * hf:4 * hf + 4]))
            V.do(lambda hf=hf: v.tensor_copy(pi_, abi[:, 4 * hf:4 * hf + 4]))
            V.do(lambda: v.tensor_scalar(npi, pi_, -1.0, None, ALU.mult))
            src, dst = xa, xb
            for lv in range(8):
                s_ = 1 << lv
                tc_ = SC.do(lambda src=src, dst=dst, s_=s_: sc.copy(dst[:, :, :, 0:s_], src[:, :, :, 0:s_]), V.last)
                n = S - s_
                for q in range(4):
                    for i in range(2):
                        a_, b_ = (pr_, npi) if i == 0 else (pr_, pi_)
                        V.do(lambda src=src, dst=dst, q=q, i=i, a_=a_, s_=s_, n=n: v.scalar_tensor_tensor(
                            dst[:, i, q, s_:S], src[:, i, q, 0:n], a_[:, q:q + 1], src[:, i, q, s_:S], ALU.mult,
                            ALU.add))
                        V.do(lambda src=src, dst=dst, q=q, i=i, b_=b_, s_=s_, n=n: v.scalar_tensor_tensor(
                            dst[:, i, q, s_:S], src[:, 1 - i, q, 0:n], b_[:, q:q + 1], dst[:, i, q, s_:S], ALU.mult,
                            ALU.add))
                t1_, t2_, t3_ = pw[:, 12:16], pw[:, 16:20], pw[:, 20:24]
                V.do(lambda: v.tensor_tensor(t1_, pr_, pr_, ALU.mult))
                V.do(lambda: v.tensor_tensor(t2_, pi_, pi_, ALU.mult))
                V.do(lambda: v.tensor_tensor(t3_, pr_, pi_, ALU.mult))
                V.do(lambda: v.tensor_tensor(pr_, t1_, t2_, ALU.subtract))
                V.do(lambda: v.tensor_scalar(pi_, t3_, 2.0, None, ALU.mult))
                V.do(lambda: v.tensor_scalar(npi, t3_, -2.0, None, ALU.mult))
                src, dst = dst, src
                V.wait(tc_)
            s5load(bre, A["s5c"][2 * hf], t)
            tl = s5load(bim, A["s5c"][2 * hf + 1])
            b = bank("misc")
            for i, wt in enumerate((bre, bim)):
                t = mm(banks[b][:, i * S:(i + 1) * S], [(wt[:, q, :], xa[:, i, q, :]) for q in range(4)], tl,
                       V.last, tc_, *drained[b])
            V.do(lambda hf=hf, b=b: v.scalar_tensor_tensor(yD[:, hf, :], uD[:, hf, :],
                                                           cols[:, C_SD + hf:C_SD + hf + 1], banks[b][:, 0:S],
                                                           ALU.mult, ALU.add), t)
            te_ = V.do(lambda hf=hf, b=b: v.tensor_tensor(yD[:, hf, :], yD[:, hf, :], banks[b][:, S:2 * S],
                                                          ALU.subtract))
            drained[b] = (te_,)
            t_prev = (t,)
        t_yD = SC.do(lambda: sc.activation(f4(yD), f4(yD), ACT.Gelu_apprx_tanh), te_)

        def glu():
            w, tw, r = tile("glu")
            sgm = area(512)
            tsg = None
            for tt in range(2):
                for hf in range(2):
                    bs_ = []
                    for part in (1, 0):
                        b = bank("main")
                        t = mm(banks[b][:], [(yD[:, c, tt * 128:(tt + 1) * 128],
                                              w[:, c * 2048 + part * D + hf * 512:
                                                c * 2048 + part * D + hf * 512 + 512]) for c in range(2)],
                               tw, t_yD, *drained[b])
                        bs_.append(b)
                        if part == 1:
                            tsg = SC.do(lambda b=b: sc.activation(sgm, banks[b][:], ACT.Sigmoid), t, V.last)
                            drained[b] = (tsg,)
                    gsl = gb[:, 0, tt, hf * 512:(hf + 1) * 512]
                    m = merged[:, tt, hf * 512:(hf + 1) * 512]
                    te_ = V.do(lambda b=b: v.tensor_tensor(sgm, sgm, banks[b][:], ALU.mult), t, tsg)
                    drained[b] = (te_,)
                    te_ = V.do(lambda g=gsl: v.tensor_tensor(g, g, sgm, ALU.mult), gtok[6 + hf][tt])
                    te_ = G.do(lambda g=gsl, m=m: gp.tensor_tensor(m, m, g, ALU.add), te_, mt[(tt, hf)])
                    mt[(tt, hf)] = te_
            done(r, t)

        glu()
        gate_tile(0, 1, *gb_free[1])
        gate_tile(1, 1)
        tm2 = [mod_T(i, 16 + 4 * (i - 6)) for i in range(6, 10)]
        mod_gt(10, 1, 0)
        mod_gt(11, 1, 1)
        w, tw, r = tile("o_ab")
        tA = merge(0, 1, zA, 0, w, 0, tw, (t_zA,), False)
        done(r, tA)

        top[0] = mark
        mer = [mt[(tt, 0)] for tt in range(2)], [mt[(tt, 1)] for tt in range(2)]
        tmerge = [mt[(1, 1)], mt[(1, 1)]]

        def cp(k, o, i, t):
            if k % 2:
                return SC.do(lambda: sc.copy(o, i), t)
            return V.do(lambda: v.tensor_copy(o, i), t)

        def residual(names, lhsT_of, nk, toks, gate, kw=512, tiles_of=None):
            ts = []
            for hf in range(2):
                w, tw, r = tile(names, hf)
                for tt in range(2):
                    b = bank("main")
                    t = mm(banks[b][:], [(lhsT_of(k, tt), w[:, k * 512:(k + 1) * 512]) for k in range(nk)], tw,
                           *toks, *drained[b])
                    ts.append(add_x(b, tt, hf, gate, t))
                done(r, t)
            return ts

        def add_x(b, tt, hf, gate, t):
            xs = xr[:, tt, hf * 512:(hf + 1) * 512]
            if gate is not None:
                js = junk[:, 0:512]
                V.do(lambda: v.tensor_tensor(js, gt[:, gate, hf * 512:(hf + 1) * 512], banks[b][:], ALU.mult), t,
                     m_tok["gt"])
                drained[b] = (V.last,)
                return V.do(lambda: v.tensor_tensor(xs, xs, js, ALU.add))
            te_ = V.do(lambda: v.tensor_tensor(xs, xs, banks[b][:], ALU.add), t)
            drained[b] = (te_,)
            return te_

        tmT = to_T(merged, hT, tmerge, cp)
        tx = residual("w_o", lambda k, tt: hT[:, k, tt * 128:(tt + 1) * 128], 8, tmT[-2:], 0)

        t_xn = rms(xn, None, *tx)
        t_h = norm_T(C_GFFN, 16, 24, t_xn, *tm2)
        hl = t_h[-1]
        fT = area(2, 4, S)
        f_free = [(), ()]
        facc = [4, 5, 6, 7]
        t_f = {}

        def up(j):
            w, tw, r = tile("w1", j)
            ts = []
            for pr in range(2):
                b = bank("main")
                for c in range(2):
                    t = gemm_T(w, 2 * pr + c, banks[b][:, c * S:(c + 1) * S], tw, hl, *drained[b])
                o = fT[:, j % 2, 2 * pr:2 * pr + 2, :].rearrange("p a b -> p (a b)")
                te_ = SC.do(lambda b=b, o=o: sc.activation(o, banks[b][:], ACT.Relu), t, *f_free[j % 2])
                drained[b] = (te_,)
                ts.append(G.do(lambda o=o: gp.tensor_tensor(o, o, o, ALU.mult), te_))
            done(r, t)
            t_f[j] = ts

        acc_t = {}

        def down(j):
            w, tw, r = tile("w2", j)
            for tt in range(2):
                for hf in range(2):
                    b = facc[2 * tt + hf]
                    for c in range(4):
                        first, last = j == 0 and c == 0, j == 7 and c == 3
                        l = fT[:, j % 2, c, tt * 128:(tt + 1) * 128]
                        rr = w[:, c * D + hf * 512:c * D + hf * 512 + 512]
                        t = PE.do(lambda b=b, l=l, rr=rr, first=first, last=last: te.matmul(
                            banks[b][:], l, rr, start=first, stop=last), tw, *t_f[j], *(drained[b] if first else ()))
                    acc_t[(tt, hf)] = t
            f_free[j % 2] = (t,)
            done(r, t)

        up(0)
        for j in range(8):
            if j < 7:
                up(j + 1)
            down(j)
        tx = [add_x(facc[2 * tt + hf], tt, hf, 1, acc_t[(tt, hf)]) for tt in range(2) for hf in range(2)]

        fg = area(D)
        t_fg = load("fg", fg, A["rowb"][0:1, :].broadcast_to([P, D]), PE.last, V.last, q=SP)
        t_x1 = rms(xr, fg, t_fg, *tx)
        t_xn = rms(xn, None, *t_x1)
        t_h = norm_T(C_GMIX2, None, None, t_xn)
        hl = t_h[-1]
        top[0] = base2
        qT_ = area(4, S)
        kT2 = area(4, S)
        pexp = area(8, S)
        pT = area(2, 3, 128)
        yT = area(8, S)
        lf = area(2, 8)
        wf = area(8, 8)
        rot_t = area(S)
        sA = area(2, 512)
        blk_end = (PE.last, V.last, SC.last, G.last)
        t_wf = load("wf", wf.rearrange("p a b -> p (a b)"), A["wf"], *blk_end, q=SP)
        b = bank("misc")
        for tt in range(2):
            t = mm(banks[b][:, tt * 8:tt * 8 + 8],
                   [(hT[:, k, tt * 128:(tt + 1) * 128], wf[:, k, :]) for k in range(8)], t_wf, hl, *drained[b])
        fx, fe = small[:, 16:32], small[:, 32:48]
        V.do(lambda b=b: v.tensor_tensor(fx.rearrange("p (a b) -> p a b", a=2),
                                         banks[b][:, 0:16].rearrange("p (a b) -> p a b", a=2),
                                         rowa[:, R_BF:R_BF + 8].unsqueeze(1).broadcast_to([P, 2, 8]), ALU.add), t)
        drained[b] = (V.last,)
        V.do(lambda: v.tensor_scalar(fe, fx, -1.0, None, ALU.mult))
        V.do(lambda: v.tensor_tensor(fe, fx, fe, ALU.max))
        t = SC.do(lambda: sc.activation(fe, fe, ACT.Exp, scale=-1.0), V.last)
        t = SC.do(lambda: sc.activation(fe, fe, ACT.Ln, bias=1.0), t)
        lff = lf.rearrange("p a b -> p (a b)")
        V.do(lambda: v.tensor_scalar(fx, fx, 0.0, None, ALU.min), t)
        t_lf = V.do(lambda: v.tensor_tensor(lff, fx, fe, ALU.subtract), *blk_end)
        b = bank("misc")
        mm(banks[b][:, 0:8], [(iu, lf[:, 0, :])], t_lf, *drained[b])
        t = mm(banks[b][:, 8:16], [(ones[:], lf[:, 0, :]), (iu, lf[:, 1, :])])
        cq = small[:, 48:64]
        t_cq = V.do(lambda b=b: v.tensor_copy(cq, banks[b][:, 0:16]), t)
        drained[b] = (t_cq,)
        nlf = cact[:, 0:16].rearrange("p (a b) -> p a b", a=2)
        t_nlf = V.do(lambda: v.tensor_scalar(cact[:, 0:16], lff, -1.0, None, ALU.mult), PE.last)
        ut = area(2, S)
        V.do(lambda: v.tensor_copy(ut[:, 0, 0:128], iu))
        V.do(lambda: v.tensor_copy(ut[:, 0, 128:256], ones[:]))
        V.do(lambda: v.memset(ut[:, 1, 0:128], 0.0))
        t_ut = V.do(lambda: v.tensor_copy(ut[:, 1, 128:256], iu))

        def project_T(i, dst, rope, scl):
            w, tw, r = tile("qkv", i)
            ts = []
            for c in range(4):
                b = bank("main")
                t = gemm_T(w, c, banks[b][:, 0:S], tw, hl, *drained[b])
                d_ = dst[:, c, :]
                te_ = SC.do(lambda b=b, d_=d_: sc.mul(d_, banks[b][:, 0:S], scl), t, PE.last)
                drained[b] = (te_,)
                if rope:
                    b2 = bank("misc")
                    t2 = mm(banks[b2][:, 0:S], [(rotm, d_)], te_, *drained[b2])
                    V.do(lambda b2=b2: v.tensor_tensor(rot_t, banks[b2][:, 0:S], K[:, K_SIN:K_SIN + S], ALU.mult), t2)
                    drained[b2] = (V.last,)
                    V.do(lambda d_=d_: v.tensor_tensor(d_, d_, K[:, K_COS:K_COS + S], ALU.mult), te_)
                    te_ = V.do(lambda d_=d_: v.tensor_tensor(d_, d_, rot_t, ALU.add))
                ts.append(te_)
            done(r, t)
            return ts

        def project_rows(i, dst):
            w, tw, r = tile("qkv", i)
            ts = []
            for tt in range(2):
                b = bank("main")
                t = gemm_rows(w, tt, banks[b][:], 0, 512, tw, hl, *drained[b])
                te_ = SC.do(lambda b=b, tt=tt: sc.copy(dst[:, tt, :], banks[b][:]), t)
                drained[b] = (te_,)
                ts.append(te_)
            done(r, t)
            return ts

        def attention(kind, tq, tk, tv):
            for qt in range(2):
                nk = 128 * (qt + 1)
                te_ = None
                tz = []
                for h in range(8):
                    c, e = h // 2, h % 2
                    b = bank("misc")
                    ql = qT_[64 * e:64 * e + 64, c, qt * 128:(qt + 1) * 128]
                    kr = kT2[64 * e:64 * e + 64, c, 0:nk]
                    if kind:
                        pairs = [(ql, kr)] + [(lb(s, h), ut[:, s, 0:nk]) for s in range(qt + 1)]
                        t = mm(banks[b][:, 0:nk], pairs, *tq, *tk, t_ut, t_lb, *drained[b])
                    else:
                        t = mm(banks[b][:, 0:nk], [(ql, kr)], *tq, *tk, *drained[b])
                    te1 = V.do(lambda b=b, h=h, nk=nk: v.tensor_tensor(pexp[:, h, nk - 128:nk],
                                                                      banks[b][:, nk - 128:nk], neg, ALU.add), t,
                                *pfree[h])
                    te2 = None
                    if qt:
                        te2 = SC.do(lambda b=b, h=h: sc.copy(pexp[:, h, 0:128], banks[b][:, 0:128]), t, te1)
                    drained[b] = (te1, te2)
                    V.do(lambda h=h, nk=nk: v.tensor_reduce(small[:, h:h + 1], pexp[:, h, 0:nk], X, ALU.max), te2)
                    V.do(lambda h=h: v.tensor_scalar(small[:, 8 + h:9 + h], small[:, h:h + 1], -1.0, None, ALU.mult))
                    if kind:
                        V.do(lambda h=h, qt=qt: v.tensor_tensor(small[:, h:h + 1], small[:, h:h + 1],
                                                                cq[:, 8 * qt + h:8 * qt + h + 1], ALU.add))
                        V.do(lambda h=h, qt=qt: v.tensor_tensor(small[:, 8 + h:9 + h],
                                                                cq[:, 8 * qt + h:8 * qt + h + 1],
                                                                small[:, h:h + 1], ALU.subtract))
                    tz = SC.do(lambda h=h, nk=nk: sc.activation(pexp[:, h, 0:nk], pexp[:, h, 0:nk], ACT.Exp,
                                                                bias=small[:, 8 + h:9 + h],
                                                                accum_out=small[:, 16 + h:17 + h]), V.last)
                    V.do(lambda h=h: v.reciprocal(small[:, 24 + h:25 + h], small[:, 16 + h:17 + h]), tz)
                    tn = V.do(lambda h=h, nk=nk: v.tensor_scalar(pexp[:, h, 0:nk], pexp[:, h, 0:nk],
                                                                 small[:, 24 + h:25 + h], None, ALU.mult))
                    b = bank("misc")
                    for kc in range(qt + 1):
                        t = tr(banks[b][:, kc * 128:(kc + 1) * 128], pexp[:, h, kc * 128:(kc + 1) * 128], tn,
                               *drained[b])
                    pfree[h] = (t,)
                    pt = pT[:, e, 0:qt + 1, :].rearrange("p a b -> p (a b)")
                    tpt = SC.do(lambda b=b, pt=pt, nk=nk: sc.copy(pt, banks[b][:, 0:nk]), t, *ptfree[e])
                    drained[b] = (tpt,)
                    b = bank("misc")
                    t = mm(banks[b][:, 0:128], [
                        (vrow(kind, kc, c), pT[:, e, kc, :]) for kc in range(qt + 1)], tpt, *tv, *drained[b])
                    ptfree[e] = (t,)
                    o = yT[64 * e:64 * e + 64, 4 * kind + c, qt * 128:(qt + 1) * 128]
                    te_ = V.do(lambda b=b, o=o, e=e: v.tensor_copy(o, banks[b][64 * e:64 * e + 64, 0:128]), t)
                    drained[b] = (te_,)
            return te_

        vals = {}

        def vrow(kind, kc, c):
            return vals[kind][:, kc, c * 128:(c + 1) * 128]

        lbt = area(2, 8, 128)
        for s_ in range(2):
            for h in range(8):
                t_lb = G.do(lambda s_=s_, h=h: gp.tensor_scalar(lbt[:, s_, h, :], ones[:], nlf[:, s_, h:h + 1], None,
                                                                ALU.mult), t_nlf, *blk_end)
        lb = lambda s_, h: lbt[:, s_, h, :]
        pfree = {h: () for h in range(8)}
        ptfree = {0: (), 1: ()}
        SC.wait(*blk_end)
        tq = project_T(0, qT_, True, 0.125)
        tk = project_T(1, kT2, True, 1.0)
        vals[0] = area(2, 512)
        tv = project_rows(2, vals[0])
        ty = attention(0, tq, tk, tv)
        tq = project_T(3, qT_, False, 0.125)
        tk = project_T(4, kT2, False, 1.0)
        vals[1] = vals[0]
        SC.wait(PE.last, V.last)
        tv = project_rows(5, vals[1])
        ty2 = attention(1, tq, tk, tv)

        wA, twA, rA = tile("ba")
        wB, twB, rB = tile("bb")
        mg = merged
        for br, (w_, tw_, r_) in enumerate(((wA, twA, rA), (wB, twB, rB))):
            for tt in range(2):
                for hf in range(2):
                    b = bank("main")
                    t = mm(banks[b][:], [(yT[:, 4 * br + c, tt * 128:(tt + 1) * 128],
                                          w_[:, c * D + hf * 512:c * D + hf * 512 + 512]) for c in range(4)],
                           tw_, ty, ty2, *drained[b])
                    o = (mg if br == 0 else xn)[:, tt, hf * 512:(hf + 1) * 512]
                    te_ = SC.do(lambda b=b, o=o: sc.copy(o, banks[b][:]), t, *blk_end)
                    drained[b] = (te_,)
            done(r_, t)
        t_br = te_
        for i in range(4):
            w, tw, r = tile("g2", i)
            for tt in range(2):
                b = bank("main")
                t = gemm_rows(w, tt, banks[b][:], 0, 512, tw, hl, *drained[b])
                s_ = sA[:, tt, :]
                te1 = SC.do(lambda b=b, s_=s_: sc.activation(s_, banks[b][:], ACT.Sigmoid), t, V.last)
                drained[b] = (te1,)
                o = (mg if i < 2 else xn)[:, tt, (i % 2) * 512:(i % 2) * 512 + 512]
                te_ = V.do(lambda s_=s_, o=o: v.tensor_tensor(o, o, s_, ALU.mult), te1, t_br)
                if i >= 2:
                    m_ = mg[:, tt, (i % 2) * 512:(i % 2) * 512 + 512]
                    te_ = V.do(lambda o=o, m_=m_: v.tensor_tensor(m_, m_, o, ALU.add))
            done(r, t)
        tmT = to_T(mg, hT, [te_, te_], lambda k, o, i, t: cp(k, o, i, t))
        tx = residual("wout", lambda k, tt: hT[:, k, tt * 128:(tt + 1) * 128], 8, tmT[-2:], None)

        fg2 = fg
        t_fg = load("fg2", gt[:], A["rowb2"].broadcast_to([P, 2 * D]), V.last, q=SP)
        t_xn = rms(xn, gt[:, 0, :], t_fg, *tx)
        t_h = to_T(xn, hT, t_xn, cp)
        top[0] = base2
        qp = area(16, S)
        scr = area(16, 128)
        tpq = []
        pre = (PE.last, V.last, SC.last)
        for i in range(4):
            w, tw, r = tile("pq", i)
            for c in range(4):
                b = bank("main")
                t = gemm_T(w, c, banks[b][:, 0:S], tw, *t_h[-2:], *drained[b])
                o = qp[:, 4 * i + c, :]
                te_ = SC.do(lambda b=b, o=o: sc.copy(o, banks[b][:, 0:S]), t, *pre)
                drained[b] = (te_,)
            done(r, t)
        t_qp = te_
        keys, tkey, rkey = tile("keys")

        sv = area(16, 16)
        siu = area(16, 16)
        sif = area(16, 16)
        work = area(128)
        cand = area(8, 256)
        cw = area(256)
        best = area(8, 16)
        pku = area(8, 16)
        pkf = area(8, 16)
        eq = area(8, 256)
        e01 = area(2, 128)
        idx = area(2, 128)
        gat = area(2, 128)
        hv = area(2, 128)
        av = area(2, 128)
        sm = area(8)
        iota = K[:, K_IOTA:K_IOTA + 16]
        U_ = lambda a: a.bitcast(U32)
        t_idx = []
        t_gat = []
        for tt in range(2):
            for g in range(4):
                b = bank("misc")
                for j in range(4):
                    hp = 4 * g + j
                    t = mm(banks[b][:, j * 128:(j + 1) * 128],
                           [(qp[:, hp, tt * 128:(tt + 1) * 128], keys[:, hp * 128:(hp + 1) * 128])], t_qp, tkey,
                           *drained[b])
                te_ = SC.do(lambda b=b, g=g: sc.copy(scr[:, 4 * g:4 * g + 4, :].rearrange("p a b -> p (a b)"),
                                                     banks[b][:]), t, V.last, *pre)
                drained[b] = (te_,)
            if tt == 1:
                done(rkey, t)
            V.wait(te_)
            for hp in range(16):
                s_ = scr[:, hp, :]
                V.do(lambda s_=s_, hp=hp: v.max(sv[:, hp, 0:8], s_))
                V.do(lambda s_=s_, hp=hp: v.max_index(U_(siu[:, hp, 0:8]), sv[:, hp, 0:8], s_))
                V.do(lambda s_=s_, hp=hp: v.match_replace(work, sv[:, hp, 0:8], s_, -3.0e38))
                V.do(lambda hp=hp: v.max(sv[:, hp, 8:16], work))
                V.do(lambda hp=hp: v.max_index(U_(siu[:, hp, 8:16]), sv[:, hp, 8:16], work))
            V.do(lambda: v.tensor_copy(sif, U_(siu)))
            for h in range(8):
                V.do(lambda h=h: v.tensor_tensor(cand[:, h, :].rearrange("p (i j) -> p i j", i=16),
                                                 sv[:, 2 * h, :].unsqueeze(2).broadcast_to([P, 16, 16]),
                                                 sv[:, 2 * h + 1, :].unsqueeze(1).broadcast_to([P, 16, 16]), ALU.add))
                cd = cand[:, h, :]
                V.do(lambda cd=cd, h=h: v.max(best[:, h, 0:8], cd))
                V.do(lambda cd=cd, h=h: v.max_index(U_(pku[:, h, 0:8]), best[:, h, 0:8], cd))
                V.do(lambda cd=cd, h=h: v.match_replace(cw, best[:, h, 0:8], cd, -3.0e38))
                V.do(lambda h=h: v.max(best[:, h, 8:16], cw))
                V.do(lambda h=h: v.max_index(U_(pku[:, h, 8:16]), best[:, h, 8:16], cw))
            for side in range(2):
                op, arg = (ALU.logical_shift_right, 4) if side == 0 else (ALU.bitwise_and, 15)
                V.do(lambda op=op, arg=arg: v.tensor_single_scalar(U_(pkf), U_(pku), arg, op))
                V.do(lambda: v.tensor_copy(cw[:, 0:128], U_(pkf).rearrange("p a b -> p (a b)")))
                e3 = eq.rearrange("p h (k i) -> p (h k) i", i=16)
                e4 = eq.rearrange("p h (k i) -> p h k i", i=16)
                V.do(lambda e3=e3: v.tensor_tensor(e3, cw[:, 0:128].unsqueeze(2).broadcast_to([P, 128, 16]),
                                                   iota.unsqueeze(1).broadcast_to([P, 128, 16]), ALU.is_equal))
                sf = sif.rearrange("p (h s) i -> p h s i", s=2)[:, :, side, :].unsqueeze(2).broadcast_to([P, 8, 16, 16])
                V.do(lambda e4=e4, sf=sf: v.tensor_tensor(e4, e4, sf, ALU.mult))
                V.do(lambda e3=e3, side=side: v.tensor_reduce(e01[:, side, :], e3, X, ALU.add))
            V.do(lambda: v.scalar_tensor_tensor(e01[:, 0, :], e01[:, 0, :], 128.0, e01[:, 1, :], ALU.mult, ALU.add))
            t_idx.append(V.do(lambda tt=tt: v.tensor_copy(U_(idx[:, tt, :]), e01[:, 0, :])))
            g3 = gat[:, tt, :].rearrange("p (h k) -> p h k", h=8)
            V.do(lambda g3=g3: v.tensor_tensor(g3, best, best[:, :, 0:1].broadcast_to([P, 8, 16]), ALU.subtract))
            t = SC.do(lambda tt=tt: sc.activation(gat[:, tt, :], gat[:, tt, :], ACT.Exp), V.last)
            V.do(lambda g3=g3: v.tensor_reduce(sm, g3, X, ALU.add), t)
            V.do(lambda: v.reciprocal(sm, sm))
            t_gat.append(V.do(lambda g3=g3: v.tensor_tensor(g3, g3, sm.unsqueeze(2).broadcast_to([P, 8, 16]),
                                                            ALU.mult)))

        rv = ring[:].rearrange("p r (a b) -> p (r a) b", b=D)
        slots = [rv[:, i, :] for i in range(NG)]
        gsem = [sem(f"gather{i}") for i in range(NG)]
        gn = [0]
        gfree = [()] * NG
        ring_quiet = PE.last

        def gather(table, tt, e):
            n = gn[0]
            gn[0] += 1
            i = n % NG
            ap = idx[:, tt, e:e + 1].bitcast(U32)
            return i, G.dma(lambda: gp.indirect_dma_start(slots[i], None, table,
                                                          bass.IndirectOffsetOnAxis(ap=ap, axis=0)),
                            gsem[i], 16 * (n // NG + 1), t_idx[tt], ring_quiet, *gfree[i])

        steps = [(tt, h) for tt in range(2) for h in range(8)]
        t_hv = {}
        t_av = {}

        def phase_u(tt, h):
            for k in range(16):
                e = 16 * h + k
                i, tg = gather(A["eu"], tt, e)
                t = V.do(lambda i=i, tt=tt, e=e: v.tensor_tensor_reduce(
                    out=junk, in0=slots[i], in1=xn[:, tt, :], scale=1.0, scalar=0.0, op0=ALU.mult, op1=ALU.add,
                    accum_out=hv[:, tt, e:e + 1]), tg)
                gfree[i] = (t,)
            o = slice(16 * h, 16 * h + 16)
            tg = SC.do(lambda: sc.activation(av[:, tt, o], hv[:, tt, o], ACT.Gelu), t)
            t_av[(tt, h)] = tg

        def phase_v(tt, h):
            o = slice(16 * h, 16 * h + 16)
            V.do(lambda: v.tensor_tensor(av[:, tt, o], av[:, tt, o], gat[:, tt, o], ALU.mult), t_av[(tt, h)],
                 t_gat[tt])
            for k in range(16):
                e = 16 * h + k
                i, tg = gather(A["ev"], tt, e)
                t = V.do(lambda i=i, tt=tt, e=e: v.scalar_tensor_tensor(
                    xr[:, tt, :], slots[i], av[:, tt, e:e + 1], xr[:, tt, :], ALU.mult, ALU.add), tg)
                gfree[i] = (t,)

        for n, (tt, h) in enumerate(steps):
            phase_u(tt, h)
            if n:
                phase_v(*steps[n - 1])
        phase_v(*steps[-1])

        t_fin = rms(xn, gt[:, 1, :], V.last)
        so = sem("out")
        SP.dma(lambda: nc.sync.dma_start(out, xn), so, 16, *t_fin)
        SP.wait((so, 16))


def shape_constants():
    k = np.zeros((P, N_K), np.float32)
    i = np.arange(P)
    k[:, K_ID:K_ID + 128] = np.eye(P)
    k[:, K_SU:K_SU + 128] = i[:, None] < i[None, :]
    k[:, K_IU:K_IU + 128] = i[:, None] <= i[None, :]
    k[:, K_SL:K_SL + 128] = i[:, None] > i[None, :]
    k[:, K_NEG:K_NEG + 128] = np.where(i[None, :] <= i[:, None], 0.0, -1e30)
    k[:, K_BLK:K_BLK + 128] = (i[:, None] // 64) == (i[None, :] // 64)
    k[:, K_HSEL:K_HSEL + 2] = (i[:, None] // 64) == np.arange(2)[None, :]
    d = i % 64
    for m in range(P):
        if d[m] < 8:
            k[m + 8, K_ROT + m] = -1.0
        elif d[m] < 16:
            k[m - 8, K_ROT + m] = 1.0
    freq = np.power(np.float32(500000.0), -np.arange(8, dtype=np.float32) / np.float32(8)).astype(np.float32)
    ang = np.arange(S, dtype=np.float32)[None, :] * freq[:, None]
    cos, sin = np.cos(ang), np.sin(ang)
    k[:, K_COS:K_COS + S] = 1.0
    for m in range(P):
        if d[m] < 16:
            k[m, K_COS:K_COS + S] = cos[d[m] % 8]
            k[m, K_SIN:K_SIN + S] = sin[d[m] % 8]
    for lv in range(7):
        s, t = i[:, None], i[None, :]
        m = (s >> (lv + 1) == t >> (lv + 1)) & ((s >> lv) & 1 == 0) & ((t >> lv) & 1 == 1)
        k[:, K_LEV + lv * 128:K_LEV + (lv + 1) * 128] = m
    k[:, K_IOTA:K_IOTA + 16] = np.arange(16)[None, :]
    return k


def lay_out(a):
    def t512(w):
        n = w.shape[1] // 512
        return np.ascontiguousarray(w.reshape(8, 128, n, 512).transpose(2, 1, 0, 3).reshape(n, 128, 4096))

    def kchunks(w):
        return w.reshape(-1, 128, w.shape[1]).transpose(1, 0, 2).reshape(128, -1)

    def col(x):
        return np.asarray(x).reshape(-1, 128).T

    f = np.float32
    ada = t512(a["ada_w"][0])
    ada = np.ascontiguousarray(ada[[0, 1, 2, 3, 4, 5, 6, 7, 8, 9, 10, 11]])
    ab = a["ada_b"][0]
    w_in = a["w_in"][0]
    wp = np.zeros((1024, 2560), f)
    wp[:, :2432] = w_in[:, :2432]
    cols = np.zeros((P, N_COLS), f)
    cols[:, C_MU:C_MU + 7] = col(a["rwkv_mu"][0])
    for c, n in ((C_W0, "rwkv_w0"), (C_A0, "rwkv_a0"), (C_KK, "rwkv_kk"), (C_KA, "rwkv_ka"), (C_RK, "rwkv_rk"),
                 (C_SD, "s5_d")):
        cols[:, c:c + 2] = col(a[n][0])
    for j in range(3):
        cols[:, C_CONV + 2 * j:C_CONV + 2 * j + 2] = col(a["conv_w"][0, j])
    cols[:, C_ARE:C_ARE + 8] = col(a["s5_a_re"][0])
    cols[:, C_AIM:C_AIM + 8] = col(a["s5_a_im"][0])
    cols[:, C_DT:C_DT + 8] = col(np.repeat(a["s5_log_dt"][0], 64))
    cols[:, C_C:C_C + 8] = col(a["c"])
    cols[:, C_GMIX:C_GMIX + 8] = col(a["norm_mix_g"])
    cols[:, C_GFFN:C_GFFN + 8] = col(a["norm_ffn_g"])
    cols[:, C_GMIX2:C_GMIX2 + 8] = col(a["norm_mix_g_2"])
    cols[:, C_ADAB:C_ADAB + 32] = col(np.concatenate([ab[0:2048], ab[3072:5120]]))
    rowa = np.zeros((1, N_ROWA), f)
    for r, n in ((R_LNXW, "rwkv_lnx_w"), (R_LNXB, "rwkv_lnx_b"), (R_SGW, "sg_ln_w"), (R_SGB, "sg_ln_b")):
        rowa[0, r:r + 256] = a[n][0]
    rowa[0, R_BF:R_BF + 8] = a["b_forget_2"][0]
    w6 = np.zeros((P, 768), f)
    w6[0:32, 0:256] = a["rwkv_w2"][0]
    w6[32:64, 256:512] = a["rwkv_a2"][0]
    w6[64:128, 512:768] = a["rwkv_g2"][0]
    ws = np.ascontiguousarray(a["sg_ws"][0].transpose(2, 0, 1))
    bs = np.zeros((P, 2, 128), f)
    for g in range(4):
        bs[64 * (g % 2):64 * (g % 2) + 64, g // 2, :] = a["sg_bs"][0, g][None, :]
    s5b = np.zeros((4, P, 4, 128), f)
    s5c = np.zeros((4, P, 4, 128), f)
    for i, (nb, ncn) in enumerate((("s5_b_re", "s5_c_re"), ("s5_b_im", "s5_c_im"))):
        for g in range(16):
            hf, q, e, ch = g // 8, (g % 8) // 2, g % 2, (g % 8) * 16
            s5b[2 * hf + i, ch:ch + 16, q, 64 * e:64 * e + 64] = a[nb][0, g].T
            s5c[2 * hf + i, 64 * e:64 * e + 64, q, ch:ch + 16] = a[ncn][0, g].T
    w2 = a["w_in_2"][0]
    return {
        "x": np.ascontiguousarray(a["x"][0].reshape(2, 128, 1024).transpose(1, 0, 2)),
        "cols": cols, "K": shape_constants(), "rowa": rowa,
        "ada": ada,
        "adab_g": np.ascontiguousarray(np.concatenate([ab[2048:3072], ab[5120:6144]])[None, :]),
        "wp": t512(wp), "gates": t512(w_in[:, 2432:6528]),
        "o_ab": np.ascontiguousarray(np.concatenate([kchunks(a["rwkv_out"][0]), kchunks(a["sg_out"][0])], 1)[None]),
        "o_c": np.ascontiguousarray(kchunks(a["conv_out"][0])[None]),
        "glu": np.ascontiguousarray(kchunks(a["s5_glu_w"][0])[None]),
        "w_o": t512(a["w_o"][0]), "w1": t512(a["ffn_w1"][0]),
        "w2": np.ascontiguousarray(a["ffn_w2"][0].reshape(8, 4, 128, 1024).transpose(0, 2, 1, 3).reshape(8, 128, 4096)),
        "w6": w6, "ws": ws, "bs": bs, "s5b": s5b, "s5c": s5c,
        "rowb": a["final_g"][None, :].copy(),
        "qkv": t512(w2[:, 0:3072]),
        "wf": np.ascontiguousarray(w2[:, 3072:3080].reshape(8, 128, 8).transpose(1, 0, 2).reshape(128, 64)),
        "g2": t512(w2[:, 3080:5128]),
        "ba": np.ascontiguousarray(kchunks(a["w_branch_a_2"][0])[None]),
        "bb": np.ascontiguousarray(kchunks(a["w_branch_b_2"][0])[None]),
        "wout": t512(a["w_out_2"][0]), "pq": t512(a["w_peer_q_2"][0]),
        "keys": np.ascontiguousarray(a["peer_sub_keys_2"][0].transpose(3, 0, 1, 2).reshape(1, 128, 2048)),
        "rowb2": np.concatenate([a["norm_ffn_g_2"][0], a["norm_final_g_2"]])[None, :].copy(),
        "eu": a["peer_expert_u_2"][0], "ev": a["peer_expert_v_2"][0],
    }


def kernel(**inputs):
    import concourse.bacc as _bacc
    from concourse.bass_utils import run_bass_kernel_spmd as _run

    a = lay_out({k: np.asarray(x) for k, x in inputs.items()})
    nc = _bacc.Bacc("TRN2", target_bir_lowering=False, num_devices=1)
    arrays, A = {}, {}
    for name, x in a.items():
        x = np.ascontiguousarray(x)
        arrays[f"in_{name}"] = x
        A[name] = nc.dram_tensor(f"in_{name}", x.shape, mybir.dt.from_np(x.dtype), kind="ExternalInput").ap()
    out = nc.dram_tensor("out_0", (P, 2, D), F32, kind="ExternalOutput").ap()
    build(nc, A, out)
    r = _run(nc, [arrays], core_ids=[0])
    return np.ascontiguousarray(r.results[0]["out_0"].transpose(1, 0, 2).reshape(1, S, D))
```

```python
from contextlib import ExitStack

import numpy as np

import concourse.bass as bass
from concourse import mybir

ALU = mybir.AluOpType
ACT = mybir.ActivationFunctionType
F32 = mybir.dt.float32
U32 = mybir.dt.uint32
X = mybir.AxisListType.X

P = 128
S = 256
D = 1024
RING = 3
TILE = 4096
ARENA = 31000
NG = 16

C_MU, C_W0, C_A0, C_KK, C_KA, C_RK, C_CONV, C_SD = 0, 7, 9, 11, 13, 15, 17, 23
C_ARE, C_AIM, C_DT, C_C, C_GMIX, C_GFFN, C_GMIX2, C_ADAB, N_COLS = 25, 33, 41, 49, 57, 65, 73, 81, 113

R_LNXW, R_LNXB, R_SGW, R_SGB, R_BF, N_ROWA = 0, 256, 512, 768, 1024, 1032

K_ID, K_SU, K_IU, K_SL, K_NEG, K_BLK, K_HSEL, K_ROT, K_COS, K_SIN = 0, 128, 256, 384, 512, 640, 768, 770, 898, 1154
K_LEV, K_IOTA, N_K = 1410, 1410 + 7 * 128, 1410 + 7 * 128 + 16


class Queue:

    def __init__(self, eng, sem, chain):
        self.eng, self.sem, self.chain = eng, sem, chain
        self.count, self.last, self.seen = 0, None, {}

    def wait(self, *tokens):
        need = {}
        for t in tokens:
            if t is not None and self.seen.get(t[0].name, 0) < t[1]:
                self.seen[t[0].name] = t[1]
                need[t[0].name] = t
        for s, n in need.values():
            self.eng.wait_ge(s, n)

    def do(self, f, *tokens, loose=False, count=True):
        if self.chain and not loose:
            tokens = tokens + (self.last,)
        self.wait(*tokens)
        ins = f()
        if count:
            ins.then_inc(self.sem, 1)
            self.count += 1
            self.last = (self.sem, self.count)
        return self.last

    def dma(self, f, sem, value, *tokens):
        self.wait(*tokens)
        f().then_inc(sem, 16)
        return (sem, value)


def build(nc, A, out, scratch=None):
    with ExitStack() as ctx:
        def sb(name, shape, dt=F32):
            return ctx.enter_context(nc.sbuf_tensor(name, shape, dt))

        def sem(name):
            return ctx.enter_context(nc.semaphore(name))

        V = Queue(nc.vector, sem("v"), True)
        SC = Queue(nc.scalar, sem("a"), True)
        G = Queue(nc.gpsimd, sem("g"), True)
        PE = Queue(nc.tensor, sem("pe"), False)
        SP = Queue(nc.sync, sem("sp"), False)
        v, sc, gp, te = nc.vector, nc.scalar, nc.gpsimd, nc.tensor

        ring = sb("ring", [P, RING, TILE])
        xr = sb("xr", [P, 2, D])
        hT = sb("hT", [P, 8, S])
        cols = sb("cols", [P, N_COLS])
        rowa = sb("rowa", [P, N_ROWA])
        K = sb("K", [P, N_K])
        gt = sb("gt", [P, 2, D])
        modT = sb("modT", [P, 32])
        small = sb("small", [P, 64])
        ones = sb("ones", [P, P])
        cact = sb("cact", [P, 16])
        arena = sb("arena", [P, ARENA])
        banks = [ctx.enter_context(nc.psum_tensor(f"ps{i}", [P, 512], F32)) for i in range(8)]
        drained = [()] * 8
        turn = {"main": 0, "misc": 0, "s5": 0}
        POOLS = {"main": (0, 1, 2, 3), "misc": (4, 5, 6, 7)}

        top = [0]

        def area(*shape):
            n = int(np.prod(shape))
            a = arena[:, top[0]:top[0] + n]
            top[0] += n
            assert top[0] <= ARENA, top
            if len(shape) == 2:
                a = a.rearrange("p (a b) -> p a b", a=shape[0])
            if len(shape) == 3:
                a = a.rearrange("p (a b c) -> p a b c", a=shape[0], b=shape[1])
            return a

        def bank(pool):
            t = turn[pool]
            turn[pool] = t + 1
            return POOLS[pool][t % len(POOLS[pool])]

        ident, su, iu, sl, neg = (K[:, o:o + 128] for o in (K_ID, K_SU, K_IU, K_SL, K_NEG))
        blk, hsel, rotm = K[:, K_BLK:K_BLK + 128], K[:, K_HSEL:K_HSEL + 2], K[:, K_ROT:K_ROT + 128]

        def load(name, dst, src, *tokens, q=SC):
            s = sem("l_" + name)
            return q.dma(lambda: q.eng.dma_start(dst, src), s, 16, *tokens)

        t_cols = load("cols", cols[:], A["cols"])
        t_x = load("x", xr[:], A["x"])
        t_K = load("K", K[:], A["K"])

        stream = ([("ada", i) for i in range(4)]
                  + [("wp", 0), ("ada", 4), ("wp", 1), ("ada", 5), ("wp", 2), ("ada", 6), ("wp", 3), ("ada", 7),
                     ("wp", 4), ("ada", 8), ("gates", 4), ("ada", 9)]
                  + [("gates", 5), ("gates", 2), ("gates", 3), ("o_ab", 0), ("o_c", 0)]
                  + [("gates", 6), ("gates", 7), ("gates", 0), ("gates", 1)]
                  + [("o_ab", 0), ("glu", 0), ("w_o", 0), ("w_o", 1)]
                  + [("w1", 0)]
                  + [x for i in range(8) for x in ([("w1", i + 1)] if i < 7 else []) + [("w2", i)]
                     + ([("ada", 10 + i // 2)] if i in (1, 3) else [])]
                  + [("qkv", i) for i in range(6)]
                  + [("ba", 0), ("bb", 0)] + [("g2", i) for i in range(4)]
                  + [("wout", i) for i in range(2)]
                  + [("pq", i) for i in range(4)] + [("keys", 0)])
        stream = [(n, i, 2048 if n in ("o_c", "keys") else TILE) for n, i in stream]
        ring_sems = [sem(f"ring{i}") for i in range(RING)]
        state = {"loaded": 0, "used": 0, "free": [()] * RING}

        def prefetch():
            n = state["loaded"]
            if n == len(stream):
                return
            state["loaded"] += 1
            name, i, w = stream[n]
            r = n % RING
            dst, src = ring[:, r, 0:w], A[name][i]
            SP.dma(lambda: nc.sync.dma_start(dst, src), ring_sems[r], 16 * (n // RING + 1), *state["free"][r])

        for _ in range(RING):
            prefetch()

        def tile(name, i=0):
            n = state["used"]
            assert stream[n][:2] == (name, i), (stream[n], name, i)
            state["used"] += 1
            return ring[:, n % RING, :], (ring_sems[n % RING], 16 * (n // RING + 1)), n % RING

        def done(r, *tokens):
            state["free"][r] = tokens
            prefetch()

        def mm(o, pairs, *tokens):
            n = len(pairs)
            for i, (l, r) in enumerate(pairs):
                t = PE.do(lambda l=l, r=r, i=i: te.matmul(o, l, r, start=(i == 0), stop=(i == n - 1)),
                          *(tokens if i == 0 else ()), count=(i == n - 1))
            return t

        def tr(o, i, *tokens):
            return PE.do(lambda: te.transpose(o, i, ident), *tokens)

        mrow = area(2, 512)
        junk = area(D)
        merged = area(2, D)
        xn = area(2, D)
        base2 = top[0]

        t_one = V.do(lambda: v.memset(ones[:], 1.0))
        t_sg = SC.do(lambda: sc.activation(cact[:, 8:16], cols[:, C_C:C_C + 8], ACT.Sigmoid), t_cols)
        t_c = V.do(lambda: v.tensor_tensor(cact[:, 0:8], cols[:, C_C:C_C + 8], cact[:, 8:16], ALU.mult), t_sg, t_cols)
        m_tok = {"gt": None, 0: None, 1: None, "n": 0}

        def ada_sum(i):
            w, tw, r = tile("ada", i)
            p = m_tok["n"] % 2
            m_tok["n"] += 1
            acc = mrow[:, p, :], junk[:, p * 512:(p + 1) * 512]
            ts = [None, None]
            for k in range(8):
                a_ = acc[k % 2]
                if k < 2:
                    t = V.do(lambda: v.tensor_scalar(a_, w[:, k * 512:(k + 1) * 512], cact[:, k:k + 1], None,
                                                     ALU.mult), tw, t_c, m_tok[p], loose=True)
                else:
                    t = V.do(lambda: v.scalar_tensor_tensor(a_, w[:, k * 512:(k + 1) * 512], cact[:, k:k + 1], a_,
                                                            ALU.mult, ALU.add), ts[k % 2], loose=True)
                ts[k % 2] = t
            done(r, t)
            return acc, t, p

        def mod_T(i, j0):
            acc, t, p = ada_sum(i)
            yield
            b = bank("misc")
            for q in range(4):
                t = mm(banks[b][:, q:q + 1], [(a_[:, q * 128:(q + 1) * 128], ones[:, 0:1]) for a_ in acc], t, t_one, *drained[b])
            m_tok[p] = t
            tc = V.do(lambda: v.tensor_tensor(modT[:, j0:j0 + 4], banks[b][:, 0:4],
                                              cols[:, C_ADAB + j0:C_ADAB + j0 + 4], ALU.add), t, t_cols)
            drained[b] = (tc,)
            tm2.append(tc)
            yield

        def mod_gt(i, which, half, pool="misc"):
            acc, t, p = ada_sum(i)
            yield
            b = bank(pool)
            t = mm(banks[b][:], [(ones[:], a_) for a_ in acc], t, t_one, *drained[b])
            m_tok[p] = t
            dst = gt[:, which, half * 512:(half + 1) * 512]
            m_tok["gt"] = V.do(lambda: v.tensor_tensor(dst, dst, banks[b][:], ALU.add), t, t_gtb)
            drained[b] = (m_tok["gt"],)
            yield

        def rms(dst, gain=None, *tokens):
            o = 0
            t1 = []
            for tt in range(2):
                t1.append(SC.do(lambda tt=tt: sc.activation(junk, xr[:, tt, :], ACT.Square,
                                                            accum_out=small[:, tt:tt + 1]), *tokens))
            V.do(lambda: v.tensor_scalar(small[:, 2:4], small[:, 0:2], 1.0 / D, 1e-6, ALU.mult, ALU.add), *t1)
            t2 = SC.do(lambda: sc.activation(small[:, 4:6], small[:, 2:4], ACT.Sqrt), V.last)
            V.do(lambda: v.reciprocal(small[:, 6:8], small[:, 4:6]), t2)
            r = []
            for tt in range(2):
                if gain is None:
                    r.append(V.do(lambda tt=tt: v.tensor_scalar(dst[:, tt, :], xr[:, tt, :], small[:, 6 + tt:7 + tt],
                                                                None, ALU.mult)))
                else:
                    r.append(V.do(lambda tt=tt: v.scalar_tensor_tensor(dst[:, tt, :], xr[:, tt, :],
                                                                       small[:, 6 + tt:7 + tt], gain, ALU.mult,
                                                                       ALU.mult)))
            return r

        def to_T(src, dst, toks, evac):
            ts = []
            for k in range(8):
                b = bank("misc")
                for tt in range(2):
                    t = tr(banks[b][:, tt * 128:(tt + 1) * 128], src[:, tt, k * 128:(k + 1) * 128], toks[tt], t_K,
                           *drained[b])
                te_ = evac(k, dst[:, k, :], banks[b][:, 0:S], t)
                drained[b] = (te_,)
                ts.append(te_)
            return ts

        def norm_T(gain, sh, scl, toks, *after):
            if scl is None:
                def ev(k, o, i, t):
                    return SC.do(lambda: sc.mul(o, i, cols[:, gain + k:gain + k + 1]), t, t_cols, *after)
            else:
                tg = V.do(lambda: v.scalar_tensor_tensor(small[:, 8:16], modT[:, scl:scl + 8], 1.0,
                                                         cols[:, gain:gain + 8], ALU.add, ALU.mult), t_cols, *after)

                def ev(k, o, i, t):
                    return SC.do(lambda: sc.activation(o, i, ACT.Identity, bias=modT[:, sh + k:sh + k + 1],
                                                       scale=small[:, 8 + k:9 + k]), t, tg, *after)
            return to_T(xn, hT, toks, ev)

        t_xn = rms(xn, None, t_x)
        tm2 = []
        for i in range(4):
            for _ in mod_T(i, 4 * i):
                pass
        tm, tm2 = tm2, []
        t_h = norm_T(C_GMIX, 0, 8, t_xn, *tm)
        hl = t_h[-1]
        t_rowa = load("rowa", rowa[:], A["rowa"].broadcast_to([P, N_ROWA]), hl)
        t_gtb = load("gtb", gt[:].rearrange("p a b -> p (a b)"), A["adab_g"].broadcast_to([P, 2 * D]), hl)

        def gemm_T(w, chunk, o, *tokens):
            return mm(o, [(w[:, k * 512 + chunk * 128:k * 512 + chunk * 128 + 128], hT[:, k, :]) for k in range(8)],
                      *tokens)

        def gemm_rows(w, tt, o, n0, n, *tokens):
            return mm(o, [(hT[:, k, tt * 128:(tt + 1) * 128], w[:, k * 512 + n0:k * 512 + n0 + n]) for k in range(8)],
                      *tokens)

        pc = area(6, S)
        uB = area(2, S)
        vB = area(2, S)
        pa = area(7, 257)
        uD = area(2, S)
        gb = area(2, 2, D)
        t_z = V.do(lambda: v.memset(pa[:, :, 0:1], 0.0))
        dest = {**{c: pa[:, c, 1:257] for c in range(7)}, 7: uD[:, 0, :], 8: uD[:, 1, :], 9: uB[:, 0, :],
                12: uB[:, 1, :], **{13 + i: pc[:, i, :] for i in range(6)}}
        tp = {}

        def p_tile(i):
            w, tw, r = tile("wp", i)
            chunks = [c for c in range(4 * i, min(4 * i + 4, 19)) if c != 11]

            def piece(c):
                b = bank("main")
                if c == 10:
                    for tt in range(2):
                        t = gemm_rows(w, tt, banks[b][:, tt * S:(tt + 1) * S], 256, 256, tw, hl, *drained[b])
                    te_ = SC.do(lambda: sc.activation(vB.rearrange("p a b -> p (a b)"), banks[b][:],
                                                      ACT.Gelu_apprx_tanh), t)
                else:
                    t = gemm_T(w, c - 4 * i, banks[b][:, 0:S], tw, hl, *drained[b])
                    if c in (9, 12):
                        te_ = SC.do(lambda: sc.activation(dest[c], banks[b][:, 0:S], ACT.Gelu_apprx_tanh), t)
                    elif c % 2 or c > 6:
                        te_ = SC.do(lambda: sc.copy(dest[c], banks[b][:, 0:S]), t)
                    else:
                        te_ = V.do(lambda: v.tensor_copy(dest[c], banks[b][:, 0:S]), t)
                tp[c] = te_
                drained[b] = (te_,)
                if c == chunks[-1]:
                    done(r, t)
            return [lambda c=c: piece(c) for c in chunks]

        gtok = {}

        def gate_tile(g, slot, *tokens):
            w, tw, r = tile("gates", g)

            open_ = {}

            def piece(tt, part):
                if part == 0:
                    open_[tt] = bank("main")
                b = open_[tt]
                for k in range(4 * part, 4 * part + 4):
                    t = PE.do(lambda: te.matmul(banks[b][:], hT[:, k, tt * 128:(tt + 1) * 128],
                                                w[:, k * 512:(k + 1) * 512], start=(k == 0), stop=(k == 7)),
                              *((tw, hl) + tuple(drained[b]) if k == 0 else ()), count=(k == 7))
                if part == 0:
                    return
                o = gb[:, slot, tt, (g % 2) * 512:(g % 2) * 512 + 512]
                te_ = SC.do(lambda: sc.activation(o, banks[b][:], ACT.Sigmoid), t, *tokens)
                drained[b] = (te_,)
                gtok.setdefault(g, []).append(te_)
                if tt:
                    done(r, t)
            return [lambda tt=tt, part=part: piece(tt, part) for tt in range(2) for part in range(2)]

        mt = {}

        def merge(br, slot, zT, toff, w, w0, tw, tz, first):
            for tt in range(2):
                for hf in range(2):
                    b = bank("main")
                    t = mm(banks[b][:], [(zT[:, c, toff + tt * 128:toff + (tt + 1) * 128],
                                          w[:, w0 + c * D + hf * 512:w0 + c * D + hf * 512 + 512]) for c in range(2)],
                           tw, *tz, *drained[b])
                    gsl = gb[:, slot, tt, hf * 512:(hf + 1) * 512]
                    m = merged[:, tt, hf * 512:(hf + 1) * 512]
                    tg = gtok[2 * br + hf][tt]
                    if first:
                        te_ = V.do(lambda b=b, g=gsl, m=m: v.tensor_tensor(m, g, banks[b][:], ALU.mult), t, tg)
                        drained[b] = (te_,)
                    else:
                        te_ = V.do(lambda b=b, g=gsl: v.tensor_tensor(g, g, banks[b][:], ALU.mult), t, tg)
                        drained[b] = (te_,)
                        te_ = G.do(lambda g=gsl, m=m: gp.tensor_tensor(m, m, g, ALU.add), te_, mt[(tt, hf)])
                    mt[(tt, hf)] = te_
            return t

        bc4 = lambda m: m.unsqueeze(1).broadcast_to([P, 4, P])
        f4 = lambda a: a.rearrange("p a b -> p (a b)")
        mark = top[0]
        zc = area(2, 258)
        yc = area(2, S)
        vln = area(2, S)
        zB = area(2, S)
        bnb = area(6)
        wsT = area(4, 128)
        bsT = area(2, 128)
        bc_end = top[0]
        t_ws = load("ws", wsT, A["ws"], hl)
        t_bs = load("bs", bsT, A["bs"], hl)
        tws = G.do(lambda: gp.tensor_tensor(wsT, wsT, bc4(iu), ALU.mult), t_ws, t_K)
        tbc = {}

        def branch_c():
            V.do(lambda: v.memset(zc[:, :, 0:2], 0.0))
            V.do(lambda: v.tensor_tensor(zc[:, :, 2:258], pc[:, 2:4, :], pc[:, 4:6, :], ALU.mult),
                 *[tp[c] for c in range(13, 19)])
            yield
            for c in range(2):
                for j in range(3):
                    cw = cols[:, C_CONV + 2 * j + c:C_CONV + 2 * j + c + 1]
                    if j == 0:
                        V.do(lambda: v.tensor_scalar(yc[:, c, :], zc[:, c, 0:S], cw, None, ALU.mult))
                    else:
                        V.do(lambda: v.scalar_tensor_tensor(yc[:, c, :], zc[:, c, j:j + S], cw, yc[:, c, :],
                                                            ALU.mult, ALU.add))
            tbc["c"] = V.do(lambda: v.tensor_tensor(yc, yc, pc[:, 0:2, :], ALU.mult))
            yield

        def branch_b():
            V.wait(tp[10])
            for tt in range(2):
                V.do(lambda: v.bn_stats(bnb, vB[:, tt, :]))
                V.do(lambda: v.bn_aggr(small[:, 20 + 2 * tt:22 + 2 * tt], bnb))
            mv = small[:, 20:24].rearrange("p (a b) -> p a b", b=2)
            V.do(lambda: v.tensor_scalar(small[:, 24:26].unsqueeze(2), mv[:, :, 1:2], 1e-5, None, ALU.add))
            ts_ = SC.do(lambda: sc.activation(small[:, 26:28], small[:, 24:26], ACT.Sqrt), V.last)
            yield
            V.do(lambda: v.reciprocal(small[:, 28:30], small[:, 26:28]), ts_)
            for tt in range(2):
                V.do(lambda: v.tensor_scalar(vln[:, tt, :], vB[:, tt, :], small[:, 20 + 2 * tt:21 + 2 * tt],
                                             small[:, 28 + tt:29 + tt], ALU.subtract, ALU.mult))
            V.do(lambda: v.tensor_tensor(vln, vln, rowa[:, R_SGW:R_SGW + 256].unsqueeze(1).broadcast_to([P, 2, S]),
                                         ALU.mult), t_rowa)
            t_vln = V.do(lambda: v.tensor_tensor(vln, vln, rowa[:, R_SGB:R_SGB + 256].unsqueeze(1)
                                                 .broadcast_to([P, 2, S]), ALU.add))
            yield
            bs_ = []
            for pr in range(2):
                b = bank("misc")
                for n in range(2):
                    t = mm(banks[b][:, n * S:(n + 1) * S],
                           [(vln[:, n, pr * 128:(pr + 1) * 128], wsT[:, 2 * pr:2 * pr + 2, :])], t_vln, tws,
                           *drained[b])
                bs_.append((b, t))
            for pr, (b, t) in enumerate(bs_):
                for g in range(2):
                    pv = banks[b][64 * g:64 * g + 64, :].rearrange("p (n g t) -> p n g t", n=2, g=2)[:, :, g, :]
                    o = zB[64 * g:64 * g + 64, pr, :].rearrange("p (n t) -> p n t", n=2)
                    bsv = bsT[64 * g:64 * g + 64, pr, :].unsqueeze(1).broadcast_to([64, 2, P])
                    te_ = V.do(lambda: v.tensor_tensor(o, pv, bsv, ALU.add), t, t_bs)
                drained[b] = (te_,)
            tbc["b"] = V.do(lambda: v.tensor_tensor(zB, zB, uB, ALU.mult), tp[9], tp[12])
            yield

        sp = area(14, 8)
        pw = area(8, 3, 8)
        wB = area(2, 2, 128)
        wC = area(2, 2, 128)
        xa = area(2, 2, S)
        xb = area(2, 2, S)
        yD = area(2, S)
        tD = {}
        semB, semC = sem("s5b"), sem("s5c")
        mark2 = top[0]

        def s5():
            lre, lim, dt_, mag, abr, abi, qr, qi = (sp[:, i, :] for i in range(8))
            s1, s2, s3, s4, s5_, nqi = (sp[:, i, :] for i in range(8, 14))
            V.do(lambda: v.tensor_scalar(lre, cols[:, C_ARE:C_ARE + 8], -1e-4, None, ALU.min))
            V.do(lambda: v.tensor_copy(lim, cols[:, C_AIM:C_AIM + 8]))
            t = SC.do(lambda: sc.activation(dt_, cols[:, C_DT:C_DT + 8], ACT.Exp))
            V.do(lambda: v.tensor_tensor(s1, lre, dt_, ALU.mult), t)
            t = SC.do(lambda: sc.activation(mag, s1, ACT.Exp), V.last)
            yield
            V.do(lambda: v.tensor_tensor(s1, lim, dt_, ALU.mult), t)
            BIG = 12582912.0
            V.do(lambda: v.tensor_scalar(s2, s1, float(np.float32(1 / (2 * np.pi))), BIG, ALU.mult, ALU.add))
            V.do(lambda: v.tensor_scalar(s2, s2, -BIG, None, ALU.add))
            for cst in (6.28125, 0.0019350051879882812, 3.0199159819567e-07):
                V.do(lambda: v.scalar_tensor_tensor(s1, s2, -cst, s1, ALU.mult, ALU.add))
            V.do(lambda: v.tensor_scalar(s1, s1, 3.1415925, -3.1415925, ALU.min, ALU.max))
            V.do(lambda: v.tensor_scalar(s3, s1, 0.5, None, ALU.mult))
            SC.do(lambda: sc.activation(s4, s1, ACT.Sin), V.last)
            t = SC.do(lambda: sc.activation(s5_, s3, ACT.Sin))
            yield
            V.do(lambda: v.tensor_tensor(s5_, s5_, s5_, ALU.mult), t)
            V.do(lambda: v.tensor_scalar(s5_, s5_, -2.0, 1.0, ALU.mult, ALU.add))
            V.do(lambda: v.tensor_tensor(abr, mag, s5_, ALU.mult))
            V.do(lambda: v.tensor_tensor(abi, mag, s4, ALU.mult))
            V.do(lambda: v.tensor_tensor(s1, lre, lre, ALU.mult))
            V.do(lambda: v.tensor_tensor(s2, lim, lim, ALU.mult))
            V.do(lambda: v.tensor_tensor(s1, s1, s2, ALU.add))
            V.do(lambda: v.reciprocal(s1, s1))
            V.do(lambda: v.tensor_scalar(s2, abr, -1.0, None, ALU.add))
            V.do(lambda: v.tensor_tensor(s3, s2, lre, ALU.mult))
            V.do(lambda: v.tensor_tensor(s4, abi, lim, ALU.mult))
            V.do(lambda: v.tensor_tensor(s3, s3, s4, ALU.add))
            V.do(lambda: v.tensor_tensor(qr, s3, s1, ALU.mult))
            V.do(lambda: v.tensor_tensor(s3, abi, lre, ALU.mult))
            V.do(lambda: v.tensor_tensor(s4, s2, lim, ALU.mult))
            V.do(lambda: v.tensor_tensor(s3, s3, s4, ALU.subtract))
            V.do(lambda: v.tensor_tensor(qi, s3, s1, ALU.mult))
            V.do(lambda: v.tensor_scalar(nqi, qi, -1.0, None, ALU.mult))

            def loadw(dst, name, n, sm_, *tokens):
                for i in range(2):
                    src = A[name][2 * (n // 2) + i][:, 2 * (n % 2):2 * (n % 2) + 2, :]
                    t = SP.dma(lambda: nc.sync.dma_start(dst[:, i, :, :], src), sm_, 32 * n + 16 * i + 16, *tokens)
                return t

            tB, tC = loadw(wB, "s5b", 0, semB), loadw(wC, "s5c", 0, semC)
            t_y = tcp_ = None
            V.do(lambda: v.tensor_copy(pw[:, 0, 0, :], abr))
            V.do(lambda: v.tensor_copy(pw[:, 0, 1, :], abi))
            V.do(lambda: v.tensor_scalar(pw[:, 0, 2, :], abi, -1.0, None, ALU.mult))
            for lv in range(1, 8):
                p0, p1 = pw[:, lv - 1, 0, :], pw[:, lv - 1, 1, :]
                V.do(lambda: v.tensor_tensor(s1, p0, p0, ALU.mult))
                V.do(lambda: v.tensor_tensor(s2, p1, p1, ALU.mult), loose=True)
                V.do(lambda: v.tensor_tensor(s3, p0, p1, ALU.mult), loose=True)
                V.do(lambda: v.tensor_tensor(pw[:, lv, 0, :], s1, s2, ALU.subtract))
                V.do(lambda: v.tensor_scalar(pw[:, lv, 1, :], s3, 2.0, None, ALU.mult), loose=True)
                t_pw = V.do(lambda: v.tensor_scalar(pw[:, lv, 2, :], s3, -2.0, None, ALU.mult), loose=True)
            V.wait(t_pw)
            for n in range(4):
                hf = n // 2
                bq = []
                for q in range(2):
                    b = bank("s5")
                    for i in range(2):
                        t = mm(banks[b][:, i * S:(i + 1) * S], [(wB[:, i, q, :], uD[:, hf, :])], tB, tp[7], tp[8],
                               *drained[b])
                    bq.append((b, t))
                if n < 3:
                    tB = loadw(wB, "s5b", n + 1, semB, t)
                yield
                for q, (b, t) in enumerate(bq):
                    j = 2 * n + q
                    for i in range(2):
                        s_a = (qr if i == 0 else qi)[:, j:j + 1]
                        s_b = (nqi if i == 0 else qr)[:, j:j + 1]
                        te1 = SC.do(lambda: sc.mul(xa[:, i, q, :], banks[b][:, 0:S], s_a), t, t_y, V.last)
                        te_ = V.do(lambda: v.scalar_tensor_tensor(xa[:, i, q, :], banks[b][:, S:2 * S], s_b,
                                                                  xa[:, i, q, :], ALU.mult, ALU.add), te1)
                    drained[b] = (te_, te1)
                yield
                src, dst = xa, xb
                tv_ = V.last
                for lv in range(8):
                    s_ = 1 << lv
                    m = S - s_
                    pr_, pi_, npi = (pw[:, lv, j, 2 * n:2 * n + 2] for j in range(3))
                    tc_ = SC.do(lambda: sc.copy(dst[:, :, :, 0:s_], src[:, :, :, 0:s_]), tv_)
                    first = {}
                    for i in range(2):
                        for q in range(2):
                            first[(i, q)] = V.do(lambda: v.scalar_tensor_tensor(
                                dst[:, i, q, s_:S], src[:, i, q, 0:m], pr_[:, q:q + 1], src[:, i, q, s_:S], ALU.mult,
                                ALU.add), tv_, tcp_, loose=True)
                    for i in range(2):
                        for q in range(2):
                            b_ = npi if i == 0 else pi_
                            tv_ = V.do(lambda: v.scalar_tensor_tensor(
                                dst[:, i, q, s_:S], src[:, 1 - i, q, 0:m], b_[:, q:q + 1], dst[:, i, q, s_:S],
                                ALU.mult, ALU.add), first[(i, q)], loose=True)
                    tcp_ = tc_
                    src, dst = dst, src
                    yield
                b = bank("s5")
                for i in range(2):
                    t = mm(banks[b][:, i * S:(i + 1) * S], [(wC[:, i, q, :], xa[:, i, q, :]) for q in range(2)], tC,
                           tv_, tcp_, *drained[b])
                if n < 3:
                    tC = loadw(wC, "s5c", n + 1, semC, t)
                t_y = t
                yield
                if n % 2 == 0:
                    V.do(lambda: v.scalar_tensor_tensor(yD[:, hf, :], uD[:, hf, :],
                                                        cols[:, C_SD + hf:C_SD + hf + 1], banks[b][:, 0:S],
                                                        ALU.mult, ALU.add), t)
                else:
                    V.do(lambda: v.tensor_tensor(yD[:, hf, :], yD[:, hf, :], banks[b][:, 0:S], ALU.add), t)
                te_ = V.do(lambda: v.tensor_tensor(yD[:, hf, :], yD[:, hf, :], banks[b][:, S:2 * S], ALU.subtract))
                drained[b] = (te_,)
            tD["y"] = SC.do(lambda: sc.activation(f4(yD), f4(yD), ACT.Gelu_apprx_tanh), te_)
            yield

        L = area(2, S)
        keep, top[0] = top[0], base2
        MT, Mrb, Mrk, MoB, Mak = (area(4, 128) for _ in range(5))
        top[0] = keep
        Dm, DT, MoA = (area(4, 128) for _ in range(3))
        bn8 = area(8, 6)
        ps = area(7, S)
        lw = area(2, S)
        Wp = area(2, S)
        aa = area(2, S)
        gr = area(2, S)
        kk = area(2, S)
        tmp = area(2, S)
        vr = area(2, S)
        am = area(2, 2, S)
        oo = tmp
        Xs = f4(lw).rearrange("p (a b) -> p a b", a=4)
        U = Wp[:, 0, :].rearrange("p (a b) -> p a b", a=4)
        St = Wp[:, 1, :].rearrange("p (a b) -> p a b", a=2)
        rm = xn.rearrange("p a b -> p (a b)")[:, 0:1024].rearrange("p (a b c) -> p a b c", a=2, b=2)
        W6 = xn.rearrange("p a b -> p (a b)")[:, 1024:1792]
        t_w6 = load("w6", W6, A["w6"], hl)
        zA = kk
        tA_ = {}

        def rwkv():
            a6 = ps[:, 6, :]
            V.do(lambda: v.tensor_tensor(ps, pa[:, :, 0:S], pa[:, :, 1:257], ALU.subtract),
                 *[tp[c] for c in range(7)])
            t0 = V.last
            for c in range(7):
                V.do(lambda: v.scalar_tensor_tensor(ps[:, c, :], ps[:, c, :], cols[:, C_MU + c:C_MU + c + 1],
                                                    pa[:, c, 1:257], ALU.mult, ALU.add), t0, loose=True)
            t_ps = V.last
            V.wait(t_ps)
            rT, kT, vT = ps[:, 0:2, :], ps[:, 2:4, :], ps[:, 4:6, :]
            SC.do(lambda: sc.activation(a6[0:32, :], a6[0:32, :], ACT.Tanh), t_ps)
            t_a6 = SC.do(lambda: sc.activation(a6[64:128, :], a6[64:128, :], ACT.Sigmoid))
            yield
            b = bank("misc")
            for tt in range(2):
                for c in range(2):
                    t = tr(banks[b][:, tt * S + c * 128:tt * S + (c + 1) * 128], vT[:, c, tt * 128:(tt + 1) * 128],
                           t_ps, *drained[b])
            t_vr = SC.do(lambda: sc.copy(f4(vr), banks[b][:]), t)
            drained[b] = (t_vr,)
            b1, b2, b3 = bank("misc"), bank("misc"), bank("misc")
            for c in range(2):
                t1 = mm(banks[b1][:, c * S:(c + 1) * S], [(W6[:, c * 128:(c + 1) * 128], a6)], t_a6, t_w6,
                        *drained[b1])
            for c in range(2):
                t2 = mm(banks[b2][:, c * S:(c + 1) * S], [(W6[:, 256 + c * 128:256 + (c + 1) * 128], a6)],
                        *drained[b2])
            for tt in range(2):
                t3 = mm(banks[b3][:, tt * S:(tt + 1) * S], [(a6[:, tt * 128:(tt + 1) * 128], W6[:, 512:768])],
                        *drained[b3])
            for c in range(2):
                t_lw = SC.do(lambda: sc.activation(lw[:, c, :], banks[b1][:, c * S:(c + 1) * S], ACT.Sigmoid,
                                                   bias=cols[:, C_W0 + c:C_W0 + c + 1]), t1)
            drained[b1] = (t_lw,)
            for c in range(2):
                t_aa = SC.do(lambda: sc.activation(aa[:, c, :], banks[b2][:, c * S:(c + 1) * S], ACT.Sigmoid,
                                                   bias=cols[:, C_A0 + c:C_A0 + c + 1]), t2)
            drained[b2] = (t_aa,)
            t_gr = SC.do(lambda: sc.copy(f4(gr), banks[b3][:]), t3)
            drained[b3] = (t_gr,)
            for c in range(2):
                V.do(lambda: v.tensor_scalar(kk[:, c, :], kT[:, c, :], cols[:, C_KK + c:C_KK + c + 1], None,
                                             ALU.mult))
            t = V.do(lambda: v.tensor_tensor(tmp, kk, kk, ALU.mult))
            yield
            b = bank("misc")
            t = mm(banks[b][:], [(blk, tmp)], t, *drained[b])
            tf = f4(tmp)
            te_ = SC.do(lambda: sc.activation(tf, banks[b][:], ACT.Sqrt), t)
            drained[b] = (te_,)
            V.do(lambda: v.tensor_scalar(lw, lw, -float(np.exp(-0.5)), None, ALU.mult), t_lw)
            t0 = V.last
            for c in range(2):
                for tt in range(2):
                    sl_ = slice(tt * 128, (tt + 1) * 128)
                    V.do(lambda: v.tensor_tensor_scan(L[:, c, sl_], ones[:], lw[:, c, sl_], 0.0, ALU.mult, ALU.add),
                         t0, loose=True)
            em = small[:, 40:48]
            L4 = L.rearrange("p c (a t) -> p (c a) t", t=128)
            V.do(lambda: v.tensor_copy(em[:, 0:4].unsqueeze(2), L4[:, :, 63:64]))
            V.do(lambda: v.tensor_tensor(em[:, 4:8].unsqueeze(2), L4[:, :, 127:128], L4[:, :, 63:64], ALU.subtract))
            V.do(lambda: v.tensor_tensor(L4, L4, em[:, 0:4].unsqueeze(2).broadcast_to([P, 4, P]), ALU.subtract))
            V.do(lambda: v.tensor_tensor(Wp, L, lw, ALU.subtract))
            t_L = V.last
            SC.do(lambda: sc.activation(f4(Wp), f4(Wp), ACT.Exp), t_L)
            SC.do(lambda: sc.activation(f4(lw), f4(L), ACT.Exp))
            SC.do(lambda: sc.activation(f4(L), f4(L), ACT.Exp, scale=-1.0))
            t_W = SC.do(lambda: sc.activation(em, em, ACT.Exp))
            V.do(lambda: v.tensor_scalar(tf, tf, 1e-12, None, ALU.max), te_)
            V.do(lambda: v.reciprocal(tf, tf))
            V.do(lambda: v.tensor_tensor(kk, kk, tmp, ALU.mult))
            yield
            for c in range(2):
                V.do(lambda: v.tensor_scalar(tmp[:, c, :], aa[:, c, :], -1.0, cols[:, C_KA + c:C_KA + c + 1],
                                             ALU.add, ALU.mult), t_aa)
            V.do(lambda: v.scalar_tensor_tensor(kT, tmp, 1.0, kT, ALU.add, ALU.mult))
            for c in range(2):
                V.do(lambda: v.scalar_tensor_tensor(tmp[:, c, :], rT[:, c, :], cols[:, C_RK + c:C_RK + c + 1],
                                                    kT[:, c, :], ALU.mult, ALU.mult))
            tb_ = V.last
            bon = small[:, 32:40]
            b = bank("misc")
            for tt in range(2):
                for c in range(2):
                    t = mm(banks[b][:, 4 * tt + 2 * c:4 * tt + 2 * c + 2],
                           [(tmp[:, c, tt * 128:(tt + 1) * 128], hsel)], tb_, *drained[b])
            t_bon = SC.do(lambda: sc.copy(bon, banks[b][:, 0:8]), t)
            drained[b] = (t_bon,)
            pb4 = pa.rearrange("p a b -> p (a b)")
            at_, bt_ = (pb4[:, i * 512:(i + 1) * 512].rearrange("p (a b) -> p a b", a=2) for i in range(2))
            kt_ = pb4[:, 1024:1536].rearrange("p (a b) -> p a b", a=2)
            V.do(lambda: v.tensor_tensor(bt_, kk, aa, ALU.mult), t_W)
            V.do(lambda: v.tensor_tensor(bt_, bt_, L, ALU.mult))
            V.do(lambda: v.scalar_tensor_tensor(at_, kk, -1.0, Wp, ALU.mult, ALU.mult), loose=True)
            V.do(lambda: v.tensor_tensor(kt_, kT, L, ALU.mult), loose=True)
            V.do(lambda: v.tensor_tensor(rT, rT, lw, ALU.mult), loose=True)
            t_abkr = V.last
            for e in range(2):
                hs = K[:, K_HSEL + e:K_HSEL + e + 1]
                SC.do(lambda: sc.mul(am[:, e, :, :], at_, hs), t_abkr)
            for e in range(2):
                hs = K[:, K_HSEL + e:K_HSEL + e + 1]
                t_arm = SC.do(lambda: sc.mul(rm[:, e, :, :], rT, hs), t3)
            yield

            lev = lambda i: K[:, K_LEV + i * 128:K_LEV + (i + 1) * 128].unsqueeze(1).broadcast_to([P, 4, P])

            def head_mats(tt, lhs, rhs, dst, mask, *after):
                b = bank("misc")
                sl_ = slice(tt * 128, (tt + 1) * 128)
                for h in range(4):
                    t = mm(banks[b][:, h * 128:(h + 1) * 128], [(lhs[:, h // 2, sl_], rhs[:, h % 2, h // 2, sl_])],
                           t_arm, t_abkr, *drained[b])
                te_ = V.do(lambda: v.tensor_tensor(f4(dst), banks[b][:], bc4(mask), ALU.mult), t, *after,
                           loose=True)
                drained[b] = (te_,)
                return te_

            t_mats = t_gdt = t_gmo = None
            for tt in range(2):
                t_MT = head_mats(tt, bt_, am, MT, su, t_mats, t_gmo)
                Mo = (MoA, MoB)
                tM0 = G.do(lambda: gp.tensor_tensor(MoA, MT, lev(0), ALU.mult), t_MT, t_mats)
                t_DT = G.do(lambda: gp.tensor_tensor(DT, MoA, bc4(ident), ALU.add))
                t_Mo = {1: G.do(lambda: gp.tensor_tensor(MoB, MT, lev(1), ALU.mult))}
                t_Mak = head_mats(tt, kt_, am, Mak, su, t_mats)
                t_Mrb = head_mats(tt, bt_, rm, Mrb, iu, t_mats)
                t_Mrk = head_mats(tt, kt_, rm, Mrk, iu, t_mats)
                yield
                b = bank("misc")
                for h in range(4):
                    t = tr(banks[b][:, h * 128:(h + 1) * 128], DT[:, h, :], t_DT, *drained[b])
                t_D = SC.do(lambda: sc.copy(f4(Dm), banks[b][:]), t)
                drained[b] = (t_D,)
                yield
                reads = {}
                for k in range(1, 7):
                    if k < 6:
                        t_Mo[k + 1] = G.do(lambda: gp.tensor_tensor(Mo[(k + 1) % 2], MT, lev(k + 1), ALU.mult),
                                           reads.get(k - 1))
                        t_gmo = t_Mo[k + 1]
                    bx = bank("misc")
                    for h in range(4):
                        t = mm(banks[bx][:, h * 128:(h + 1) * 128], [(Mo[k % 2][:, h, :], Dm[:, h, :])], t_Mo[k],
                               t_D, *drained[bx])
                    reads[k] = t
                    t_X = SC.do(lambda: sc.copy(f4(Xs), banks[bx][:]), t)
                    drained[bx] = (t_X,)
                    yield
                    by = bank("misc")
                    if k < 6:
                        for h in range(4):
                            t = mm(banks[by][:, h * 128:(h + 1) * 128], [(DT[:, h, :], Xs[:, h, :])], t_X, t_DT,
                                   *drained[by])
                        t_D = V.do(lambda: v.tensor_tensor(f4(Dm), f4(Dm), banks[by][:], ALU.add), t, t_D,
                                   loose=True)
                        drained[by] = (t_D,)
                        bz = bank("misc")
                    else:
                        bz = by
                    for h in range(4):
                        t = mm(banks[bz][:, h * 128:(h + 1) * 128], [(Xs[:, h, :], DT[:, h, :])], t_X, t_DT,
                               *drained[bz])
                    t_DT = V.do(lambda: v.tensor_tensor(f4(DT), f4(DT), banks[bz][:], ALU.add), t, t_DT, loose=True)
                    drained[bz] = (t_DT,)
                    yield
                sl_ = slice(tt * 128, (tt + 1) * 128)
                b = bank("misc")
                for h in range(4):
                    c, e = h // 2, h % 2
                    pairs = [(Mak[:, h, :], vr[:, tt, h * 64:h * 64 + 64])]
                    if tt:
                        pairs.append((am[:, e, c, sl_], St[:, c, e * 64:e * 64 + 64]))
                    t = mm(banks[b][:, h * 64:h * 64 + 64], pairs, t_Mak, t_vr, *([tS] if tt else []), *drained[b])
                Xv = f4(Xs)[:, 0:256]
                t_X = SC.do(lambda: sc.copy(Xv, banks[b][:, 0:256]), t)
                drained[b] = (t_X,)
                yield
                b = bank("misc")
                for h in range(4):
                    t = mm(banks[b][:, h * 64:h * 64 + 64], [(DT[:, h, :], Xv[:, h * 64:h * 64 + 64])], t_X, t_DT,
                           *drained[b])
                t_U = SC.do(lambda: sc.copy(f4(U), banks[b][:, 0:256]), t)
                drained[b] = (t_U,)
                if tt == 0:
                    b = bank("misc")
                    for i, src in enumerate((bt_, kt_)):
                        for c in range(2):
                            t = tr(banks[b][:, (i * 2 + c) * 128:(i * 2 + c + 1) * 128], src[:, c, 0:128], t_abkr,
                                   *drained[b])
                    bkr = f4(MoA)
                    t_r = SC.do(lambda: sc.copy(bkr, banks[b][:]), t)
                    drained[b] = (t_r,)
                yield
                b = bank("misc")
                for h in range(4):
                    c, e = h // 2, h % 2
                    pairs = [(Mrb[:, h, :], U[:, h, :]), (Mrk[:, h, :], vr[:, tt, h * 64:h * 64 + 64])]
                    if tt:
                        pairs.append((rm[:, e, c, sl_], St[:, c, e * 64:e * 64 + 64]))
                    t = mm(banks[b][:, h * 64:h * 64 + 64], pairs, t_U, t_Mrb, t_Mrk, *drained[b])
                t_o = SC.do(lambda: sc.copy(oo[:, tt, :], banks[b][:, 0:256]), t)
                drained[b] = (t_o,)
                if tt == 0:
                    b = bank("misc")
                    for c in range(2):
                        t = mm(banks[b][:, c * 128:(c + 1) * 128],
                               [(bkr[:, c * 128:(c + 1) * 128], f4(U)[:, c * 128:(c + 1) * 128]),
                                (bkr[:, 256 + c * 128:256 + (c + 1) * 128], vr[:, 0, c * 128:(c + 1) * 128])],
                               t_r, t_U, t_vr, *drained[b])
                    for c in range(2):
                        tS = V.do(lambda: v.tensor_scalar(St[:, c, :], banks[b][:, c * 128:(c + 1) * 128],
                                                          em[:, 4 + 2 * c:5 + 2 * c], em[:, 2 * c + 1:2 * c + 2],
                                                          ALU.mult, ALU.mult), t, t_W, loose=True)
                    drained[b] = (tS,)
                t_mats = t
                yield
            V.wait(t_o, tS)
            mvh = small[:, 48:64].rearrange("p (a b) -> p a b", b=2)
            for i in range(8):
                src = oo[:, i // 4, (i % 4) * 64:(i % 4 + 1) * 64]
                V.do(lambda: v.bn_stats(bn8[:, i, :], src), loose=True)
            for i in range(8):
                V.do(lambda: v.bn_aggr(mvh[:, i, :], bn8[:, i, :]), *([V.last] if i == 0 else []), loose=True)
            rs8 = small[:, 8:16]
            V.do(lambda: v.tensor_scalar(rs8.unsqueeze(2), mvh[:, :, 1:2], 64e-5, None, ALU.add))
            ts_ = SC.do(lambda: sc.activation(rs8, rs8, ACT.Sqrt), V.last)
            yield
            V.do(lambda: v.reciprocal(rs8, rs8), ts_)
            o8 = oo.rearrange("p a (h i) -> p (a h) i", h=4)
            V.do(lambda: v.tensor_tensor(o8, o8, mvh[:, :, 0:1].broadcast_to([P, 8, 64]), ALU.subtract))
            V.do(lambda: v.tensor_tensor(o8, o8, rs8.unsqueeze(2).broadcast_to([P, 8, 64]), ALU.mult))
            V.do(lambda: v.tensor_tensor(oo, oo, rowa[:, R_LNXW:R_LNXW + 256].unsqueeze(1).broadcast_to([P, 2, S]),
                                         ALU.mult), t_rowa)
            V.do(lambda: v.tensor_tensor(oo, oo, rowa[:, R_LNXB:R_LNXB + 256].unsqueeze(1).broadcast_to([P, 2, S]),
                                         ALU.add))
            yield
            vr8 = vr.rearrange("p a (h i) -> p (a h) i", h=4)
            V.do(lambda: v.tensor_tensor(vr8, vr8, bon.unsqueeze(2).broadcast_to([P, 8, 64]), ALU.mult), t_bon,
                 t_mats)
            V.do(lambda: v.tensor_tensor(oo, oo, vr, ALU.add))
            t = V.do(lambda: v.tensor_tensor(oo, oo, gr, ALU.mult), t_gr)
            yield
            b = bank("misc")
            for c in range(2):
                for tt in range(2):
                    t2 = tr(banks[b][:, c * S + tt * 128:c * S + (tt + 1) * 128], oo[:, tt, c * 128:(c + 1) * 128],
                            t, *drained[b])
            tA_["z"] = SC.do(lambda: sc.copy(f4(zA), banks[b][:]), t2)
            drained[b] = (tA_["z"],)
            yield

        POOLS.update({"main": (0, 1, 2), "misc": (4, 5, 6), "s5": (3, 7)})
        gen_a, gen_d, gen_b, gen_c = rwkv(), s5(), branch_b(), branch_c()

        def step(*gens):
            for g in gens:
                next(g, None)

        def weave(pieces, *gens):
            for f in pieces:
                f()
                step(*gens)

        def then(mod, pieces, *gens):
            next(mod)
            weave(pieces(), *gens)
            next(mod)

        weave(p_tile(0))
        then(mod_gt(4, 0, 0), lambda: p_tile(1))
        then(mod_gt(5, 0, 1), lambda: p_tile(2), gen_a, gen_d)
        then(mod_T(6, 16), lambda: p_tile(3), gen_d)
        then(mod_T(7, 20), lambda: p_tile(4), gen_b, gen_d)
        mod = mod_T(8, 24)
        next(mod)
        gt4 = gate_tile(4, 0)
        weave(gt4[0:2], gen_b, gen_c, gen_d)
        for g_ in (gen_b, gen_c):
            for _ in g_:
                pass
        weave(gt4[2:], gen_a, gen_d)
        next(mod)
        then(mod_T(9, 28), lambda: gate_tile(5, 0), gen_a, gen_d)
        weave(gate_tile(2, 1) + gate_tile(3, 1), gen_a, gen_d)
        w, tw, r = tile("o_ab")
        w2_, tw2, r2 = tile("o_c")
        tC_ = merge(2, 0, yc, 0, w2_, 0, tw2, (tbc["c"],), True)
        step(gen_a, gen_d)
        tB_ = merge(1, 1, zB, 0, w, 2048, tw, (tbc["b"],), False)
        done(r, tB_)
        done(r2, tC_)
        gb_free = tuple(mt[k] for k in mt)
        step(gen_a, gen_d)
        weave(gate_tile(6, 0, *gb_free) + gate_tile(7, 0) + gate_tile(0, 1, *gb_free), gen_a, gen_d)
        weave(gate_tile(1, 1), gen_a, gen_d)
        for _ in gen_a:
            step(gen_d)
        w, tw, r = tile("o_ab")
        tA = merge(0, 1, zA, 0, w, 0, tw, (tA_["z"],), False)
        done(r, tA)
        for _ in gen_d:
            pass
        POOLS.update({"main": (0, 1, 2, 3), "misc": (4, 5, 6, 7)})

        def glu():
            w, tw, r = tile("glu")
            sgm = junk
            tsg = None
            for tt in range(2):
                for hf in range(2):
                    for part in (1, 0):
                        b = bank("main")
                        t = mm(banks[b][:], [(yD[:, c, tt * 128:(tt + 1) * 128],
                                              w[:, c * 2048 + part * D + hf * 512:
                                                c * 2048 + part * D + hf * 512 + 512]) for c in range(2)],
                               tw, tD["y"], *drained[b])
                        if part == 1:
                            sg_ = sgm[:, 512 * hf:512 * hf + 512]
                            tsg = SC.do(lambda: sc.activation(sg_, banks[b][:], ACT.Sigmoid), t, V.last)
                            drained[b] = (tsg,)
                    gsl = gb[:, 0, tt, hf * 512:(hf + 1) * 512]
                    m = merged[:, tt, hf * 512:(hf + 1) * 512]
                    te_ = V.do(lambda: v.tensor_tensor(sg_, sg_, banks[b][:], ALU.mult), t, tsg)
                    drained[b] = (te_,)
                    te_ = V.do(lambda: v.tensor_tensor(gsl, gsl, sg_, ALU.mult), gtok[6 + hf][tt])
                    te_ = G.do(lambda: gp.tensor_tensor(m, m, gsl, ALU.add), te_, mt[(tt, hf)])
                    mt[(tt, hf)] = te_
            done(r, t)

        glu()

        top[0] = mark
        mer = [mt[(tt, 0)] for tt in range(2)], [mt[(tt, 1)] for tt in range(2)]
        tmerge = [mt[(1, 1)], mt[(1, 1)]]

        def cp(k, o, i, t):
            if k % 2:
                return SC.do(lambda: sc.copy(o, i), t)
            return V.do(lambda: v.tensor_copy(o, i), t)

        def residual(names, lhsT_of, nk, toks, gate, kw=512, tiles_of=None):
            ts = []
            for hf in range(2):
                w, tw, r = tile(names, hf)
                for tt in range(2):
                    b = bank("main")
                    t = mm(banks[b][:], [(lhsT_of(k, tt), w[:, k * 512:(k + 1) * 512]) for k in range(nk)], tw,
                           *toks, *drained[b])
                    ts.append(add_x(b, tt, hf, gate, t))
                done(r, t)
            return ts

        def add_x(b, tt, hf, gate, t):
            xs = xr[:, tt, hf * 512:(hf + 1) * 512]
            if gate is not None:
                js = junk[:, 0:512]
                V.do(lambda: v.tensor_tensor(js, gt[:, gate, hf * 512:(hf + 1) * 512], banks[b][:], ALU.mult), t,
                     m_tok["gt"])
                drained[b] = (V.last,)
                return V.do(lambda: v.tensor_tensor(xs, xs, js, ALU.add))
            te_ = V.do(lambda: v.tensor_tensor(xs, xs, banks[b][:], ALU.add), t)
            drained[b] = (te_,)
            return te_

        tmT = to_T(merged, hT, tmerge, cp)
        tx = residual("w_o", lambda k, tt: hT[:, k, tt * 128:(tt + 1) * 128], 8, tmT[-2:], 0)

        t_xn = rms(xn, None, *tx)
        t_h = norm_T(C_GFFN, 16, 24, t_xn, *tm2)
        hl = t_h[-1]
        fT = area(2, 4, S)
        f_free = [(), ()]
        facc = [4, 5, 6, 7]
        t_f = {}

        def up(j):
            w, tw, r = tile("w1", j)
            ts = []
            for pr in range(2):
                b = bank("main")
                for c in range(2):
                    t = gemm_T(w, 2 * pr + c, banks[b][:, c * S:(c + 1) * S], tw, hl, *drained[b])
                o = fT[:, j % 2, 2 * pr:2 * pr + 2, :].rearrange("p a b -> p (a b)")
                te_ = SC.do(lambda b=b, o=o: sc.activation(o, banks[b][:], ACT.Relu), t, *f_free[j % 2])
                drained[b] = (te_,)
                ts.append(G.do(lambda o=o: gp.tensor_tensor(o, o, o, ALU.mult), te_))
            done(r, t)
            t_f[j] = ts

        acc_t = {}

        def down(j):
            w, tw, r = tile("w2", j)
            for tt in range(2):
                for hf in range(2):
                    b = facc[2 * tt + hf]
                    for c in range(4):
                        first, last = j == 0 and c == 0, j == 7 and c == 3
                        l = fT[:, j % 2, c, tt * 128:(tt + 1) * 128]
                        rr = w[:, c * D + hf * 512:c * D + hf * 512 + 512]
                        t = PE.do(lambda b=b, l=l, rr=rr, first=first, last=last: te.matmul(
                            banks[b][:], l, rr, start=first, stop=last), tw, *t_f[j], *(drained[b] if first else ()))
                    acc_t[(tt, hf)] = t
            f_free[j % 2] = (t,)
            done(r, t)

        up(0)
        mods = []
        for j in range(8):
            if j < 7:
                up(j + 1)
            down(j)
            for mod in mods:
                next(mod)
            mods = []
            if j in (1, 3):
                mods.append(mod_gt(10 + j // 2, 1, j // 2, "main"))
                next(mods[0])
        tx = [add_x(facc[2 * tt + hf], tt, hf, 1, acc_t[(tt, hf)]) for tt in range(2) for hf in range(2)]

        fg = area(D)
        t_fg = load("fg", fg, A["rowb"][0:1, :].broadcast_to([P, D]), PE.last, V.last, q=SP)
        t_x1 = rms(xr, fg, t_fg, *tx)
        t_xn = rms(xn, None, *t_x1)
        t_h = norm_T(C_GMIX2, None, None, t_xn)
        hl = t_h[-1]
        top[0] = base2
        qT_ = area(4, S)
        kT2 = area(4, S)
        pexp = area(8, S)
        pT = area(2, 3, 128)
        yT = area(8, S)
        lf = area(2, 8)
        wf = area(8, 8)
        rot_t = area(S)
        sA = area(2, 512)
        blk_end = (PE.last, V.last, SC.last, G.last)
        t_wf = load("wf", wf.rearrange("p a b -> p (a b)"), A["wf"], *blk_end, q=SP)
        b = bank("misc")
        for tt in range(2):
            t = mm(banks[b][:, tt * 8:tt * 8 + 8],
                   [(hT[:, k, tt * 128:(tt + 1) * 128], wf[:, k, :]) for k in range(8)], t_wf, hl, *drained[b])
        fx, fe = small[:, 16:32], small[:, 32:48]
        V.do(lambda b=b: v.tensor_tensor(fx.rearrange("p (a b) -> p a b", a=2),
                                         banks[b][:, 0:16].rearrange("p (a b) -> p a b", a=2),
                                         rowa[:, R_BF:R_BF + 8].unsqueeze(1).broadcast_to([P, 2, 8]), ALU.add), t)
        drained[b] = (V.last,)
        V.do(lambda: v.tensor_scalar(fe, fx, -1.0, None, ALU.mult))
        V.do(lambda: v.tensor_tensor(fe, fx, fe, ALU.max))
        t = SC.do(lambda: sc.activation(fe, fe, ACT.Exp, scale=-1.0), V.last)
        t = SC.do(lambda: sc.activation(fe, fe, ACT.Ln, bias=1.0), t)
        lff = lf.rearrange("p a b -> p (a b)")
        V.do(lambda: v.tensor_scalar(fx, fx, 0.0, None, ALU.min), t)
        t_lf = V.do(lambda: v.tensor_tensor(lff, fx, fe, ALU.subtract), *blk_end)
        b = bank("misc")
        mm(banks[b][:, 0:8], [(iu, lf[:, 0, :])], t_lf, *drained[b])
        t = mm(banks[b][:, 8:16], [(ones[:], lf[:, 0, :]), (iu, lf[:, 1, :])])
        cq = small[:, 48:64]
        t_cq = V.do(lambda b=b: v.tensor_copy(cq, banks[b][:, 0:16]), t)
        drained[b] = (t_cq,)
        nlf = cact[:, 0:16].rearrange("p (a b) -> p a b", a=2)
        t_nlf = V.do(lambda: v.tensor_scalar(cact[:, 0:16], lff, -1.0, None, ALU.mult), PE.last)
        ut = area(2, S)
        V.do(lambda: v.tensor_copy(ut[:, 0, 0:128], iu))
        V.do(lambda: v.tensor_copy(ut[:, 0, 128:256], ones[:]))
        V.do(lambda: v.memset(ut[:, 1, 0:128], 0.0))
        t_ut = V.do(lambda: v.tensor_copy(ut[:, 1, 128:256], iu))

        def project_T(i, dst, rope, scl):
            w, tw, r = tile("qkv", i)
            ts = []
            for c in range(4):
                b = bank("main")
                t = gemm_T(w, c, banks[b][:, 0:S], tw, hl, *drained[b])
                d_ = dst[:, c, :]
                te_ = SC.do(lambda b=b, d_=d_: sc.mul(d_, banks[b][:, 0:S], scl), t, PE.last)
                drained[b] = (te_,)
                if rope:
                    b2 = bank("misc")
                    t2 = mm(banks[b2][:, 0:S], [(rotm, d_)], te_, *drained[b2])
                    V.do(lambda b2=b2: v.tensor_tensor(rot_t, banks[b2][:, 0:S], K[:, K_SIN:K_SIN + S], ALU.mult), t2)
                    drained[b2] = (V.last,)
                    V.do(lambda d_=d_: v.tensor_tensor(d_, d_, K[:, K_COS:K_COS + S], ALU.mult), te_)
                    te_ = V.do(lambda d_=d_: v.tensor_tensor(d_, d_, rot_t, ALU.add))
                ts.append(te_)
            done(r, t)
            return ts

        def project_rows(i, dst):
            w, tw, r = tile("qkv", i)
            ts = []
            for tt in range(2):
                b = bank("main")
                t = gemm_rows(w, tt, banks[b][:], 0, 512, tw, hl, *drained[b])
                te_ = SC.do(lambda b=b, tt=tt: sc.copy(dst[:, tt, :], banks[b][:]), t)
                drained[b] = (te_,)
                ts.append(te_)
            done(r, t)
            return ts

        def attention(kind, tq, tk, tv):
            for qt in range(2):
                nk = 128 * (qt + 1)
                te_ = None
                tz = []
                for h in range(8):
                    c, e = h // 2, h % 2
                    b = bank("misc")
                    ql = qT_[64 * e:64 * e + 64, c, qt * 128:(qt + 1) * 128]
                    kr = kT2[64 * e:64 * e + 64, c, 0:nk]
                    if kind:
                        pairs = [(ql, kr)] + [(lb(s, h), ut[:, s, 0:nk]) for s in range(qt + 1)]
                        t = mm(banks[b][:, 0:nk], pairs, *tq, *tk, t_ut, t_lb, *drained[b])
                    else:
                        t = mm(banks[b][:, 0:nk], [(ql, kr)], *tq, *tk, *drained[b])
                    te1 = V.do(lambda b=b, h=h, nk=nk: v.tensor_tensor(pexp[:, h, nk - 128:nk],
                                                                      banks[b][:, nk - 128:nk], neg, ALU.add), t,
                                *pfree[h])
                    te2 = None
                    if qt:
                        te2 = SC.do(lambda b=b, h=h: sc.copy(pexp[:, h, 0:128], banks[b][:, 0:128]), t, te1)
                    drained[b] = (te1, te2)
                    V.do(lambda h=h, nk=nk: v.tensor_reduce(small[:, h:h + 1], pexp[:, h, 0:nk], X, ALU.max), te2)
                    V.do(lambda h=h: v.tensor_scalar(small[:, 8 + h:9 + h], small[:, h:h + 1], -1.0, None, ALU.mult))
                    if kind:
                        V.do(lambda h=h, qt=qt: v.tensor_tensor(small[:, h:h + 1], small[:, h:h + 1],
                                                                cq[:, 8 * qt + h:8 * qt + h + 1], ALU.add))
                        V.do(lambda h=h, qt=qt: v.tensor_tensor(small[:, 8 + h:9 + h],
                                                                cq[:, 8 * qt + h:8 * qt + h + 1],
                                                                small[:, h:h + 1], ALU.subtract))
                    tz = SC.do(lambda h=h, nk=nk: sc.activation(pexp[:, h, 0:nk], pexp[:, h, 0:nk], ACT.Exp,
                                                                bias=small[:, 8 + h:9 + h],
                                                                accum_out=small[:, 16 + h:17 + h]), V.last)
                    V.do(lambda h=h: v.reciprocal(small[:, 24 + h:25 + h], small[:, 16 + h:17 + h]), tz)
                    tn = V.do(lambda h=h, nk=nk: v.tensor_scalar(pexp[:, h, 0:nk], pexp[:, h, 0:nk],
                                                                 small[:, 24 + h:25 + h], None, ALU.mult))
                    b = bank("misc")
                    for kc in range(qt + 1):
                        t = tr(banks[b][:, kc * 128:(kc + 1) * 128], pexp[:, h, kc * 128:(kc + 1) * 128], tn,
                               *drained[b])
                    pfree[h] = (t,)
                    pt = pT[:, e, 0:qt + 1, :].rearrange("p a b -> p (a b)")
                    tpt = SC.do(lambda b=b, pt=pt, nk=nk: sc.copy(pt, banks[b][:, 0:nk]), t, *ptfree[e])
                    drained[b] = (tpt,)
                    b = bank("misc")
                    t = mm(banks[b][:, 0:128], [
                        (vrow(kind, kc, c), pT[:, e, kc, :]) for kc in range(qt + 1)], tpt, *tv, *drained[b])
                    ptfree[e] = (t,)
                    o = yT[64 * e:64 * e + 64, 4 * kind + c, qt * 128:(qt + 1) * 128]
                    te_ = V.do(lambda b=b, o=o, e=e: v.tensor_copy(o, banks[b][64 * e:64 * e + 64, 0:128]), t)
                    drained[b] = (te_,)
            return te_

        vals = {}

        def vrow(kind, kc, c):
            return vals[kind][:, kc, c * 128:(c + 1) * 128]

        lbt = area(2, 8, 128)
        for s_ in range(2):
            for h in range(8):
                t_lb = G.do(lambda s_=s_, h=h: gp.tensor_scalar(lbt[:, s_, h, :], ones[:], nlf[:, s_, h:h + 1], None,
                                                                ALU.mult), t_nlf, *blk_end)
        lb = lambda s_, h: lbt[:, s_, h, :]
        pfree = {h: () for h in range(8)}
        ptfree = {0: (), 1: ()}
        SC.wait(*blk_end)
        tq = project_T(0, qT_, True, 0.125)
        tk = project_T(1, kT2, True, 1.0)
        vals[0] = area(2, 512)
        tv = project_rows(2, vals[0])
        ty = attention(0, tq, tk, tv)
        tq = project_T(3, qT_, False, 0.125)
        tk = project_T(4, kT2, False, 1.0)
        vals[1] = vals[0]
        SC.wait(PE.last, V.last)
        tv = project_rows(5, vals[1])
        ty2 = attention(1, tq, tk, tv)

        wA, twA, rA = tile("ba")
        wB, twB, rB = tile("bb")
        mg = merged
        for br, (w_, tw_, r_) in enumerate(((wA, twA, rA), (wB, twB, rB))):
            for tt in range(2):
                for hf in range(2):
                    b = bank("main")
                    t = mm(banks[b][:], [(yT[:, 4 * br + c, tt * 128:(tt + 1) * 128],
                                          w_[:, c * D + hf * 512:c * D + hf * 512 + 512]) for c in range(4)],
                           tw_, ty, ty2, *drained[b])
                    o = (mg if br == 0 else xn)[:, tt, hf * 512:(hf + 1) * 512]
                    te_ = SC.do(lambda b=b, o=o: sc.copy(o, banks[b][:]), t, *blk_end)
                    drained[b] = (te_,)
            done(r_, t)
        t_br = te_
        for i in range(4):
            w, tw, r = tile("g2", i)
            for tt in range(2):
                b = bank("main")
                t = gemm_rows(w, tt, banks[b][:], 0, 512, tw, hl, *drained[b])
                s_ = sA[:, tt, :]
                te1 = SC.do(lambda b=b, s_=s_: sc.activation(s_, banks[b][:], ACT.Sigmoid), t, V.last)
                drained[b] = (te1,)
                o = (mg if i < 2 else xn)[:, tt, (i % 2) * 512:(i % 2) * 512 + 512]
                te_ = V.do(lambda s_=s_, o=o: v.tensor_tensor(o, o, s_, ALU.mult), te1, t_br)
                if i >= 2:
                    m_ = mg[:, tt, (i % 2) * 512:(i % 2) * 512 + 512]
                    te_ = V.do(lambda o=o, m_=m_: v.tensor_tensor(m_, m_, o, ALU.add))
            done(r, t)
        tmT = to_T(mg, hT, [te_, te_], lambda k, o, i, t: cp(k, o, i, t))
        tx = residual("wout", lambda k, tt: hT[:, k, tt * 128:(tt + 1) * 128], 8, tmT[-2:], None)

        fg2 = fg
        t_fg = load("fg2", gt[:], A["rowb2"].broadcast_to([P, 2 * D]), V.last, q=SP)
        t_xn = rms(xn, gt[:, 0, :], t_fg, *tx)
        t_h = to_T(xn, hT, t_xn, cp)
        top[0] = base2
        scr = area(2, 16, 128)
        qp = area(16, S)
        sv = area(2, 16)
        siu = area(2, 16)
        sif = area(2, 16)
        work = area(128)
        cand = area(16, 16)
        cw = area(256)
        best = area(16)
        pku = area(16)
        pij = area(2, 16)
        eq = area(2, 256)
        e01 = area(2, 16)
        idx = area(2, 128)
        gat = area(2, 128)
        hv = area(2, 128)
        av = area(2, 128)
        sm = area(8)
        acc2 = area(2, D)
        extra = [area(D) for _ in range((ARENA - top[0]) // D)]
        iota = K[:, K_IOTA:K_IOTA + 16]
        U_ = lambda a: a.bitcast(U32)
        pre = (PE.last, V.last, SC.last)
        tq_ = {}
        for i in range(4):
            w, tw, r = tile("pq", i)
            for c in range(0, 4, 2):
                b = bank("main")
                for e in range(2):
                    t = gemm_T(w, c + e, banks[b][:, e * S:(e + 1) * S], tw, *t_h[-2:], *drained[b])
                o = qp[:, 4 * i + c:4 * i + c + 2, :].rearrange("p a b -> p (a b)")
                te_ = SC.do(lambda: sc.copy(o, banks[b][:]), t, *pre)
                drained[b] = (te_,)
            tq_[i] = te_
            done(r, t)
        keys, tkey, rkey = tile("keys")
        t_scr = {}
        for tt in range(2):
            for g in range(4):
                b = bank("misc")
                for j in range(4):
                    hp = 4 * g + j
                    t = mm(banks[b][:, j * 128:(j + 1) * 128],
                           [(qp[:, hp, tt * 128:(tt + 1) * 128], keys[:, hp * 128:(hp + 1) * 128])], tq_[g], tkey,
                           *drained[b])
                o = scr[:, tt, 4 * g:4 * g + 4, :].rearrange("p a b -> p (a b)")
                te_ = SC.do(lambda: sc.copy(o, banks[b][:]), t, *pre)
                drained[b] = (te_,)
                t_scr[(tt, g)] = te_
        done(rkey, t)

        t_idx = {}
        t_gat = {}
        last = {"exp": None}

        def choose(tt, h):
            V.wait(t_scr[(tt, h // 2)])
            for s_ in range(2):
                x_ = scr[:, tt, 2 * h + s_, :]
                V.do(lambda: v.max(sv[:, s_, 0:8], x_))
                V.do(lambda: v.max_index(U_(siu[:, s_, 0:8]), sv[:, s_, 0:8], x_))
                V.do(lambda: v.match_replace(work, sv[:, s_, 0:8], x_, -3.0e38))
                V.do(lambda: v.max(sv[:, s_, 8:16], work))
                V.do(lambda: v.max_index(U_(siu[:, s_, 8:16]), sv[:, s_, 8:16], work))
            V.do(lambda: v.tensor_copy(sif, U_(siu)))
            V.do(lambda: v.tensor_tensor(cand, sv[:, 0, :].unsqueeze(2).broadcast_to([P, 16, 16]),
                                         sv[:, 1, :].unsqueeze(1).broadcast_to([P, 16, 16]), ALU.add))
            cd = cand.rearrange("p a b -> p (a b)")
            V.do(lambda: v.max(best[:, 0:8], cd))
            V.do(lambda: v.max_index(U_(pku[:, 0:8]), best[:, 0:8], cd))
            V.do(lambda: v.match_replace(cw, best[:, 0:8], cd, -3.0e38))
            V.do(lambda: v.max(best[:, 8:16], cw))
            V.do(lambda: v.max_index(U_(pku[:, 8:16]), best[:, 8:16], cw))
            V.do(lambda: v.tensor_scalar(sm[:, 0:1], best[:, 0:1], -1.0, None, ALU.mult), last["exp"])
            o = slice(16 * h, 16 * h + 16)
            t = SC.do(lambda: sc.activation(gat[:, tt, o], best, ACT.Exp, bias=sm[:, 0:1],
                                            accum_out=sm[:, 1:2]), V.last)
            last["exp"] = t
            V.do(lambda: v.tensor_single_scalar(U_(pij[:, 0, :]), U_(pku), 4, ALU.logical_shift_right))
            V.do(lambda: v.tensor_single_scalar(U_(pij[:, 1, :]), U_(pku), 15, ALU.bitwise_and))
            V.do(lambda: v.tensor_copy(e01, U_(pij)))
            e3 = eq.rearrange("p s (k i) -> p (s k) i", i=16)
            e4 = eq.rearrange("p s (k i) -> p s k i", i=16)
            ef = e01.rearrange("p s k -> p (s k)")
            V.do(lambda: v.tensor_tensor(e3, ef.unsqueeze(2).broadcast_to([P, 32, 16]),
                                         iota.unsqueeze(1).broadcast_to([P, 32, 16]), ALU.is_equal))
            V.do(lambda: v.tensor_tensor(e4, e4, sif.unsqueeze(2).broadcast_to([P, 2, 16, 16]), ALU.mult))
            V.do(lambda: v.tensor_reduce(ef, e3, X, ALU.add))
            V.do(lambda: v.scalar_tensor_tensor(e01[:, 0, :], e01[:, 0, :], 128.0, e01[:, 1, :], ALU.mult, ALU.add))
            t_idx[(tt, h)] = V.do(lambda: v.tensor_copy(U_(idx[:, tt, o]), e01[:, 0, :]))
            V.do(lambda: v.reciprocal(sm[:, 2:3], sm[:, 1:2]), t)
            t_gat[(tt, h)] = V.do(lambda: v.tensor_scalar(gat[:, tt, o], gat[:, tt, o], sm[:, 2:3], None, ALU.mult))

        rv = ring[:].rearrange("p r (a b) -> p (r a) b", b=D)
        slots = extra + [rv[:, i, :] for i in range(4 * RING)]
        NG = len(slots)
        gsem = [sem(f"gather{i}") for i in range(NG)]
        gn = [0]
        gfree = [()] * NG
        quiet = (PE.last, blk_end[1])

        def gather(table, tt, e):
            n = gn[0]
            gn[0] += 1
            i = n % NG
            ap = U_(idx[:, tt, e:e + 1])
            return i, G.dma(lambda: gp.indirect_dma_start(slots[i], None, table,
                                                          bass.IndirectOffsetOnAxis(ap=ap, axis=0)),
                            gsem[i], 16 * (n // NG + 1), t_idx[(tt, e // 16)], *quiet, *gfree[i])

        steps = [(tt, h) for tt in range(2) for h in range(8)]
        t_av = {}

        def phase_u(tt, h):
            for k in range(16):
                e = 16 * h + k
                i, tg = gather(A["eu"], tt, e)
                t = V.do(lambda: v.tensor_tensor_reduce(
                    out=slots[i], in0=slots[i], in1=xn[:, tt, :],
                    scale=1.0, scalar=0.0, op0=ALU.mult, op1=ALU.add,
                    accum_out=hv[:, tt, e:e + 1]), tg, loose=True)
                gfree[i] = (t,)
            o = slice(16 * h, 16 * h + 16)
            t_av[(tt, h)] = SC.do(lambda: sc.activation(av[:, tt, o], hv[:, tt, o], ACT.Gelu), t)

        def phase_v(tt, h):
            o = slice(16 * h, 16 * h + 16)
            ta = V.do(lambda: v.tensor_tensor(av[:, tt, o], av[:, tt, o], gat[:, tt, o], ALU.mult), t_av[(tt, h)],
                      t_gat[(tt, h)])
            for k in range(16):
                e = 16 * h + k
                i, tg = gather(A["ev"], tt, e)
                acc = (xr[:, tt, :], acc2[:, tt, :])[k % 2]
                t = V.do(lambda: v.scalar_tensor_tensor(acc, slots[i], av[:, tt, e:e + 1], acc, ALU.mult, ALU.add),
                         tg, ta, accs[(tt, k % 2)], loose=True)
                accs[(tt, k % 2)] = t
                gfree[i] = (t,)

        t = V.do(lambda: v.memset(acc2, 0.0), *pre)
        accs = {(tt, p): t for tt in range(2) for p in range(2)}
        choose(*steps[0])
        for n, (tt, h) in enumerate(steps):
            if n + 1 < len(steps):
                choose(*steps[n + 1])
            phase_u(tt, h)
            if n:
                phase_v(*steps[n - 1])
        phase_v(*steps[-1])
        V.do(lambda: v.tensor_tensor(xr[:], xr[:], acc2, ALU.add))

        t_fin = rms(xn, gt[:, 1, :], V.last)
        so = sem("out")
        SP.dma(lambda: nc.sync.dma_start(out, xn), so, 16, *t_fin)
        SP.wait((so, 16))


def shape_constants():
    k = np.zeros((P, N_K), np.float32)
    i = np.arange(P)
    k[:, K_ID:K_ID + 128] = np.eye(P)
    k[:, K_SU:K_SU + 128] = i[:, None] < i[None, :]
    k[:, K_IU:K_IU + 128] = i[:, None] <= i[None, :]
    k[:, K_SL:K_SL + 128] = i[:, None] > i[None, :]
    k[:, K_NEG:K_NEG + 128] = np.where(i[None, :] <= i[:, None], 0.0, -1e30)
    k[:, K_BLK:K_BLK + 128] = (i[:, None] // 64) == (i[None, :] // 64)
    k[:, K_HSEL:K_HSEL + 2] = (i[:, None] // 64) == np.arange(2)[None, :]
    d = i % 64
    for m in range(P):
        if d[m] < 8:
            k[m + 8, K_ROT + m] = -1.0
        elif d[m] < 16:
            k[m - 8, K_ROT + m] = 1.0
    freq = np.power(np.float32(500000.0), -np.arange(8, dtype=np.float32) / np.float32(8)).astype(np.float32)
    ang = np.arange(S, dtype=np.float32)[None, :] * freq[:, None]
    cos, sin = np.cos(ang), np.sin(ang)
    k[:, K_COS:K_COS + S] = 1.0
    for m in range(P):
        if d[m] < 16:
            k[m, K_COS:K_COS + S] = cos[d[m] % 8]
            k[m, K_SIN:K_SIN + S] = sin[d[m] % 8]
    for lv in range(7):
        s, t = i[:, None], i[None, :]
        m = (s >> (lv + 1) == t >> (lv + 1)) & ((s >> lv) & 1 == 0) & ((t >> lv) & 1 == 1)
        k[:, K_LEV + lv * 128:K_LEV + (lv + 1) * 128] = m
    k[:, K_IOTA:K_IOTA + 16] = np.arange(16)[None, :]
    return k


def lay_out(a):
    def t512(w):
        n = w.shape[1] // 512
        return np.ascontiguousarray(w.reshape(8, 128, n, 512).transpose(2, 1, 0, 3).reshape(n, 128, 4096))

    def kchunks(w):
        return w.reshape(-1, 128, w.shape[1]).transpose(1, 0, 2).reshape(128, -1)

    def col(x):
        return np.asarray(x).reshape(-1, 128).T

    f = np.float32
    ada = t512(a["ada_w"][0])
    ada = np.ascontiguousarray(ada[[0, 1, 2, 3, 4, 5, 6, 7, 8, 9, 10, 11]])
    ab = a["ada_b"][0]
    w_in = a["w_in"][0]
    wp = np.zeros((1024, 2560), f)
    chunk = [w_in[:, 128 * i:128 * i + 128] for i in range(19)]
    order = [0, 1, 2, 3, 4, 5, 6, 17, 18, 7, 9, 10, 8, 11, 12, 13, 14, 15, 16]
    for n, i in enumerate(order):
        wp[:, 128 * n:128 * n + 128] = chunk[i]
    cols = np.zeros((P, N_COLS), f)
    cols[:, C_MU:C_MU + 7] = col(a["rwkv_mu"][0])
    for c, n in ((C_W0, "rwkv_w0"), (C_A0, "rwkv_a0"), (C_KK, "rwkv_kk"), (C_KA, "rwkv_ka"), (C_RK, "rwkv_rk"),
                 (C_SD, "s5_d")):
        cols[:, c:c + 2] = col(a[n][0])
    for j in range(3):
        cols[:, C_CONV + 2 * j:C_CONV + 2 * j + 2] = col(a["conv_w"][0, j])
    cols[:, C_ARE:C_ARE + 8] = col(a["s5_a_re"][0])
    cols[:, C_AIM:C_AIM + 8] = col(a["s5_a_im"][0])
    cols[:, C_DT:C_DT + 8] = col(np.repeat(a["s5_log_dt"][0], 64))
    cols[:, C_C:C_C + 8] = col(a["c"])
    cols[:, C_GMIX:C_GMIX + 8] = col(a["norm_mix_g"])
    cols[:, C_GFFN:C_GFFN + 8] = col(a["norm_ffn_g"])
    cols[:, C_GMIX2:C_GMIX2 + 8] = col(a["norm_mix_g_2"])
    cols[:, C_ADAB:C_ADAB + 32] = col(np.concatenate([ab[0:2048], ab[3072:5120]]))
    rowa = np.zeros((1, N_ROWA), f)
    for r, n in ((R_LNXW, "rwkv_lnx_w"), (R_LNXB, "rwkv_lnx_b"), (R_SGW, "sg_ln_w"), (R_SGB, "sg_ln_b")):
        rowa[0, r:r + 256] = a[n][0]
    rowa[0, R_BF:R_BF + 8] = a["b_forget_2"][0]
    w6 = np.zeros((P, 768), f)
    w6[0:32, 0:256] = a["rwkv_w2"][0]
    w6[32:64, 256:512] = a["rwkv_a2"][0]
    w6[64:128, 512:768] = a["rwkv_g2"][0]
    ws = np.ascontiguousarray(a["sg_ws"][0].transpose(2, 0, 1))
    bs = np.zeros((P, 2, 128), f)
    for g in range(4):
        bs[64 * (g % 2):64 * (g % 2) + 64, g // 2, :] = a["sg_bs"][0, g][None, :]
    s5b = np.zeros((4, P, 4, 128), f)
    s5c = np.zeros((4, P, 4, 128), f)
    for i, (nb, ncn) in enumerate((("s5_b_re", "s5_c_re"), ("s5_b_im", "s5_c_im"))):
        for g in range(16):
            hf, q, e, ch = g // 8, (g % 8) // 2, g % 2, (g % 8) * 16
            s5b[2 * hf + i, ch:ch + 16, q, 64 * e:64 * e + 64] = a[nb][0, g].T
            s5c[2 * hf + i, 64 * e:64 * e + 64, q, ch:ch + 16] = a[ncn][0, g].T
    w2 = a["w_in_2"][0]
    return {
        "x": np.ascontiguousarray(a["x"][0].reshape(2, 128, 1024).transpose(1, 0, 2)),
        "cols": cols, "K": shape_constants(), "rowa": rowa,
        "ada": ada,
        "adab_g": np.ascontiguousarray(np.concatenate([ab[2048:3072], ab[5120:6144]])[None, :]),
        "wp": t512(wp), "gates": t512(w_in[:, 2432:6528]),
        "o_ab": np.ascontiguousarray(np.concatenate([kchunks(a["rwkv_out"][0]), kchunks(a["sg_out"][0])], 1)[None]),
        "o_c": np.ascontiguousarray(kchunks(a["conv_out"][0])[None]),
        "glu": np.ascontiguousarray(kchunks(a["s5_glu_w"][0])[None]),
        "w_o": t512(a["w_o"][0]), "w1": t512(a["ffn_w1"][0]),
        "w2": np.ascontiguousarray(a["ffn_w2"][0].reshape(8, 4, 128, 1024).transpose(0, 2, 1, 3).reshape(8, 128, 4096)),
        "w6": w6, "ws": ws, "bs": bs, "s5b": s5b, "s5c": s5c,
        "rowb": a["final_g"][None, :].copy(),
        "qkv": t512(w2[:, 0:3072]),
        "wf": np.ascontiguousarray(w2[:, 3072:3080].reshape(8, 128, 8).transpose(1, 0, 2).reshape(128, 64)),
        "g2": t512(w2[:, 3080:5128]),
        "ba": np.ascontiguousarray(kchunks(a["w_branch_a_2"][0])[None]),
        "bb": np.ascontiguousarray(kchunks(a["w_branch_b_2"][0])[None]),
        "wout": t512(a["w_out_2"][0]), "pq": t512(a["w_peer_q_2"][0]),
        "keys": np.ascontiguousarray(a["peer_sub_keys_2"][0].transpose(3, 0, 1, 2).reshape(1, 128, 2048)),
        "rowb2": np.concatenate([a["norm_ffn_g_2"][0], a["norm_final_g_2"]])[None, :].copy(),
        "eu": a["peer_expert_u_2"][0], "ev": a["peer_expert_v_2"][0],
    }


def kernel(**inputs):
    import concourse.bacc as _bacc
    from concourse.bass_utils import run_bass_kernel_spmd as _run

    a = lay_out({k: np.asarray(x) for k, x in inputs.items()})
    nc = _bacc.Bacc("TRN2", target_bir_lowering=False, num_devices=1)
    arrays, A = {}, {}
    for name, x in a.items():
        x = np.ascontiguousarray(x)
        arrays[f"in_{name}"] = x
        A[name] = nc.dram_tensor(f"in_{name}", x.shape, mybir.dt.from_np(x.dtype), kind="ExternalInput").ap()
    out = nc.dram_tensor("out_0", (P, 2, D), F32, kind="ExternalOutput").ap()
    build(nc, A, out)
    r = _run(nc, [arrays], core_ids=[0])
    return np.ascontiguousarray(r.results[0]["out_0"].transpose(1, 0, 2).reshape(1, S, D))
```

```python
from contextlib import ExitStack

import numpy as np

import concourse.bass as bass
from concourse import mybir

ALU = mybir.AluOpType
ACT = mybir.ActivationFunctionType
F32 = mybir.dt.float32
U32 = mybir.dt.uint32
X = mybir.AxisListType.X

P = 128
S = 256
D = 1024
RING = 3
TILE = 4096
ARENA = 30936

C_MU, C_W0, C_A0, C_KK, C_KA, C_RK, C_CONV, C_SD = 0, 7, 9, 11, 13, 15, 17, 23
C_ARE, C_AIM, C_DT, C_C, C_GMIX, C_GFFN, C_GMIX2, C_ADAB, N_COLS = 25, 33, 41, 49, 57, 65, 73, 81, 113

R_LNXW, R_LNXB, R_SGW, R_SGB, R_BF, N_ROWA = 0, 256, 512, 768, 1024, 1032

K_ID, K_SU, K_IU, K_ZN, K_NEG, K_BLK, K_HSEL, K_ROT, K_COS, K_SIN = 0, 128, 256, 384, 512, 640, 768, 770, 898, 1154
K_LEV, K_IOTA, N_K = 1410, 1410 + 7 * 128, 1410 + 7 * 128 + 16


class Queue:

    def __init__(self, eng, sem, chain):
        self.eng, self.sem, self.chain = eng, sem, chain
        self.count, self.last, self.seen = 0, None, {}

    def wait(self, *tokens):
        need = {}
        for t in tokens:
            if t is not None and self.seen.get(t[0].name, 0) < t[1]:
                self.seen[t[0].name] = t[1]
                need[t[0].name] = t
        for s, n in need.values():
            self.eng.wait_ge(s, n)

    def do(self, f, *tokens, loose=False, count=True):
        if self.chain and not loose:
            tokens = tokens + (self.last,)
        self.wait(*tokens)
        ins = f()
        if count:
            ins.then_inc(self.sem, 1)
            self.count += 1
            self.last = (self.sem, self.count)
        return self.last

    def dma(self, f, sem, value, *tokens):
        self.wait(*tokens)
        f().then_inc(sem, 16)
        return (sem, value)


SCHEDULE = ["", "", "", "", "", "", "", "d", "ad", "d", "ad", "da", "d", "db", "d", "bd", "b", "d", "bcd", "bcd",
            "ad", "ad", "ad", "ad", "ad", "a", "add", "a", "ad", "ad", "d", "ad", "ad", "ad", "ad", "ad", "ad", "ad",
            "ad", "ad", "d", "dd", "ad", "ada", "ad", "ad", "ada", "ad", "ad", "ad", "add", "a", "add"]
PLAN = [("gates", 4), ("ada", 4), ("gates", 5), ("gates", 2), ("ada", 5), ("gates", 3), ("bc", 0), ("gates", 6),
        ("gates", 7), ("ada", 6), ("gates", 0), ("ada", 7), ("gates", 1)]


def build(nc, A, out):
    with ExitStack() as ctx:
        def sb(name, shape, dt=F32):
            return ctx.enter_context(nc.sbuf_tensor(name, shape, dt))

        def sem(name):
            return ctx.enter_context(nc.semaphore(name))

        V = Queue(nc.vector, sem("v"), True)
        SC = Queue(nc.scalar, sem("a"), True)
        G = Queue(nc.gpsimd, sem("g"), True)
        PE = Queue(nc.tensor, sem("pe"), False)
        SP = Queue(nc.sync, sem("sp"), False)
        v, sc, gp, te = nc.vector, nc.scalar, nc.gpsimd, nc.tensor

        ring = sb("ring", [P, RING, TILE])
        xr = sb("xr", [P, 2, D])
        hT = sb("hT", [P, 8, S])
        cols = sb("cols", [P, N_COLS])
        rowa = sb("rowa", [P, N_ROWA])
        K = sb("K", [P, N_K])
        gt = sb("gt", [P, 2, D])
        modT = sb("modT", [P, 32])
        small = sb("small", [P, 112])
        ones = sb("ones", [P, P])
        cact = sb("cact", [P, 16])
        wf = sb("wf", [P, 8, 8])
        arena = sb("arena", [P, ARENA])
        banks = [ctx.enter_context(nc.psum_tensor(f"ps{i}", [P, 512], F32)) for i in range(8)]
        drained = [()] * 8
        turn = {"main": 0, "misc": 0, "s5": 0}
        POOLS = {"main": (0, 1, 2, 3), "misc": (4, 5, 6, 7)}

        top = [0]

        def area(*shape):
            n = int(np.prod(shape))
            a = arena[:, top[0]:top[0] + n]
            top[0] += n
            assert top[0] <= ARENA, top
            if len(shape) == 2:
                a = a.rearrange("p (a b) -> p a b", a=shape[0])
            if len(shape) == 3:
                a = a.rearrange("p (a b c) -> p a b c", a=shape[0], b=shape[1])
            return a

        def bank(pool):
            t = turn[pool]
            turn[pool] = t + 1
            return POOLS[pool][t % len(POOLS[pool])]

        ident, su, iu = (K[:, o:o + 128] for o in (K_ID, K_SU, K_IU))
        blk, hsel, rotm = K[:, K_BLK:K_BLK + 128], K[:, K_HSEL:K_HSEL + 2], K[:, K_ROT:K_ROT + 128]

        def load(name, dst, src, *tokens, q=SC):
            s = sem("l_" + name)
            return q.dma(lambda: q.eng.dma_start(dst, src), s, 16, *tokens)

        t_cols = load("cols", cols[:], A["cols"], q=SP)
        t_K = load("ident", ident, A["K"][:, 0:128])

        stream = ([("ada", i) for i in range(4)]
                  + [("wp", i) for i in range(5)]
                  + [x for kind, i in PLAN for x in ([(kind, i)] if kind != "bc" else [("o_ab", 0), ("o_c", 0)])]
                  + [("ada", 8), ("o_ab", 0), ("ada", 9), ("glu", 0), ("w_o", 0), ("w_o", 1)]
                  + [("w1", 0)]
                  + [x for i in range(8) for x in ([("w1", i + 1)] if i < 7 else []) + [("w2", i)]
                     + ([("ada", 10 + i // 2)] if i in (1, 3) else [])]
                  + [("qkv", i) for i in range(6)]
                  + [("g2", 0), ("g2", 1), ("ba", 0), ("g2", 2), ("g2", 3), ("bb", 0)]
                  + [("wout", i) for i in range(2)]
                  + [("pq", i) for i in range(4)])
        stream = [(n, i, 2048 if n == "o_c" else TILE) for n, i in stream]
        ring_sems = [sem(f"ring{i}") for i in range(RING)]
        state = {"loaded": 0, "used": 0, "free": [()] * RING}

        def prefetch():
            n = state["loaded"]
            if n == len(stream):
                return
            state["loaded"] += 1
            name, i, w = stream[n]
            r = n % RING
            dst, src = ring[:, r, 0:w], A[name][i]
            SP.dma(lambda: nc.sync.dma_start(dst, src), ring_sems[r], 16 * (n // RING + 1), *state["free"][r])

        prefetch()
        prefetch()
        t_x = load("x", xr[:], A["x"], q=SP)
        prefetch()

        def tile(name, i=0):
            n = state["used"]
            assert stream[n][:2] == (name, i), (stream[n], name, i)
            state["used"] += 1
            return ring[:, n % RING, :], (ring_sems[n % RING], 16 * (n // RING + 1)), n % RING

        def done(r, *tokens):
            state["free"][r] = tokens
            prefetch()

        def mm(o, pairs, *tokens):
            n = len(pairs)
            for i, (l, r) in enumerate(pairs):
                t = PE.do(lambda l=l, r=r, i=i: te.matmul(o, l, r, start=(i == 0), stop=(i == n - 1)),
                          *(tokens if i == 0 else ()), count=(i == n - 1))
            return t

        def tr(o, i, *tokens):
            return PE.do(lambda: te.transpose(o, i, ident), *tokens)

        mrow = area(2, 512)
        junk = area(D)
        merged = area(2, D)
        xn = area(2, D)
        base2 = top[0]

        t_one = V.do(lambda: v.memset(ones[:], 1.0))
        t_eps = V.do(lambda: v.memset(small[:, 64:65], 1e-6))
        t_sg = SC.do(lambda: sc.activation(cact[:, 8:16], cols[:, C_C:C_C + 8], ACT.Sigmoid), t_cols)
        t_c = V.do(lambda: v.tensor_tensor(cact[:, 0:8], cols[:, C_C:C_C + 8], cact[:, 8:16], ALU.mult), t_sg, t_cols)
        m_tok = {"gt": None, 0: None, 1: None, "n": 0}

        def ada_sum(i):
            w, tw, r = tile("ada", i)
            p = m_tok["n"] % 2
            m_tok["n"] += 1
            acc = mrow[:, p, :], junk[:, p * 512:(p + 1) * 512]
            ts = [None, None]
            for k in range(8):
                a_ = acc[k % 2]
                if k < 2:
                    t = V.do(lambda: v.tensor_scalar(a_, w[:, k * 512:(k + 1) * 512], cact[:, k:k + 1], None,
                                                     ALU.mult), tw, t_c, m_tok[p], loose=True)
                else:
                    t = V.do(lambda: v.scalar_tensor_tensor(a_, w[:, k * 512:(k + 1) * 512], cact[:, k:k + 1], a_,
                                                            ALU.mult, ALU.add), ts[k % 2], loose=True)
                ts[k % 2] = t
            done(r, t)
            t = V.do(lambda: v.tensor_tensor(acc[0], acc[0], acc[1], ALU.add), t)
            return acc[0], t, p

        def mod_T(i, j0):
            acc, t, p = ada_sum(i)
            yield
            b = bank("misc")
            for q in range(4):
                t = mm(banks[b][:, q:q + 1], [(acc[:, q * 128:(q + 1) * 128], ones[:, 0:1])], t, t_one,
                       *drained[b])
            m_tok[p] = t
            tc = V.do(lambda: v.tensor_tensor(modT[:, j0:j0 + 4], banks[b][:, 0:4],
                                              cols[:, C_ADAB + j0:C_ADAB + j0 + 4], ALU.add), t, t_cols)
            drained[b] = (tc,)
            tm2.append(tc)
            yield

        def mod_gt(i, which, half, pool="misc"):
            acc, t, p = ada_sum(i)
            yield
            b = bank(pool)
            t = mm(banks[b][:], [(ones[:], acc)], t, t_one, *drained[b])
            m_tok[p] = t
            dst = gt[:, which, half * 512:(half + 1) * 512]
            m_tok["gt"] = V.do(lambda: v.tensor_tensor(dst, dst, banks[b][:], ALU.add), t, t_gtb)
            drained[b] = (m_tok["gt"],)
            yield

        def rms_rows(tt, dst, gain, o, junk_, *toks, on_act=False):
            s_ = small[:, o + 8 * tt:o + 8 * tt + 8]
            for hf, tk_ in enumerate(toks):
                c_ = slice(hf * 512, hf * 512 + 512)
                t = SC.do(lambda: sc.activation(junk_[:, tt, c_], xr[:, tt, c_], ACT.Square,
                                                accum_out=s_[:, hf:hf + 1]), tk_, loose=True)
            V.do(lambda: v.tensor_scalar(s_[:, 2:3], s_[:, 0:1], s_[:, 1:2], 1.0 / D, ALU.add, ALU.mult), t)
            t = SC.do(lambda: sc.activation(s_[:, 3:4], s_[:, 2:3], ACT.Sqrt, bias=small[:, 64:65]), V.last, t_eps)
            V.do(lambda: v.reciprocal(s_[:, 4:5], s_[:, 3:4]), t)
            if on_act:
                return SC.do(lambda: sc.mul(dst[:, tt, :], xr[:, tt, :], s_[:, 4:5]), V.last)
            if gain is None:
                return V.do(lambda: v.tensor_scalar(dst[:, tt, :], xr[:, tt, :], s_[:, 4:5], None, ALU.mult))
            return V.do(lambda: v.scalar_tensor_tensor(dst[:, tt, :], xr[:, tt, :], s_[:, 4:5], gain, ALU.mult,
                                                       ALU.mult))

        def rows_T(src, tt, toks, scale=None, bias=None, pool="misc"):
            r = {}
            for g in range(2):
                b = bank(pool)
                for q in range(4):
                    k = 4 * g + q
                    t = tr(banks[b][:, q * 128:(q + 1) * 128], src[:, tt, k * 128:(k + 1) * 128], *toks, t_K,
                           *drained[b])
                for q in range(4):
                    k = 4 * g + q
                    i_, o_ = banks[b][:, q * 128:(q + 1) * 128], hT[:, k, tt * 128:(tt + 1) * 128]
                    if scale is None:
                        if q:
                            continue
                        i_ = banks[b][:].rearrange("p (a b) -> p a b", a=4)
                        o_ = hT[:, 4 * g:4 * g + 4, tt * 128:(tt + 1) * 128]
                        f = (lambda: sc.copy(o_, i_)) if g else (lambda: v.tensor_copy(o_, i_))
                    elif g:
                        f = lambda: sc.activation(o_, i_, ACT.Identity, bias=bias(k) if bias else 0.0, scale=scale(k))
                    elif bias is None:
                        f = lambda: v.tensor_scalar(o_, i_, scale(k), None, ALU.mult)
                    else:
                        f = lambda: v.tensor_scalar(o_, i_, scale(k), bias(k), ALU.mult, ALU.add)
                    r[g] = (SC if g else V).do(f, t, loose=True)
                drained[b] = (r[g],)
            return r[0], r[1]

        tm2 = []

        mods = [mod_T(i, 4 * i) for i in range(4)]
        next(mods[0])
        next(mods[1])
        t_xn = [rms_rows(tt, xn, None, 66, xn, t_x, t_x, on_act=True) for tt in range(2)]
        next(mods[0])
        next(mods[2])
        next(mods[1])
        t_tr = []
        for m_ in range(4):
            for e in range(2):
                for tt in range(2):
                    k = 2 * m_ + e
                    t = tr(banks[m_][:, e * S + tt * 128:e * S + (tt + 1) * 128], xn[:, tt, k * 128:(k + 1) * 128],
                           t_K, t_xn[tt])
            t_tr.append(t)
        next(mods[3])
        next(mods[2])
        next(mods[3])
        tm2 = []
        tg = V.do(lambda: v.scalar_tensor_tensor(small[:, 8:16], modT[:, 8:16], 1.0, cols[:, C_GMIX:C_GMIX + 8],
                                                 ALU.add, ALU.mult))
        for m_ in range(4):
            for e in range(2):
                k = 2 * m_ + e
                o_, i_ = hT[:, k, :], banks[m_][:, e * S:(e + 1) * S]
                sc_, bi_ = small[:, 8 + k:9 + k], modT[:, k:k + 1]
                if m_ % 2:
                    te_ = SC.do(lambda: sc.activation(o_, i_, ACT.Identity, bias=bi_, scale=sc_), t_tr[m_], tg,
                                loose=True)
                else:
                    te_ = V.do(lambda: v.tensor_scalar(o_, i_, sc_, bi_, ALU.mult, ALU.add), t_tr[m_], tg,
                               loose=True)
            drained[m_] = (te_,)
        PE.wait(drained[2][0])
        hl = te_
        t_K2 = load("K", K[:, 128:N_K], A["K"][:, 128:N_K], t_one)
        t_rowa = load("rowa", rowa[:], A["rowa"].broadcast_to([P, N_ROWA]), hl)
        t_gtb = load("gtb", gt[:].rearrange("p a b -> p (a b)"), A["adab_g"].broadcast_to([P, 2 * D]), hl)

        def gemm_T(w, chunk, o, *tokens):
            return mm(o, [(w[:, k * 512 + chunk * 128:k * 512 + chunk * 128 + 128], hT[:, k, :]) for k in range(8)],
                      *tokens)

        def gemm_rows(w, tt, o, n0, n, *tokens):
            return mm(o, [(hT[:, k, tt * 128:(tt + 1) * 128], w[:, k * 512 + n0:k * 512 + n0 + n]) for k in range(8)],
                      *tokens)

        pc = area(6, S)
        uB = area(2, S)
        vB = area(2, S)
        pa = area(7, 257)
        uD = area(2, S)
        gb = area(2, 2, D)
        V.do(lambda: v.memset(pa[:, :, 0:1], 0.0))
        dest = {**{c: pa[:, c, 1:257] for c in range(7)}, 7: uD[:, 0, :], 8: uD[:, 1, :], 9: uB[:, 0, :],
                12: uB[:, 1, :], **{13 + i: pc[:, i, :] for i in range(6)}}
        tp = {}

        def p_tile(i):
            w, tw, r = tile("wp", i)
            chunks = [c for c in range(4 * i, min(4 * i + 4, 19)) if c != 11]

            def piece(c):
                b = bank("main")
                if c == 10:
                    for tt in range(2):
                        t = gemm_rows(w, tt, banks[b][:, tt * S:(tt + 1) * S], 256, 256, tw, hl, *drained[b])
                    te_ = SC.do(lambda: sc.activation(vB.rearrange("p a b -> p (a b)"), banks[b][:],
                                                      ACT.Gelu_apprx_tanh), t)
                else:
                    t = gemm_T(w, c - 4 * i, banks[b][:, 0:S], tw, hl, *drained[b])
                    if c in (9, 12):
                        te_ = SC.do(lambda: sc.activation(dest[c], banks[b][:, 0:S], ACT.Gelu_apprx_tanh), t)
                    elif c % 2 or c > 6:
                        te_ = SC.do(lambda: sc.copy(dest[c], banks[b][:, 0:S]), t)
                    else:
                        te_ = V.do(lambda: v.tensor_copy(dest[c], banks[b][:, 0:S]), t)
                tp[c] = te_
                drained[b] = (te_,)
                if c == chunks[-1]:
                    done(r, t)
            return [lambda c=c: piece(c) for c in chunks]

        gtok = {}

        def gate_tile(g, slot, *tokens):
            w, tw, r = tile("gates", g)

            open_ = {}

            def piece(tt, part):
                if part == 0:
                    open_[tt] = bank("main")
                b = open_[tt]
                for k in range(4 * part, 4 * part + 4):
                    t = PE.do(lambda: te.matmul(banks[b][:], hT[:, k, tt * 128:(tt + 1) * 128],
                                                w[:, k * 512:(k + 1) * 512], start=(k == 0), stop=(k == 7)),
                              *((tw, hl) + tuple(drained[b]) if k == 0 else ()), count=(k == 7))
                if part == 0:
                    return
                o = gb[:, slot, tt, (g % 2) * 512:(g % 2) * 512 + 512]
                te_ = SC.do(lambda: sc.activation(o, banks[b][:], ACT.Sigmoid), t, *tokens)
                drained[b] = (te_,)
                gtok.setdefault(g, []).append(te_)
                if tt:
                    done(r, t)
            return [lambda tt=tt, part=part: piece(tt, part) for tt in range(2) for part in range(2)]

        mt = {}

        def merge(br, slot, zT, toff, w, w0, tw, tz, first):
            for tt in range(2):
                for hf in range(2):
                    b = bank("main")
                    t = mm(banks[b][:], [(zT[:, c, toff + tt * 128:toff + (tt + 1) * 128],
                                          w[:, w0 + c * D + hf * 512:w0 + c * D + hf * 512 + 512]) for c in range(2)],
                           tw, *tz, *drained[b])
                    gsl = gb[:, slot, tt, hf * 512:(hf + 1) * 512]
                    m = merged[:, tt, hf * 512:(hf + 1) * 512]
                    tg = gtok[2 * br + hf][tt]
                    if first:
                        te_ = V.do(lambda b=b, g=gsl, m=m: v.tensor_tensor(m, g, banks[b][:], ALU.mult), t, tg)
                        drained[b] = (te_,)
                    else:
                        te_ = V.do(lambda b=b, g=gsl: v.tensor_tensor(g, g, banks[b][:], ALU.mult), t, tg)
                        drained[b] = (te_,)
                        te_ = G.do(lambda g=gsl, m=m: gp.tensor_tensor(m, m, g, ALU.add), te_, mt[(tt, hf)])
                    mt[(tt, hf)] = te_
            return t

        bc4 = lambda m: m.unsqueeze(1).broadcast_to([P, 4, P])
        f4 = lambda a: a.rearrange("p a b -> p (a b)")
        mark = top[0]
        zc = area(2, 258)
        yc = area(2, S)
        vln = area(2, S)
        zB = area(2, S)
        bnb = area(6)
        wsT = area(4, 128)
        bsT = area(2, 128)
        t_ws = load("ws", wsT, A["ws"], hl)
        t_bs = load("bs", bsT, A["bs"], hl)
        tws = G.do(lambda: gp.tensor_tensor(wsT, wsT, bc4(iu), ALU.mult), t_ws, t_K2)
        tbc = {}

        def branch_c():
            V.do(lambda: v.memset(zc[:, :, 0:2], 0.0))
            V.do(lambda: v.tensor_tensor(zc[:, :, 2:258], pc[:, 2:4, :], pc[:, 4:6, :], ALU.mult),
                 *[tp[c] for c in range(13, 19)])
            yield
            for c in range(2):
                for j in range(3):
                    cw = cols[:, C_CONV + 2 * j + c:C_CONV + 2 * j + c + 1]
                    if j == 0:
                        V.do(lambda: v.tensor_scalar(yc[:, c, :], zc[:, c, 0:S], cw, None, ALU.mult))
                    else:
                        V.do(lambda: v.scalar_tensor_tensor(yc[:, c, :], zc[:, c, j:j + S], cw, yc[:, c, :],
                                                            ALU.mult, ALU.add))
            tbc["c"] = V.do(lambda: v.tensor_tensor(yc, yc, pc[:, 0:2, :], ALU.mult))
            yield

        def branch_b():
            V.wait(tp[10])
            for tt in range(2):
                V.do(lambda: v.bn_stats(bnb, vB[:, tt, :]))
                V.do(lambda: v.bn_aggr(small[:, 20 + 2 * tt:22 + 2 * tt], bnb))
            mv = small[:, 20:24].rearrange("p (a b) -> p a b", b=2)
            V.do(lambda: v.tensor_scalar(small[:, 24:26].unsqueeze(2), mv[:, :, 1:2], 1e-5, None, ALU.add))
            ts_ = SC.do(lambda: sc.activation(small[:, 26:28], small[:, 24:26], ACT.Sqrt), V.last)
            yield
            V.do(lambda: v.reciprocal(small[:, 28:30], small[:, 26:28]), ts_)
            for tt in range(2):
                V.do(lambda: v.tensor_scalar(vln[:, tt, :], vB[:, tt, :], small[:, 20 + 2 * tt:21 + 2 * tt],
                                             small[:, 28 + tt:29 + tt], ALU.subtract, ALU.mult))
            V.do(lambda: v.tensor_tensor(vln, vln, rowa[:, R_SGW:R_SGW + 256].unsqueeze(1).broadcast_to([P, 2, S]),
                                         ALU.mult), t_rowa)
            t_vln = V.do(lambda: v.tensor_tensor(vln, vln, rowa[:, R_SGB:R_SGB + 256].unsqueeze(1)
                                                 .broadcast_to([P, 2, S]), ALU.add))
            yield
            bs_ = []
            for pr in range(2):
                b = bank("misc")
                for n in range(2):
                    t = mm(banks[b][:, n * S:(n + 1) * S],
                           [(vln[:, n, pr * 128:(pr + 1) * 128], wsT[:, 2 * pr:2 * pr + 2, :])], t_vln, tws,
                           *drained[b])
                bs_.append((b, t))
            for pr, (b, t) in enumerate(bs_):
                for g in range(2):
                    pv = banks[b][64 * g:64 * g + 64, :].rearrange("p (n g t) -> p n g t", n=2, g=2)[:, :, g, :]
                    o = zB[64 * g:64 * g + 64, pr, :].rearrange("p (n t) -> p n t", n=2)
                    bsv = bsT[64 * g:64 * g + 64, pr, :].unsqueeze(1).broadcast_to([64, 2, P])
                    te_ = V.do(lambda: v.tensor_tensor(o, pv, bsv, ALU.add), t, t_bs)
                drained[b] = (te_,)
            tbc["b"] = V.do(lambda: v.tensor_tensor(zB, zB, uB, ALU.mult), tp[9], tp[12])
            yield

        sp = area(14, 8)
        pw = area(8, 3, 8)
        wB = [area(2, 2, 128) for _ in range(2)]
        wC = [area(2, 2, 128)]
        xa = area(2, 2, S)
        xb = area(2, 2, S)
        yD = area(2, S)
        tD = {}
        semB, semC = (sem("s5b0"), sem("s5b1")), (sem("s5c"),)

        def s5():
            def loadw(dst, name, n, sm_, *tokens):
                for i in range(2):
                    src = A[name][2 * (n // 2) + i][:, 2 * (n % 2):2 * (n % 2) + 2, :]
                    m = len(dst)
                    t = SP.dma(lambda: nc.sync.dma_start(dst[n % m][:, i, :, :], src), sm_[n % m],
                               32 * (n // m) + 16 * i + 16, *tokens)
                return t

            tB = [loadw(wB, "s5b", n, semB, hl) for n in range(2)]
            tC = loadw(wC, "s5c", 0, semC, hl)
            yield
            lre, lim, dt_, mag, abr, abi, qr, qi = (sp[:, i, :] for i in range(8))
            s1, s2, s3, s4, s5_, nqi = (sp[:, i, :] for i in range(8, 14))
            V.do(lambda: v.tensor_scalar(lre, cols[:, C_ARE:C_ARE + 8], -1e-4, None, ALU.min))
            V.do(lambda: v.tensor_copy(lim, cols[:, C_AIM:C_AIM + 8]))
            t = SC.do(lambda: sc.activation(dt_, cols[:, C_DT:C_DT + 8], ACT.Exp))
            V.do(lambda: v.tensor_tensor(s1, lre, dt_, ALU.mult), t)
            t = SC.do(lambda: sc.activation(mag, s1, ACT.Exp), V.last)
            yield
            V.do(lambda: v.tensor_tensor(s1, lim, dt_, ALU.mult), t)
            BIG = 12582912.0
            V.do(lambda: v.tensor_scalar(s2, s1, float(np.float32(1 / (2 * np.pi))), BIG, ALU.mult, ALU.add))
            V.do(lambda: v.tensor_scalar(s2, s2, -BIG, None, ALU.add))
            for cst in (6.28125, 0.0019350051879882812, 3.0199159819567e-07):
                V.do(lambda: v.scalar_tensor_tensor(s1, s2, -cst, s1, ALU.mult, ALU.add))
            V.do(lambda: v.tensor_scalar(s1, s1, 3.1415925, -3.1415925, ALU.min, ALU.max))
            V.do(lambda: v.tensor_scalar(s3, s1, 0.5, None, ALU.mult))
            SC.do(lambda: sc.activation(s4, s1, ACT.Sin), V.last)
            t = SC.do(lambda: sc.activation(s5_, s3, ACT.Sin))
            yield
            V.do(lambda: v.tensor_tensor(s5_, s5_, s5_, ALU.mult), t)
            V.do(lambda: v.tensor_scalar(s5_, s5_, -2.0, 1.0, ALU.mult, ALU.add))
            V.do(lambda: v.tensor_tensor(abr, mag, s5_, ALU.mult))
            V.do(lambda: v.tensor_tensor(abi, mag, s4, ALU.mult))
            V.do(lambda: v.tensor_tensor(s1, lre, lre, ALU.mult))
            V.do(lambda: v.tensor_tensor(s2, lim, lim, ALU.mult))
            V.do(lambda: v.tensor_tensor(s1, s1, s2, ALU.add))
            V.do(lambda: v.reciprocal(s1, s1))
            V.do(lambda: v.tensor_scalar(s2, abr, -1.0, None, ALU.add))
            V.do(lambda: v.tensor_tensor(s3, s2, lre, ALU.mult))
            V.do(lambda: v.tensor_tensor(s4, abi, lim, ALU.mult))
            V.do(lambda: v.tensor_tensor(s3, s3, s4, ALU.add))
            V.do(lambda: v.tensor_tensor(qr, s3, s1, ALU.mult))
            V.do(lambda: v.tensor_tensor(s3, abi, lre, ALU.mult))
            V.do(lambda: v.tensor_tensor(s4, s2, lim, ALU.mult))
            V.do(lambda: v.tensor_tensor(s3, s3, s4, ALU.subtract))
            V.do(lambda: v.tensor_tensor(qi, s3, s1, ALU.mult))
            V.do(lambda: v.tensor_scalar(nqi, qi, -1.0, None, ALU.mult))

            t_y = tcp_ = None
            V.do(lambda: v.tensor_copy(pw[:, 0, 0, :], abr))
            V.do(lambda: v.tensor_copy(pw[:, 0, 1, :], abi))
            V.do(lambda: v.tensor_scalar(pw[:, 0, 2, :], abi, -1.0, None, ALU.mult))
            for lv in range(1, 8):
                p0, p1 = pw[:, lv - 1, 0, :], pw[:, lv - 1, 1, :]
                V.do(lambda: v.tensor_tensor(s1, p0, p0, ALU.mult))
                V.do(lambda: v.tensor_tensor(s2, p1, p1, ALU.mult), loose=True)
                V.do(lambda: v.tensor_tensor(s3, p0, p1, ALU.mult), loose=True)
                V.do(lambda: v.tensor_tensor(pw[:, lv, 0, :], s1, s2, ALU.subtract))
                V.do(lambda: v.tensor_scalar(pw[:, lv, 1, :], s3, 2.0, None, ALU.mult), loose=True)
                t_pw = V.do(lambda: v.tensor_scalar(pw[:, lv, 2, :], s3, -2.0, None, ALU.mult), loose=True)
            V.wait(t_pw)

            def b_times_u(n):
                bq = []
                for q in range(2):
                    b = bank("s5")
                    for i in range(2):
                        t = mm(banks[b][:, i * S:(i + 1) * S], [(wB[n % 2][:, i, q, :], uD[:, n // 2, :])], tB[n % 2],
                               tp[7], tp[8], *drained[b])
                    bq.append((b, t))
                if n < 2:
                    tB[n] = loadw(wB, "s5b", n + 2, semB, t)
                return bq

            def add_y(n, b, t):
                hf = n // 2
                if n % 2 == 0:
                    V.do(lambda: v.scalar_tensor_tensor(yD[:, hf, :], uD[:, hf, :],
                                                        cols[:, C_SD + hf:C_SD + hf + 1], banks[b][:, 0:S],
                                                        ALU.mult, ALU.add), t)
                else:
                    V.do(lambda: v.tensor_tensor(yD[:, hf, :], yD[:, hf, :], banks[b][:, 0:S], ALU.add), t)
                te_ = V.do(lambda: v.tensor_tensor(yD[:, hf, :], yD[:, hf, :], banks[b][:, S:2 * S], ALU.subtract))
                drained[b] = (te_,)
                return te_

            bq = b_times_u(0)
            yield
            out_ = None
            for n in range(4):
                src, dst = (xa, xb) if n % 2 == 0 else (xb, xa)
                for q, (b, t) in enumerate(bq):
                    j = 2 * n + q
                    for i in range(2):
                        s_a = (qr if i == 0 else qi)[:, j:j + 1]
                        s_b = (nqi if i == 0 else qr)[:, j:j + 1]
                        te1 = SC.do(lambda: sc.mul(src[:, i, q, :], banks[b][:, 0:S], s_a), t, V.last)
                        te_ = V.do(lambda: v.scalar_tensor_tensor(src[:, i, q, :], banks[b][:, S:2 * S], s_b,
                                                                  src[:, i, q, :], ALU.mult, ALU.add), te1)
                    drained[b] = (te_, te1)
                yield
                tv_ = V.last
                for lv in range(8):
                    s_ = 1 << lv
                    m = S - s_
                    pr_, pi_, npi = (pw[:, lv, j, 2 * n:2 * n + 2] for j in range(3))
                    tc_ = SC.do(lambda: sc.copy(dst[:, :, :, 0:s_], src[:, :, :, 0:s_]), tv_, t_y)
                    first = {}
                    for i in range(2):
                        for q in range(2):
                            first[(i, q)] = V.do(lambda: v.scalar_tensor_tensor(
                                dst[:, i, q, s_:S], src[:, i, q, 0:m], pr_[:, q:q + 1], src[:, i, q, s_:S], ALU.mult,
                                ALU.add), tv_, tcp_, t_y, loose=True)
                    for i in range(2):
                        for q in range(2):
                            b_ = npi if i == 0 else pi_
                            tv_ = V.do(lambda: v.scalar_tensor_tensor(
                                dst[:, i, q, s_:S], src[:, 1 - i, q, 0:m], b_[:, q:q + 1], dst[:, i, q, s_:S],
                                ALU.mult, ALU.add), first[(i, q)], loose=True)
                    tcp_ = tc_
                    src, dst = dst, src
                    yield
                    if lv == 0 and out_:
                        add_y(*out_)
                    if lv == 4 and n < 3:
                        bq = b_times_u(n + 1)
                b = bank("s5")
                for i in range(2):
                    t = mm(banks[b][:, i * S:(i + 1) * S], [(wC[0][:, i, q, :], src[:, i, q, :]) for q in range(2)], tC,
                           tv_, tcp_, *drained[b])
                if n < 3:
                    tC = loadw(wC, "s5c", n + 1, semC, t)
                t_y = t
                out_ = n, b, t
            yield
            te_ = add_y(*out_)
            tD["y"] = SC.do(lambda: sc.activation(f4(yD), f4(yD), ACT.Gelu_apprx_tanh), te_)
            yield

        L = area(2, S)
        keep, top[0] = top[0], base2
        MT, Mrb, Mrk, MoB, Mak = (area(4, 128) for _ in range(5))
        top[0] = keep
        Dm, DT, MoA = (area(4, 128) for _ in range(3))
        bn8 = area(8, 6)
        ps = area(7, S)
        lw = area(2, S)
        Wp = area(2, S)
        aa = area(2, S)
        gr = area(2, S)
        kk = area(2, S)
        tmp = area(2, S)
        vr = area(2, S)
        am = area(2, 2, S)
        oo = tmp
        Xs = f4(lw).rearrange("p (a b) -> p a b", a=4)
        U = Wp[:, 0, :].rearrange("p (a b) -> p a b", a=4)
        St = Wp[:, 1, :].rearrange("p (a b) -> p a b", a=2)
        rm = xn.rearrange("p a b -> p (a b)")[:, 0:1024].rearrange("p (a b c) -> p a b c", a=2, b=2)
        W6 = xn.rearrange("p a b -> p (a b)")[:, 1024:1792]
        t_w6 = load("w6", W6, A["w6"], hl)
        t_wf = load("wf", wf[:].rearrange("p a b -> p (a b)"), A["wf"], hl)
        zA = kk
        tA_ = {}

        def rwkv():
            a6 = ps[:, 6, :]
            V.do(lambda: v.tensor_tensor(ps, pa[:, :, 0:S], pa[:, :, 1:257], ALU.subtract),
                 *[tp[c] for c in range(7)])
            t0 = V.last
            for c in range(7):
                V.do(lambda: v.scalar_tensor_tensor(ps[:, c, :], ps[:, c, :], cols[:, C_MU + c:C_MU + c + 1],
                                                    pa[:, c, 1:257], ALU.mult, ALU.add), t0, loose=True)
            t_ps = V.last
            V.wait(t_ps)
            rT, kT, vT = ps[:, 0:2, :], ps[:, 2:4, :], ps[:, 4:6, :]
            SC.do(lambda: sc.activation(a6[0:32, :], a6[0:32, :], ACT.Tanh), t_ps)
            t_a6 = SC.do(lambda: sc.activation(a6[64:128, :], a6[64:128, :], ACT.Sigmoid))
            yield
            b = bank("misc")
            for tt in range(2):
                for c in range(2):
                    t = tr(banks[b][:, tt * S + c * 128:tt * S + (c + 1) * 128], vT[:, c, tt * 128:(tt + 1) * 128],
                           t_ps, *drained[b])
            t_vr = SC.do(lambda: sc.copy(f4(vr), banks[b][:]), t)
            drained[b] = (t_vr,)
            b1, b2, b3 = bank("misc"), bank("misc"), bank("misc")
            for c in range(2):
                t1 = mm(banks[b1][:, c * S:(c + 1) * S], [(W6[:, c * 128:(c + 1) * 128], a6)], t_a6, t_w6,
                        *drained[b1])
            for c in range(2):
                t2 = mm(banks[b2][:, c * S:(c + 1) * S], [(W6[:, 256 + c * 128:256 + (c + 1) * 128], a6)],
                        *drained[b2])
            for tt in range(2):
                t3 = mm(banks[b3][:, tt * S:(tt + 1) * S], [(a6[:, tt * 128:(tt + 1) * 128], W6[:, 512:768])],
                        *drained[b3])
            for c in range(2):
                t_lw = SC.do(lambda: sc.activation(lw[:, c, :], banks[b1][:, c * S:(c + 1) * S], ACT.Sigmoid,
                                                   bias=cols[:, C_W0 + c:C_W0 + c + 1]), t1)
            drained[b1] = (t_lw,)
            for c in range(2):
                t_aa = SC.do(lambda: sc.activation(aa[:, c, :], banks[b2][:, c * S:(c + 1) * S], ACT.Sigmoid,
                                                   bias=cols[:, C_A0 + c:C_A0 + c + 1]), t2)
            drained[b2] = (t_aa,)
            t_gr = SC.do(lambda: sc.copy(f4(gr), banks[b3][:]), t3)
            drained[b3] = (t_gr,)
            for c in range(2):
                V.do(lambda: v.tensor_scalar(kk[:, c, :], kT[:, c, :], cols[:, C_KK + c:C_KK + c + 1], None,
                                             ALU.mult))
            t = V.do(lambda: v.tensor_tensor(tmp, kk, kk, ALU.mult))
            yield
            b = bank("misc")
            t = mm(banks[b][:], [(blk, tmp)], t, *drained[b])
            tf = f4(tmp)
            te_ = SC.do(lambda: sc.activation(tf, banks[b][:], ACT.Sqrt), t)
            drained[b] = (te_,)
            V.do(lambda: v.tensor_scalar(lw, lw, -float(np.exp(-0.5)), None, ALU.mult), t_lw)
            t0 = V.last
            for c in range(2):
                for tt in range(2):
                    sl_ = slice(tt * 128, (tt + 1) * 128)
                    V.do(lambda: v.tensor_tensor_scan(L[:, c, sl_], ones[:], lw[:, c, sl_], 0.0, ALU.mult, ALU.add),
                         t0, loose=True)
            em = small[:, 40:48]
            L4 = L.rearrange("p c (a t) -> p (c a) t", t=128)
            V.do(lambda: v.tensor_copy(em[:, 0:4].unsqueeze(2), L4[:, :, 63:64]))
            V.do(lambda: v.tensor_tensor(em[:, 4:8].unsqueeze(2), L4[:, :, 127:128], L4[:, :, 63:64], ALU.subtract))
            V.do(lambda: v.tensor_tensor(L4, L4, em[:, 0:4].unsqueeze(2).broadcast_to([P, 4, P]), ALU.subtract))
            V.do(lambda: v.tensor_tensor(Wp, L, lw, ALU.subtract))
            t_L = V.last
            SC.do(lambda: sc.activation(f4(Wp), f4(Wp), ACT.Exp), t_L)
            SC.do(lambda: sc.activation(f4(lw), f4(L), ACT.Exp))
            SC.do(lambda: sc.activation(f4(L), f4(L), ACT.Exp, scale=-1.0))
            t_W = SC.do(lambda: sc.activation(em, em, ACT.Exp))
            V.do(lambda: v.tensor_scalar(tf, tf, 1e-12, None, ALU.max), te_)
            V.do(lambda: v.reciprocal(tf, tf))
            V.do(lambda: v.tensor_tensor(kk, kk, tmp, ALU.mult))
            yield
            for c in range(2):
                V.do(lambda: v.tensor_scalar(tmp[:, c, :], aa[:, c, :], -1.0, cols[:, C_KA + c:C_KA + c + 1],
                                             ALU.add, ALU.mult), t_aa)
            V.do(lambda: v.scalar_tensor_tensor(kT, tmp, 1.0, kT, ALU.add, ALU.mult))
            for c in range(2):
                V.do(lambda: v.scalar_tensor_tensor(tmp[:, c, :], rT[:, c, :], cols[:, C_RK + c:C_RK + c + 1],
                                                    kT[:, c, :], ALU.mult, ALU.mult))
            tb_ = V.last
            bon = small[:, 32:40]
            b = bank("misc")
            for tt in range(2):
                for c in range(2):
                    t = mm(banks[b][:, 4 * tt + 2 * c:4 * tt + 2 * c + 2],
                           [(tmp[:, c, tt * 128:(tt + 1) * 128], hsel)], tb_, *drained[b])
            t_bon = SC.do(lambda: sc.copy(bon, banks[b][:, 0:8]), t)
            drained[b] = (t_bon,)
            pb4 = pa.rearrange("p a b -> p (a b)")
            at_, bt_ = (pb4[:, i * 512:(i + 1) * 512].rearrange("p (a b) -> p a b", a=2) for i in range(2))
            kt_ = pb4[:, 1024:1536].rearrange("p (a b) -> p a b", a=2)
            V.do(lambda: v.tensor_tensor(bt_, kk, aa, ALU.mult), t_W)
            V.do(lambda: v.tensor_tensor(bt_, bt_, L, ALU.mult))
            V.do(lambda: v.scalar_tensor_tensor(at_, kk, -1.0, Wp, ALU.mult, ALU.mult), loose=True)
            V.do(lambda: v.tensor_tensor(kt_, kT, L, ALU.mult), loose=True)
            V.do(lambda: v.tensor_tensor(rT, rT, lw, ALU.mult), loose=True)
            t_abkr = V.last
            for e in range(2):
                hs = K[:, K_HSEL + e:K_HSEL + e + 1]
                SC.do(lambda: sc.mul(am[:, e, :, :], at_, hs), t_abkr)
            for e in range(2):
                hs = K[:, K_HSEL + e:K_HSEL + e + 1]
                t_arm = SC.do(lambda: sc.mul(rm[:, e, :, :], rT, hs), t3)
            yield

            lev = lambda i: K[:, K_LEV + i * 128:K_LEV + (i + 1) * 128].unsqueeze(1).broadcast_to([P, 4, P])

            def head_mats(tt, lhs, rhs, dst, mask, *after):
                b = bank("misc")
                sl_ = slice(tt * 128, (tt + 1) * 128)
                for h in range(4):
                    t = mm(banks[b][:, h * 128:(h + 1) * 128], [(lhs[:, h // 2, sl_], rhs[:, h % 2, h // 2, sl_])],
                           t_arm, t_abkr, *drained[b])
                te_ = V.do(lambda: v.tensor_tensor(f4(dst), banks[b][:], bc4(mask), ALU.mult), t, *after,
                           loose=True)
                drained[b] = (te_,)
                return te_

            t_mats = t_gmo = None
            for tt in range(2):
                t_MT = head_mats(tt, bt_, am, MT, su, t_mats, t_gmo)
                Mo = (MoA, MoB)
                G.do(lambda: gp.tensor_tensor(MoA, MT, lev(0), ALU.mult), t_MT, t_mats)
                t_DT = G.do(lambda: gp.tensor_tensor(DT, MoA, bc4(ident), ALU.add))
                t_Mo = {1: G.do(lambda: gp.tensor_tensor(MoB, MT, lev(1), ALU.mult))}
                t_Mak = head_mats(tt, kt_, am, Mak, su, t_mats)
                t_Mrb = head_mats(tt, bt_, rm, Mrb, iu, t_mats)
                t_Mrk = head_mats(tt, kt_, rm, Mrk, iu, t_mats)
                yield
                b = bank("misc")
                for h in range(4):
                    t = tr(banks[b][:, h * 128:(h + 1) * 128], DT[:, h, :], t_DT, *drained[b])
                t_D = SC.do(lambda: sc.copy(f4(Dm), banks[b][:]), t)
                drained[b] = (t_D,)
                yield
                reads = {}
                for k in range(1, 7):
                    if k < 6:
                        t_Mo[k + 1] = G.do(lambda: gp.tensor_tensor(Mo[(k + 1) % 2], MT, lev(k + 1), ALU.mult),
                                           reads.get(k - 1))
                        t_gmo = t_Mo[k + 1]
                    bx = bank("misc")
                    for h in range(4):
                        t = mm(banks[bx][:, h * 128:(h + 1) * 128], [(Mo[k % 2][:, h, :], Dm[:, h, :])], t_Mo[k],
                               t_D, *drained[bx])
                    reads[k] = t
                    t_X = SC.do(lambda: sc.copy(f4(Xs), banks[bx][:]), t)
                    drained[bx] = (t_X,)
                    yield
                    by = bank("misc")
                    if k < 6:
                        for h in range(4):
                            t = mm(banks[by][:, h * 128:(h + 1) * 128], [(DT[:, h, :], Xs[:, h, :])], t_X, t_DT,
                                   *drained[by])
                        t_D = V.do(lambda: v.tensor_tensor(f4(Dm), f4(Dm), banks[by][:], ALU.add), t, t_D,
                                   loose=True)
                        drained[by] = (t_D,)
                        bz = bank("misc")
                    else:
                        bz = by
                    for h in range(4):
                        t = mm(banks[bz][:, h * 128:(h + 1) * 128], [(Xs[:, h, :], DT[:, h, :])], t_X, t_DT,
                               *drained[bz])
                    t_DT = V.do(lambda: v.tensor_tensor(f4(DT), f4(DT), banks[bz][:], ALU.add), t, t_DT, loose=True)
                    drained[bz] = (t_DT,)
                    yield
                sl_ = slice(tt * 128, (tt + 1) * 128)
                b = bank("misc")
                for h in range(4):
                    c, e = h // 2, h % 2
                    pairs = [(Mak[:, h, :], vr[:, tt, h * 64:h * 64 + 64])]
                    if tt:
                        pairs.append((am[:, e, c, sl_], St[:, c, e * 64:e * 64 + 64]))
                    t = mm(banks[b][:, h * 64:h * 64 + 64], pairs, t_Mak, t_vr, *([tS] if tt else []), *drained[b])
                Xv = f4(Xs)[:, 0:256]
                t_X = SC.do(lambda: sc.copy(Xv, banks[b][:, 0:256]), t)
                drained[b] = (t_X,)
                yield
                b = bank("misc")
                for h in range(4):
                    t = mm(banks[b][:, h * 64:h * 64 + 64], [(DT[:, h, :], Xv[:, h * 64:h * 64 + 64])], t_X, t_DT,
                           *drained[b])
                t_U = SC.do(lambda: sc.copy(f4(U), banks[b][:, 0:256]), t)
                drained[b] = (t_U,)
                if tt == 0:
                    b = bank("misc")
                    for i, src in enumerate((bt_, kt_)):
                        for c in range(2):
                            t = tr(banks[b][:, (i * 2 + c) * 128:(i * 2 + c + 1) * 128], src[:, c, 0:128], t_abkr,
                                   *drained[b])
                    bkr = f4(MoA)
                    t_r = SC.do(lambda: sc.copy(bkr, banks[b][:]), t)
                    drained[b] = (t_r,)
                yield
                b = bank("misc")
                for h in range(4):
                    c, e = h // 2, h % 2
                    pairs = [(Mrb[:, h, :], U[:, h, :]), (Mrk[:, h, :], vr[:, tt, h * 64:h * 64 + 64])]
                    if tt:
                        pairs.append((rm[:, e, c, sl_], St[:, c, e * 64:e * 64 + 64]))
                    t = mm(banks[b][:, h * 64:h * 64 + 64], pairs, t_U, t_Mrb, t_Mrk, *drained[b])
                t_o = SC.do(lambda: sc.copy(oo[:, tt, :], banks[b][:, 0:256]), t)
                drained[b] = (t_o,)
                if tt == 0:
                    b = bank("misc")
                    for c in range(2):
                        t = mm(banks[b][:, c * 128:(c + 1) * 128],
                               [(bkr[:, c * 128:(c + 1) * 128], f4(U)[:, c * 128:(c + 1) * 128]),
                                (bkr[:, 256 + c * 128:256 + (c + 1) * 128], vr[:, 0, c * 128:(c + 1) * 128])],
                               t_r, t_U, t_vr, *drained[b])
                    for c in range(2):
                        tS = V.do(lambda: v.tensor_scalar(St[:, c, :], banks[b][:, c * 128:(c + 1) * 128],
                                                          em[:, 4 + 2 * c:5 + 2 * c], em[:, 2 * c + 1:2 * c + 2],
                                                          ALU.mult, ALU.mult), t, t_W, loose=True)
                    drained[b] = (tS,)
                t_mats = t
                yield
            V.wait(t_o, tS)
            mvh = small[:, 48:64].rearrange("p (a b) -> p a b", b=2)
            for i in range(8):
                src = oo[:, i // 4, (i % 4) * 64:(i % 4 + 1) * 64]
                V.do(lambda: v.bn_stats(bn8[:, i, :], src), loose=True)
            for i in range(8):
                V.do(lambda: v.bn_aggr(mvh[:, i, :], bn8[:, i, :]), *([V.last] if i == 0 else []), loose=True)
            rs8 = small[:, 8:16]
            V.do(lambda: v.tensor_scalar(rs8.unsqueeze(2), mvh[:, :, 1:2], 64e-5, None, ALU.add))
            ts_ = SC.do(lambda: sc.activation(rs8, rs8, ACT.Sqrt), V.last)
            yield
            V.do(lambda: v.reciprocal(rs8, rs8), ts_)
            o8 = oo.rearrange("p a (h i) -> p (a h) i", h=4)
            V.do(lambda: v.tensor_tensor(o8, o8, mvh[:, :, 0:1].broadcast_to([P, 8, 64]), ALU.subtract))
            V.do(lambda: v.tensor_tensor(o8, o8, rs8.unsqueeze(2).broadcast_to([P, 8, 64]), ALU.mult))
            V.do(lambda: v.tensor_tensor(oo, oo, rowa[:, R_LNXW:R_LNXW + 256].unsqueeze(1).broadcast_to([P, 2, S]),
                                         ALU.mult), t_rowa)
            V.do(lambda: v.tensor_tensor(oo, oo, rowa[:, R_LNXB:R_LNXB + 256].unsqueeze(1).broadcast_to([P, 2, S]),
                                         ALU.add))
            yield
            vr8 = vr.rearrange("p a (h i) -> p (a h) i", h=4)
            V.do(lambda: v.tensor_tensor(vr8, vr8, bon.unsqueeze(2).broadcast_to([P, 8, 64]), ALU.mult), t_bon,
                 t_mats)
            V.do(lambda: v.tensor_tensor(oo, oo, vr, ALU.add))
            t = V.do(lambda: v.tensor_tensor(oo, oo, gr, ALU.mult), t_gr)
            yield
            b = bank("misc")
            for c in range(2):
                for tt in range(2):
                    t2 = tr(banks[b][:, c * S + tt * 128:c * S + (tt + 1) * 128], oo[:, tt, c * 128:(c + 1) * 128],
                            t, *drained[b])
            tA_["z"] = SC.do(lambda: sc.copy(f4(zA), banks[b][:]), t2)
            drained[b] = (tA_["z"],)
            yield

        POOLS.update({"main": (0, 1), "misc": (4, 5, 6), "s5": (2, 3, 7)})
        gen_a, gen_d, gen_b, gen_c = rwkv(), s5(), branch_b(), branch_c()

        def step(*gens):
            for g in gens:
                next(g, None)

        def weave(pieces, *gens):
            for f in pieces:
                f()
                step(*gens)

        after = iter(SCHEDULE)
        gens = {"a": gen_a, "b": gen_b, "c": gen_c, "d": gen_d}

        def weave_s(pieces):
            for f in pieces:
                f()
                for g_ in next(after):
                    next(gens[g_], None)

        weave_s(p_tile(0))
        for q_ in (V, SC, G, PE):
            q_.wait(t_K2)
        for i in range(1, 5):
            weave_s(p_tile(i))
        open_mod, gb_free, slot_of = [], (), {4: 0, 5: 0, 2: 1, 3: 1, 6: 0, 7: 0, 0: 1, 1: 1}
        for kind, i in PLAN:
            if kind == "ada":
                open_mod.append(mod_gt(i, 0, i - 4) if i < 6 else mod_T(i, 4 * i - 8))
                next(open_mod[-1])
            elif kind == "gates":
                if i in (6, 0):
                    weave_s(gate_tile(i, slot_of[i], *gb_free))
                else:
                    weave_s(gate_tile(i, slot_of[i]))
                for mod in open_mod:
                    next(mod)
                open_mod = []
            else:
                for g_ in (gen_b, gen_c):
                    for _ in g_:
                        pass
                w, tw, r = tile("o_ab")
                w2_, tw2, r2 = tile("o_c")
                weave_s([lambda: merge(2, 0, yc, 0, w2_, 0, tw2, (tbc["c"],), True),
                         lambda: merge(1, 1, zB, 0, w, 2048, tw, (tbc["b"],), False)])
                done(r, PE.last)
                done(r2, PE.last)
                gb_free = tuple(mt[k] for k in mt)
        for _ in gen_a:
            step(gen_d)
        mod = mod_T(8, 24)
        next(mod)
        w, tw, r = tile("o_ab")
        tA = merge(0, 1, zA, 0, w, 0, tw, (tA_["z"],), False)
        done(r, tA)
        next(mod)
        for _ in gen_d:
            pass
        POOLS.update({"main": (0, 1, 2, 3), "misc": (4, 5, 6, 7)})

        top[0] = mark
        sgm = area(D)

        def glu(w, tw, tt, hf):
            for part in (1, 0):
                b = bank("main")
                t = mm(banks[b][:], [(yD[:, c, tt * 128:(tt + 1) * 128],
                                      w[:, c * 2048 + part * D + hf * 512:
                                        c * 2048 + part * D + hf * 512 + 512]) for c in range(2)],
                       tw, tD["y"], *drained[b])
                if part == 1:
                    sg_ = sgm[:, 512 * hf:512 * hf + 512]
                    tsg = SC.do(lambda: sc.activation(sg_, banks[b][:], ACT.Sigmoid), t, V.last)
                    drained[b] = (tsg,)
            gsl = gb[:, 0, tt, hf * 512:(hf + 1) * 512]
            m = merged[:, tt, hf * 512:(hf + 1) * 512]
            te_ = V.do(lambda: v.tensor_tensor(sg_, sg_, banks[b][:], ALU.mult), t, tsg)
            drained[b] = (te_,)
            te_ = V.do(lambda: v.tensor_tensor(gsl, gsl, sg_, ALU.mult), gtok[6 + hf][tt])
            mt[(tt, hf)] = V.do(lambda: v.tensor_tensor(m, m, gsl, ALU.add), te_, mt[(tt, hf)])
            return t

        def out_rows(tiles, tt, hf, gate, toks):
            w, tw, r = tiles[hf]
            b = bank("main")
            t = mm(banks[b][:], [(hT[:, k, tt * 128:(tt + 1) * 128], w[:, k * 512:(k + 1) * 512]) for k in range(8)],
                   tw, *toks, *drained[b])
            if tt:
                done(r, t)
            return b, t

        def out_norm(tiles, z, tz, gate, gain, make, scale, bias, r_make, ready=None):
            for n, f in enumerate(make):
                if n == 3:
                    tT0 = rows_T(z, 0, (tz[(0, 0)], tz[(0, 1)]))
                t = f()
            done(r_make, t)
            t_sc = ready and ready()
            bt = [out_rows(tiles, 0, hf, gate, tT0) for hf in range(2)]
            tT1 = rows_T(z, 1, (tz[(1, 0)], tz[(1, 1)]))
            tx = [add_x(b, 0, hf, gate, t) for hf, (b, t) in enumerate(bt)]
            t_x0 = rms_rows(0, xn, gain, 66, xn, *tx)
            bt = [out_rows(tiles, 1, 0, gate, tT1)]
            SC.wait(t_sc)
            V.wait(t_sc)
            tH = rows_T(xn, 0, (t_x0,), scale, bias)
            bt.append(out_rows(tiles, 1, 1, gate, ()))
            tx = [add_x(b, 1, hf, gate, t) for hf, (b, t) in enumerate(bt)]
            return tH, rms_rows(1, xn, gain, 66, xn, *tx), tx[1]

        def add_x(b, tt, hf, gate, t):
            xs = xr[:, tt, hf * 512:(hf + 1) * 512]
            if gate is not None:
                js = junk[:, 0:512]
                V.do(lambda: v.tensor_tensor(js, gt[:, gate, hf * 512:(hf + 1) * 512], banks[b][:], ALU.mult), t,
                     m_tok["gt"])
                drained[b] = (V.last,)
                return V.do(lambda: v.tensor_tensor(xs, xs, js, ALU.add))
            te_ = V.do(lambda: v.tensor_tensor(xs, xs, banks[b][:], ALU.add), t)
            drained[b] = (te_,)
            return te_

        def split_gemm(w, tt, bs, *tokens):
            for c in range(4):
                o = banks[bs[c // 2]][:, (c % 2) * S + tt * 128:(c % 2) * S + tt * 128 + 128]
                t = mm(o, [(w[:, k * 512 + c * 128:k * 512 + c * 128 + 128], hT[:, k, tt * 128:(tt + 1) * 128])
                           for k in range(8)], *tokens, *drained[bs[c // 2]])
            return t

        mod9 = mod_T(9, 28)
        next(mod9)
        tile_glu = tile("glu")
        tiles = tile("w_o", 0), tile("w_o", 1)
        scale1, bias1 = lambda k: small[:, 8 + k:9 + k], lambda k: modT[:, 16 + k:17 + k]

        def ready():
            next(mod9)
            return V.do(lambda: v.scalar_tensor_tensor(small[:, 8:16], modT[:, 24:32], 1.0,
                                                       cols[:, C_GFFN:C_GFFN + 8], ALU.add, ALU.mult), *tm2)

        make = [lambda tt=tt, hf=hf: glu(*tile_glu[:2], tt, hf) for tt in range(2) for hf in range(2)]
        tT0, t_xn1, tx1 = out_norm(tiles, merged, mt, 0, None, make, scale1, bias1, tile_glu[2], ready)
        t_fg = load("fg", gt[:, 0, :], A["rowb"].broadcast_to([P, D]), tx1, q=SP)

        fT = area(2, 4, S)
        f_free = [(), ()]
        facc = [4, 5, 6, 7]
        t_f = {}

        def up(j):
            w, tw, r = tile("w1", j)
            for pr in range(2):
                b = bank("main")
                for c in range(2):
                    t = gemm_T(w, 2 * pr + c, banks[b][:, c * S:(c + 1) * S], tw, *drained[b])
                relu2_part(j, pr, b, t)
            done(r, t)

        def relu2_part(j, pr, b, t):
            o = fT[:, j % 2, 2 * pr:2 * pr + 2, :].rearrange("p a b -> p (a b)")
            te_ = SC.do(lambda: sc.activation(o, banks[b][:], ACT.Relu), t, *f_free[j % 2])
            drained[b] = (te_,)
            t_f.setdefault(j, []).append(G.do(lambda: gp.tensor_tensor(o, o, o, ALU.mult), te_))

        acc_t = {}

        def down(j):
            w, tw, r = tile("w2", j)
            for tt in range(2):
                for hf in range(2):
                    b = facc[2 * tt + hf]
                    for c in range(4):
                        first, last = j == 0 and c == 0, j == 7 and c == 3
                        l = fT[:, j % 2, c, tt * 128:(tt + 1) * 128]
                        rr = w[:, c * D + hf * 512:c * D + hf * 512 + 512]
                        t = PE.do(lambda b=b, l=l, rr=rr, first=first, last=last: te.matmul(
                            banks[b][:], l, rr, start=first, stop=last), tw, *t_f[j], *(drained[b] if first else ()))
                    acc_t[(tt, hf)] = t
            f_free[j % 2] = (t,)
            done(r, t)

        w, tw, r = tile("w1", 0)
        bs = bank("main"), bank("main")
        for tt in range(2):
            tT = rows_T(xn, 1, (t_xn1,), scale1, bias1) if tt else tT0
            t = split_gemm(w, tt, bs, tw, *tT)
        for pr in range(2):
            relu2_part(0, pr, bs[pr], t)
        done(r, t)
        mods = []
        for j in range(8):
            if j < 7:
                up(j + 1)
            down(j)
            for mod in mods:
                next(mod)
            mods = []
            if j in (1, 3):
                mods.append(mod_gt(10 + j // 2, 1, j // 2, "main"))
                next(mods[0])

        w0_, tw0_, r0_ = tile("qkv", 0)
        bs0 = None
        V.wait(t_fg)
        for tt in range(2):
            tx = [add_x(facc[2 * tt + hf], tt, hf, 1, acc_t[(tt, hf)]) for hf in range(2)]
            t_x1 = rms_rows(tt, xr, gt[:, 0, :], 66, xn, *tx)
            t_xn = rms_rows(tt, xn, None, 82, xn, t_x1, t_x1)
            if tt == 1:
                blk_end = (acc_t[(1, 1)], V.last, SC.last, G.last)
            tT = rows_T(xn, tt, (t_xn,), lambda k: cols[:, C_GMIX2 + k:C_GMIX2 + k + 1], pool="main")
            bs0 = bs0 or (bank("main"), bank("main"))
            t_q0 = split_gemm(w0_, tt, bs0, tw0_, *tT)
        done(r0_, t_q0)
        t_g2 = load("fg2", gt[:], A["rowb2"].broadcast_to([P, 2 * D]), V.last, q=SP)
        top[0] = base2
        qT_ = area(2, 4, S)
        kT2 = area(2, 4, S)
        vals = area(2, 2, 512)
        pexp = area(8, S)
        pT = area(2, 4, 128)
        yT = area(8, S)
        lf = area(2, 8)
        rot_t = area(S)
        ut = area(2, S)
        lbt = area(2, 8, 128)
        sg2 = area(4, 2, 512)
        for q_ in (V, SC, G):
            q_.wait(*blk_end)
        negm = K[:, K_ZN:K_ZN + S]
        keys = arena[:, ARENA - 2048:ARENA]
        assert top[0] <= ARENA - 2048
        t_keys = load("keys", keys, A["keys"][0], *blk_end, q=SP)

        def forget():
            b = bank("misc")
            for tt in range(2):
                t = mm(banks[b][:, tt * 8:tt * 8 + 8],
                       [(hT[:, k, tt * 128:(tt + 1) * 128], wf[:, k, :]) for k in range(8)], t_wf, hl, *drained[b])
            fx, fe = small[:, 16:32], small[:, 32:48]
            V.do(lambda: v.tensor_tensor(fx.rearrange("p (a b) -> p a b", a=2),
                                         banks[b][:, 0:16].rearrange("p (a b) -> p a b", a=2),
                                         rowa[:, R_BF:R_BF + 8].unsqueeze(1).broadcast_to([P, 2, 8]), ALU.add), t)
            drained[b] = (V.last,)
            V.do(lambda: v.tensor_scalar(fe, fx, -1.0, None, ALU.mult))
            V.do(lambda: v.tensor_tensor(fe, fx, fe, ALU.max))
            t = SC.do(lambda: sc.activation(fe, fe, ACT.Exp, scale=-1.0), V.last)
            t = SC.do(lambda: sc.activation(fe, fe, ACT.Ln, bias=1.0), t)
            yield
            lff = f4(lf)
            V.do(lambda: v.tensor_scalar(fx, fx, 0.0, None, ALU.min), t)
            t_lf = V.do(lambda: v.tensor_tensor(lff, fx, fe, ALU.subtract))
            nlf = cact[:, 0:16].rearrange("p (a b) -> p a b", a=2)
            t_nlf = V.do(lambda: v.tensor_scalar(cact[:, 0:16], lff, -1.0, None, ALU.mult))
            for s_ in range(2):
                for h in range(8):
                    tk["lb"] = G.do(lambda: gp.tensor_scalar(lbt[:, s_, h, :], ones[:], nlf[:, s_, h:h + 1], None,
                                                             ALU.mult), t_nlf, loose=True)
            V.do(lambda: v.tensor_copy(ut[:, 0, 0:128], iu), loose=True)
            V.do(lambda: v.tensor_copy(ut[:, 0, 128:256], ones[:]), loose=True)
            V.do(lambda: v.memset(ut[:, 1, 0:128], 0.0), loose=True)
            tk["ut"] = V.do(lambda: v.tensor_copy(ut[:, 1, 128:256], iu), loose=True)
            yield
            b = bank("misc")
            mm(banks[b][:, 0:8], [(iu, lf[:, 0, :])], t_lf, *drained[b])
            t = mm(banks[b][:, 8:16], [(ones[:], lf[:, 0, :]), (iu, lf[:, 1, :])])
            tk["cq"] = V.do(lambda: v.tensor_copy(small[:, 48:64], banks[b][:, 0:16]), t)
            drained[b] = (tk["cq"],)
            yield

        tk = {}

        def project_T(i, kind, dst, rope, scl):
            if i:
                w, tw, r = tile("qkv", i)
            wait_rot = []
            key = (kind, i % 3)
            tk[key] = []

            def rotate():
                for d_, t_ in wait_rot:
                    b2 = bank("misc")
                    t2 = mm(banks[b2][:, 0:S], [(rotm, d_)], t_, *drained[b2])
                    V.do(lambda: v.tensor_tensor(rot_t, banks[b2][:, 0:S], K[:, K_SIN:K_SIN + S], ALU.mult), t2)
                    drained[b2] = (V.last,)
                    V.do(lambda: v.tensor_tensor(d_, d_, K[:, K_COS:K_COS + S], ALU.mult), t_)
                    tk[key].append(V.do(lambda: v.tensor_tensor(d_, d_, rot_t, ALU.add)))
                del wait_rot[:]

            def piece(c):
                if i:
                    b = bank("main")
                    t = gemm_T(w, c, banks[b][:, 0:S], tw, hl, *drained[b])
                    i_ = banks[b][:, 0:S]
                else:
                    b, t = bs0[c // 2], t_q0
                    i_ = banks[b][:, (c % 2) * S:(c % 2 + 1) * S]
                d_ = dst[:, kind, c, :]
                te_ = SC.do(lambda: sc.mul(d_, i_, scl), t)
                drained[b] = (te_,)
                if rope:
                    rotate()
                    wait_rot.append((d_, te_))
                else:
                    tk[key].append(te_)
                if c == 3 and i:
                    done(r, t)
            return [lambda c=c: piece(c) for c in range(4)], rotate

        def project_rows(i, kind):
            w, tw, r = tile("qkv", i)
            tk[(kind, 2)] = []

            def piece(tt):
                b = bank("main")
                t = gemm_rows(w, tt, banks[b][:], 0, 512, tw, hl, *drained[b])
                te_ = SC.do(lambda: sc.copy(vals[:, kind, tt, :], banks[b][:]), t)
                drained[b] = (te_,)
                tk[(kind, 2)].append(te_)
                if tt:
                    done(r, t)
            return [lambda: piece(0), lambda: piece(1)]

        free = {"pexp": (), "pT": ()}
        pexp_ec = pexp.rearrange("p (e c) k -> p e c k", e=2)

        def attention(kind):
            tqk = tk[(kind, 0)] + tk[(kind, 1)]
            for qt in range(2):
                nk = 128 * (qt + 1)
                per = 4 // (qt + 1)
                for g in range(8 // per):
                    b = bank("misc")
                    for j in range(per):
                        p_ = per * g + j
                        e, c = p_ // 4, p_ % 4
                        pairs = [(qT_[64 * e:64 * e + 64, kind, c, qt * 128:(qt + 1) * 128],
                                  kT2[64 * e:64 * e + 64, kind, c, 0:nk])]
                        if kind:
                            pairs += [(lbt[:, s_, p_, :], ut[:, s_, 0:nk]) for s_ in range(qt + 1)]
                            extra_t = (tk["lb"], tk["ut"])
                        else:
                            extra_t = ()
                        t = mm(banks[b][:, j * nk:(j + 1) * nk], pairs, *tqk, *extra_t, *drained[b])
                    pe_ = pexp[:, per * g:per * g + per, 0:nk]
                    mask = negm[:, S - nk:S].unsqueeze(1).broadcast_to([P, per, nk])
                    te_ = V.do(lambda: v.tensor_tensor(pe_, banks[b][:].rearrange("p (a b) -> p a b", a=per), mask,
                                                       ALU.add), t, *free["pexp"])
                    drained[b] = (te_,)
                    V.do(lambda: v.tensor_reduce(small[:, per * g:per * g + per], pe_, X, ALU.max))
                    yield
                m_, nb_ = small[:, 0:8], small[:, 8:16]
                if kind:
                    cq = small[:, 48 + 8 * qt:56 + 8 * qt]
                    V.do(lambda: v.tensor_tensor(m_, m_, cq, ALU.add), tk["cq"])
                    t = V.do(lambda: v.tensor_tensor(nb_, cq, m_, ALU.subtract))
                else:
                    t = V.do(lambda: v.tensor_scalar(nb_, m_, -1.0, None, ALU.mult))
                tn = {}

                def exps(c):
                    for e in range(2):
                        p_ = 4 * e + c
                        tz = SC.do(lambda: sc.activation(pexp[:, p_, 0:nk], pexp[:, p_, 0:nk], ACT.Exp,
                                                         bias=small[:, 8 + p_:9 + p_],
                                                         accum_out=small[:, 16 + p_:17 + p_]), t, loose=True)
                    sums = small[:, 16:24].rearrange("p (e c) -> p e c", e=2)[:, :, c:c + 1]
                    inv = small[:, 24:32].rearrange("p (e c) -> p e c", e=2)[:, :, c:c + 1]
                    V.do(lambda: v.reciprocal(inv, sums), tz)
                    pv = pexp_ec[:, :, c, 0:nk]
                    tn[c] = V.do(lambda: v.tensor_tensor(pv, pv, inv.broadcast_to([P, 2, nk]), ALU.mult))

                exps(0)
                exps(1)
                yield
                pend = None
                for c in range(4):
                    b = bank("misc")
                    for kc in range(qt + 1):
                        for e in range(2):
                            t2 = tr(banks[b][:, (2 * kc + e) * 128:(2 * kc + e + 1) * 128],
                                    pexp[:, 4 * e + c, kc * 128:(kc + 1) * 128], tn[c], *drained[b])
                    pt = pT[:, c % 2, :, :].rearrange("p a b -> p (a b)")[:, 0:2 * nk]
                    tpt = SC.do(lambda: sc.copy(pt, banks[b][:, 0:2 * nk]), t2, *free["pT"])
                    drained[b] = (tpt,)
                    if c < 2:
                        exps(c + 2)
                    yield
                    b = bank("misc")
                    t3 = mm(banks[b][:, 0:256], [(vals[:, kind, kc, c * 128:(c + 1) * 128],
                                                  pt[:, kc * 256:(kc + 1) * 256]) for kc in range(qt + 1)], tpt,
                            *tk[(kind, 2)], *drained[b])
                    free["pT"] = (pend,)
                    pend = t3
                    for e in range(2):
                        o = yT[64 * e:64 * e + 64, 4 * kind + c, qt * 128:(qt + 1) * 128]
                        te_ = V.do(lambda: v.tensor_copy(o, banks[b][64 * e:64 * e + 64,
                                                                     e * 128:(e + 1) * 128]), t3, loose=True)
                    drained[b] = (te_,)
                free["pexp"], free["pT"] = (t2,), (t3,)
                yield
            tk[("y", kind)] = te_

        gate_t = {}

        def gate2_tile(i):
            w, tw, r = tile("g2", i)
            open_ = {}

            def piece(tt, part):
                if part == 0:
                    open_[tt] = bank("main")
                b = open_[tt]
                for k in range(4 * part, 4 * part + 4):
                    t = PE.do(lambda: te.matmul(banks[b][:], hT[:, k, tt * 128:(tt + 1) * 128],
                                                w[:, k * 512:(k + 1) * 512], start=(k == 0), stop=(k == 7)),
                              *((tw, hl) + tuple(drained[b]) if k == 0 else ()), count=(k == 7))
                if part == 0:
                    return
                gate_t[(i, tt)] = SC.do(lambda: sc.activation(sg2[:, i, tt, :], banks[b][:], ACT.Sigmoid), t)
                drained[b] = (gate_t[(i, tt)],)
                if tt:
                    done(r, t)
            return [lambda tt=tt, part=part: piece(tt, part) for tt in range(2) for part in range(2)]

        mg = merged
        tk_m = {}

        def branch_out(kind):
            w, tw, r = tile("ba" if kind == 0 else "bb")

            def piece(tt, hf):
                b = bank("main")
                t = mm(banks[b][:], [(yT[:, 4 * kind + c, tt * 128:(tt + 1) * 128],
                                      w[:, c * D + hf * 512:c * D + hf * 512 + 512]) for c in range(4)],
                       tw, tk[("y", kind)], *drained[b])
                o = (mg, xn)[kind][:, tt, hf * 512:(hf + 1) * 512]
                gs = sg2[:, 2 * kind + hf, tt, :]
                te_ = V.do(lambda: v.tensor_tensor(o, gs, banks[b][:], ALU.mult), t, gate_t[(2 * kind + hf, tt)],
                           loose=True)
                drained[b] = (te_,)
                if kind:
                    m_ = mg[:, tt, hf * 512:(hf + 1) * 512]
                    te_ = V.do(lambda: v.tensor_tensor(m_, m_, o, ALU.add))
                tk_m[(tt, hf)] = te_
                return t
            return [lambda tt=tt, hf=hf: piece(tt, hf) for tt in range(2) for hf in range(2)], r

        gen_f = forget()
        pq_, rot = project_T(0, 0, qT_, True, 0.125)
        weave(pq_, gen_f)
        rot()
        pk_, rot = project_T(1, 0, kT2, True, 1.0)
        weave(pk_, gen_f)
        weave(project_rows(2, 0))
        rot()
        gen_0 = attention(0)
        weave(project_T(3, 1, qT_, False, 0.125)[0], gen_0)
        weave(project_T(4, 1, kT2, False, 1.0)[0], gen_0)
        weave(project_rows(5, 1), gen_0, gen_0)
        weave(gate2_tile(0), gen_0)
        weave(gate2_tile(1), gen_0)
        for _ in gen_0:
            pass
        gen_1 = attention(1)
        make, r_ba = branch_out(0)
        weave(make, gen_1)
        done(r_ba, PE.last)
        weave(gate2_tile(2), gen_1, gen_1)
        weave(gate2_tile(3), gen_1, gen_1)
        for _ in gen_1:
            pass
        V.wait(t_g2)
        make, r_bb = branch_out(1)
        quiet = (PE.last, V.last, SC.last, tk[("y", 1)])
        tiles = tile("wout", 0), tile("wout", 1)
        tT0, t_xn1, tx1 = out_norm(tiles, mg, tk_m, None, gt[:, 0, :], make, None, None, r_bb)
        top[0] = base2
        scr = area(2, 16, 128)
        qp = area(16, S)
        sv = area(2, 16)
        siu = area(2, 16)
        sif = area(2, 16)
        work = area(128)
        cand = area(16, 16)
        cw = area(256)
        best2 = area(2, 16)
        pku = area(16)
        pij = area(2, 16)
        eq = area(2, 256)
        e01 = area(2, 16)
        idx = area(2, 128)
        gat = area(2, 128)
        hv = area(2, 128)
        av = area(2, 128)
        inv = area(2, 8)
        sm2 = area(2, 8)
        diag = area(8, 128)
        early = [area(D) for _ in range((ARENA - 2048 - top[0]) // D)]
        iota = K[:, K_IOTA:K_IOTA + 16]
        U_ = lambda a: a.bitcast(U32)
        t_scr = {}
        POOLS.update({"main": (0, 1), "misc": (2, 3)})
        t_diag, t_acc = [()] * 8, {}

        def scores(tt, g, *tq):
            b = bank("misc")
            for j in range(4):
                hp = 4 * g + j
                t = mm(banks[b][:, j * 128:(j + 1) * 128],
                       [(qp[:, hp, tt * 128:(tt + 1) * 128], keys[:, hp * 128:(hp + 1) * 128])], *tq, t_keys,
                       *drained[b])
            o = scr[:, tt, 4 * g:4 * g + 4, :].rearrange("p a b -> p (a b)")
            te_ = SC.do(lambda: sc.copy(o, banks[b][:]), t, *quiet)
            drained[b] = (te_,)
            t_scr[(tt, g)] = te_

        t_idx = {}
        t_inv = {}
        t_exp = {}

        def choose(tt, h):
            V.wait(t_scr[(tt, h // 2)], t_exp.get((tt, h - 1)))
            best, sm = best2[:, tt, :], sm2[:, tt, :]
            for s_ in range(2):
                x_ = scr[:, tt, 2 * h + s_, :]
                V.do(lambda: v.max(sv[:, s_, 0:8], x_))
                V.do(lambda: v.max_index(U_(siu[:, s_, 0:8]), sv[:, s_, 0:8], x_))
                V.do(lambda: v.match_replace(work, sv[:, s_, 0:8], x_, -3.0e38))
                V.do(lambda: v.max(sv[:, s_, 8:16], work))
                V.do(lambda: v.max_index(U_(siu[:, s_, 8:16]), sv[:, s_, 8:16], work))
            V.do(lambda: v.tensor_copy(sif, U_(siu)))
            V.do(lambda: v.tensor_tensor(cand, sv[:, 0, :].unsqueeze(2).broadcast_to([P, 16, 16]),
                                         sv[:, 1, :].unsqueeze(1).broadcast_to([P, 16, 16]), ALU.add))
            cd = cand.rearrange("p a b -> p (a b)")
            V.do(lambda: v.max(best[:, 0:8], cd))
            V.do(lambda: v.max_index(U_(pku[:, 0:8]), best[:, 0:8], cd))
            V.do(lambda: v.match_replace(cw, best[:, 0:8], cd, -3.0e38))
            V.do(lambda: v.max(best[:, 8:16], cw))
            V.do(lambda: v.max_index(U_(pku[:, 8:16]), best[:, 8:16], cw))
            V.do(lambda: v.tensor_scalar(sm[:, 0:1], best[:, 0:1], -1.0, None, ALU.mult))
            o = slice(16 * h, 16 * h + 16)
            t = SC.do(lambda: sc.activation(gat[:, tt, o], best, ACT.Exp, bias=sm[:, 0:1],
                                            accum_out=sm[:, 1:2]), V.last)
            t_exp[(tt, h)] = t
            V.do(lambda: v.tensor_single_scalar(U_(pij[:, 0, :]), U_(pku), 4, ALU.logical_shift_right))
            V.do(lambda: v.tensor_single_scalar(U_(pij[:, 1, :]), U_(pku), 15, ALU.bitwise_and))
            V.do(lambda: v.tensor_copy(e01, U_(pij)))
            e3 = eq.rearrange("p s (k i) -> p (s k) i", i=16)
            e4 = eq.rearrange("p s (k i) -> p s k i", i=16)
            ef = e01.rearrange("p s k -> p (s k)")
            V.do(lambda: v.tensor_tensor(e3, ef.unsqueeze(2).broadcast_to([P, 32, 16]),
                                         iota.unsqueeze(1).broadcast_to([P, 32, 16]), ALU.is_equal))
            V.do(lambda: v.tensor_tensor(e4, e4, sif.unsqueeze(2).broadcast_to([P, 2, 16, 16]), ALU.mult))
            V.do(lambda: v.tensor_reduce(ef, e3, X, ALU.add))
            V.do(lambda: v.scalar_tensor_tensor(e01[:, 0, :], e01[:, 0, :], 128.0, e01[:, 1, :], ALU.mult, ALU.add))
            V.do(lambda: v.tensor_copy(U_(idx[:, tt, o]), e01[:, 0, :]))
            t_idx[(tt, h)] = V.last

        gsem, gcount, gfree, fifo = {}, {}, {}, []

        def more(which, *tokens):
            new = []
            for a_ in which:
                i = len(gsem)
                gsem[i], gcount[i], gfree[i], slot_ap[i] = sem(f"gather{i}"), 0, tokens, a_
                new.append(i)
            fifo[:0] = new

        slot_ap = {}
        more(early, *quiet)
        when = {}
        n_gather = [0]

        def gather(table, tt, e):
            if n_gather[0] in when:
                which, t = when[n_gather[0]]
                more(which, t)
            n_gather[0] += 1
            i = fifo.pop(0)
            fifo.append(i)
            gcount[i] += 16
            ap = U_(idx[:, tt, e:e + 1])
            return i, G.dma(lambda: gp.indirect_dma_start(slot_ap[i], None, table,
                                                          bass.IndirectOffsetOnAxis(ap=ap, axis=0)),
                            gsem[i], gcount[i], t_idx[(tt, e // 16)], *gfree[i])

        steps = [(tt, h) for h in range(8) for tt in range(2)]
        t_av = {}

        def phase_u(tt, h):
            for k in range(16):
                e = 16 * h + k
                i, tg = gather(A["eu"], tt, e)
                t = V.do(lambda: v.tensor_tensor_reduce(
                    out=slot_ap[i], in0=slot_ap[i], in1=xn[:, tt, :],
                    scale=1.0, scalar=0.0, op0=ALU.mult, op1=ALU.add,
                    accum_out=hv[:, tt, e:e + 1]), tg, loose=True)
                gfree[i] = (t,)
            o = slice(16 * h, 16 * h + 16)
            t_inv[(tt, h)] = V.do(lambda: v.reciprocal(inv[:, tt, h:h + 1], sm2[:, tt, 1:2]), t_exp[(tt, h)],
                                  loose=True)
            t_av[(tt, h)] = SC.do(lambda: sc.activation(av[:, tt, o], hv[:, tt, o], ACT.Gelu), t)

        accs = {}

        def phase_v(tt, h):
            n = steps.index((tt, h))
            on_dve = range(16) if n < 3 else range(0, 16, 2) if n > 13 else range(0, 16, 4)
            o = slice(16 * h, 16 * h + 16)
            V.do(lambda: v.tensor_tensor(av[:, tt, o], av[:, tt, o], gat[:, tt, o], ALU.mult), t_av[(tt, h)],
                 t_exp[(tt, h)])
            ta = V.do(lambda: v.tensor_scalar(av[:, tt, o], av[:, tt, o], inv[:, tt, h:h + 1], None, ALU.mult),
                      t_inv[(tt, h)])
            for k in range(16):
                e = 16 * h + k
                i, tg = gather(A["ev"], tt, e)
                if k % 16 in on_dve:
                    xs = xr[:, tt, :]
                    t = V.do(lambda: v.scalar_tensor_tensor(xs, slot_ap[i], av[:, tt, e:e + 1], xs, ALU.mult,
                                                            ALU.add), tg, ta, accs.get(tt), loose=True)
                    accs[tt] = t
                    gfree[i] = (t,)
                    continue
                d_ = diag[:, k % 8, :]
                td = SC.do(lambda: sc.mul(d_, ident, av[:, tt, e:e + 1]), ta, *t_diag[k % 8], loose=True)
                for hf in range(2):
                    b = 4 + 2 * tt + hf
                    t = PE.do(lambda: te.matmul(banks[b][:], d_, slot_ap[i][:, hf * 512:(hf + 1) * 512],
                                                start=((tt, hf) not in t_acc), stop=(e == 127)), td, tg,
                              *(drained[b] if (tt, hf) not in t_acc else ()))
                    t_acc[(tt, hf)] = t
                t_diag[k % 8] = gfree[i] = (t,)

        so = sem("out")

        def finish(tt):
            tx = []
            for hf in range(2):
                xs = xr[:, tt, hf * 512:(hf + 1) * 512]
                tx.append(V.do(lambda: v.tensor_tensor(xs, xs, banks[4 + 2 * tt + hf][:], ALU.add),
                               t_acc[(tt, hf)]))
            t_fin = rms_rows(tt, xn, gt[:, 1, :], 66, xn, *tx)
            SP.dma(lambda: nc.sync.dma_start(out[:, tt, :], xn[:, tt, :]), so, 16 * (tt + 1), t_fin)

        w, tw, r = tile("pq", 0)
        bs = bank("main"), bank("main")
        for tt in range(2):
            tT = rows_T(xn, 1, (t_xn1,)) if tt else tT0
            if tt:
                choose(*steps[0])
            t = split_gemm(w, tt, bs, tw, *tT)
            for pr in range(2):
                i_ = banks[bs[pr]][:].rearrange("p (a b) -> p a b", a=2)[:, :, tt * 128:(tt + 1) * 128]
                o = qp[:, 2 * pr:2 * pr + 2, tt * 128:(tt + 1) * 128]
                te_ = SC.do(lambda: sc.copy(o, i_), t, *quiet)
            drained[bs[0]] = drained[bs[1]] = (te_,)
            scores(tt, 0, te_)
        done(r, t)

        def queries(i):
            w, tw, r = tile("pq", i)
            for c in range(0, 4, 2):
                b = bank("main")
                for e in range(2):
                    t = gemm_T(w, c + e, banks[b][:, e * S:(e + 1) * S], tw, *drained[b])
                o = qp[:, 4 * i + c:4 * i + c + 2, :].rearrange("p a b -> p (a b)")
                te_ = SC.do(lambda: sc.copy(o, banks[b][:]), t)
                drained[b] = (te_,)
            done(r, t)
            for tt in range(2):
                scores(tt, i, te_)
            which = [ring[:, r, j * D:(j + 1) * D] for j in range(4)]
            if i == 3:
                which += [keys[:, 0:D], keys[:, D:2 * D]]
                which += [qp[:, 4 * j:4 * j + 4, :].rearrange("p a b -> p (a b)") for j in range(4)]
            when[n_gather[0] + 16] = (which, PE.last)

        for n, (tt, h) in enumerate(steps):
            if n < 3:
                queries(n + 1)
            if n + 1 < len(steps):
                choose(*steps[n + 1])
            phase_u(tt, h)
            if n:
                phase_v(*steps[n - 1])
        finish(0)
        phase_v(*steps[-1])
        finish(1)
        SP.wait((so, 32))


def shape_constants():
    k = np.zeros((P, N_K), np.float32)
    i = np.arange(P)
    k[:, K_ID:K_ID + 128] = np.eye(P)
    k[:, K_SU:K_SU + 128] = i[:, None] < i[None, :]
    k[:, K_IU:K_IU + 128] = i[:, None] <= i[None, :]
    k[:, K_NEG:K_NEG + 128] = np.where(i[None, :] <= i[:, None], 0.0, -1e30)
    k[:, K_BLK:K_BLK + 128] = (i[:, None] // 64) == (i[None, :] // 64)
    k[:, K_HSEL:K_HSEL + 2] = (i[:, None] // 64) == np.arange(2)[None, :]
    d = i % 64
    for m in range(P):
        if d[m] < 8:
            k[m + 8, K_ROT + m] = -1.0
        elif d[m] < 16:
            k[m - 8, K_ROT + m] = 1.0
    freq = np.power(np.float32(500000.0), -np.arange(8, dtype=np.float32) / np.float32(8)).astype(np.float32)
    ang = np.arange(S, dtype=np.float32)[None, :] * freq[:, None]
    cos, sin = np.cos(ang), np.sin(ang)
    k[:, K_COS:K_COS + S] = 1.0
    for m in range(P):
        if d[m] < 16:
            k[m, K_COS:K_COS + S] = cos[d[m] % 8]
            k[m, K_SIN:K_SIN + S] = sin[d[m] % 8]
    for lv in range(7):
        s, t = i[:, None], i[None, :]
        m = (s >> (lv + 1) == t >> (lv + 1)) & ((s >> lv) & 1 == 0) & ((t >> lv) & 1 == 1)
        k[:, K_LEV + lv * 128:K_LEV + (lv + 1) * 128] = m
    k[:, K_IOTA:K_IOTA + 16] = np.arange(16)[None, :]
    return k


def lay_out(a):
    def t512(w):
        n = w.shape[1] // 512
        return np.ascontiguousarray(w.reshape(8, 128, n, 512).transpose(2, 1, 0, 3).reshape(n, 128, 4096))

    def kchunks(w):
        return w.reshape(-1, 128, w.shape[1]).transpose(1, 0, 2).reshape(128, -1)

    def col(x):
        return np.asarray(x).reshape(-1, 128).T

    f = np.float32
    ada = t512(a["ada_w"][0])
    ada = np.ascontiguousarray(ada[[0, 1, 2, 3, 4, 5, 6, 7, 8, 9, 10, 11]])
    ab = a["ada_b"][0]
    w_in = a["w_in"][0]
    wp = np.zeros((1024, 2560), f)
    chunk = [w_in[:, 128 * i:128 * i + 128] for i in range(19)]
    order = [0, 1, 2, 3, 4, 5, 6, 17, 18, 7, 9, 10, 8, 11, 12, 13, 14, 15, 16]
    for n, i in enumerate(order):
        wp[:, 128 * n:128 * n + 128] = chunk[i]
    cols = np.zeros((P, N_COLS), f)
    cols[:, C_MU:C_MU + 7] = col(a["rwkv_mu"][0])
    for c, n in ((C_W0, "rwkv_w0"), (C_A0, "rwkv_a0"), (C_KK, "rwkv_kk"), (C_KA, "rwkv_ka"), (C_RK, "rwkv_rk"),
                 (C_SD, "s5_d")):
        cols[:, c:c + 2] = col(a[n][0])
    for j in range(3):
        cols[:, C_CONV + 2 * j:C_CONV + 2 * j + 2] = col(a["conv_w"][0, j])
    cols[:, C_ARE:C_ARE + 8] = col(a["s5_a_re"][0])
    cols[:, C_AIM:C_AIM + 8] = col(a["s5_a_im"][0])
    cols[:, C_DT:C_DT + 8] = col(np.repeat(a["s5_log_dt"][0], 64))
    cols[:, C_C:C_C + 8] = col(a["c"])
    cols[:, C_GMIX:C_GMIX + 8] = col(a["norm_mix_g"])
    cols[:, C_GFFN:C_GFFN + 8] = col(a["norm_ffn_g"])
    cols[:, C_GMIX2:C_GMIX2 + 8] = col(a["norm_mix_g_2"])
    cols[:, C_ADAB:C_ADAB + 32] = col(np.concatenate([ab[0:2048], ab[3072:5120]]))
    rowa = np.zeros((1, N_ROWA), f)
    for r, n in ((R_LNXW, "rwkv_lnx_w"), (R_LNXB, "rwkv_lnx_b"), (R_SGW, "sg_ln_w"), (R_SGB, "sg_ln_b")):
        rowa[0, r:r + 256] = a[n][0]
    place = [0, 2, 4, 6, 1, 3, 5, 7]
    rowa[0, R_BF:R_BF + 8] = a["b_forget_2"][0][place]
    w6 = np.zeros((P, 768), f)
    w6[0:32, 0:256] = a["rwkv_w2"][0]
    w6[32:64, 256:512] = a["rwkv_a2"][0]
    w6[64:128, 512:768] = a["rwkv_g2"][0]
    ws = np.ascontiguousarray(a["sg_ws"][0].transpose(2, 0, 1))
    bs = np.zeros((P, 2, 128), f)
    for g in range(4):
        bs[64 * (g % 2):64 * (g % 2) + 64, g // 2, :] = a["sg_bs"][0, g][None, :]
    s5b = np.zeros((4, P, 4, 128), f)
    s5c = np.zeros((4, P, 4, 128), f)
    for i, (nb, ncn) in enumerate((("s5_b_re", "s5_c_re"), ("s5_b_im", "s5_c_im"))):
        for g in range(16):
            hf, q, e, ch = g // 8, (g % 8) // 2, g % 2, (g % 8) * 16
            s5b[2 * hf + i, ch:ch + 16, q, 64 * e:64 * e + 64] = a[nb][0, g].T
            s5c[2 * hf + i, 64 * e:64 * e + 64, q, ch:ch + 16] = a[ncn][0, g].T
    w2 = a["w_in_2"][0]
    return {
        "x": np.ascontiguousarray(a["x"][0].reshape(2, 128, 1024).transpose(1, 0, 2)),
        "cols": cols, "K": shape_constants(), "rowa": rowa,
        "ada": ada,
        "adab_g": np.ascontiguousarray(np.concatenate([ab[2048:3072], ab[5120:6144]])[None, :]),
        "wp": t512(wp), "gates": t512(w_in[:, 2432:6528]),
        "o_ab": np.ascontiguousarray(np.concatenate([kchunks(a["rwkv_out"][0]), kchunks(a["sg_out"][0])], 1)[None]),
        "o_c": np.ascontiguousarray(kchunks(a["conv_out"][0])[None]),
        "glu": np.ascontiguousarray(kchunks(a["s5_glu_w"][0])[None]),
        "w_o": t512(a["w_o"][0]), "w1": t512(a["ffn_w1"][0]),
        "w2": np.ascontiguousarray(a["ffn_w2"][0].reshape(8, 4, 128, 1024).transpose(0, 2, 1, 3).reshape(8, 128, 4096)),
        "w6": w6, "ws": ws, "bs": bs, "s5b": s5b, "s5c": s5c,
        "rowb": a["final_g"][None, :].copy(),
        "qkv": t512(w2[:, 0:3072]),
        "wf": np.ascontiguousarray(w2[:, 3072:3080][:, place].reshape(8, 128, 8).transpose(1, 0, 2).reshape(128, 64)),
        "g2": t512(w2[:, 3080:5128]),
        "ba": np.ascontiguousarray(kchunks(a["w_branch_a_2"][0])[None]),
        "bb": np.ascontiguousarray(kchunks(a["w_branch_b_2"][0])[None]),
        "wout": t512(a["w_out_2"][0]), "pq": t512(a["w_peer_q_2"][0]),
        "keys": np.ascontiguousarray(a["peer_sub_keys_2"][0].transpose(3, 0, 1, 2).reshape(1, 128, 2048)),
        "rowb2": np.concatenate([a["norm_ffn_g_2"][0], a["norm_final_g_2"]])[None, :].copy(),
        "eu": a["peer_expert_u_2"][0], "ev": a["peer_expert_v_2"][0],
    }


def kernel(**inputs):
    import concourse.bacc as _bacc
    from concourse.bass_utils import run_bass_kernel_spmd as _run

    a = lay_out({k: np.asarray(x) for k, x in inputs.items()})
    nc = _bacc.Bacc("TRN2", target_bir_lowering=False, num_devices=1)
    arrays, A = {}, {}
    for name, x in a.items():
        x = np.ascontiguousarray(x)
        arrays[f"in_{name}"] = x
        A[name] = nc.dram_tensor(f"in_{name}", x.shape, mybir.dt.from_np(x.dtype), kind="ExternalInput").ap()
    out = nc.dram_tensor("out_0", (P, 2, D), F32, kind="ExternalOutput").ap()
    build(nc, A, out)
    r = _run(nc, [arrays], core_ids=[0])
    return np.ascontiguousarray(r.results[0]["out_0"].transpose(1, 0, 2).reshape(1, S, D))
```
